# Optimizing a Trainium2 kernel written in Bass

```python
import math
import jax
import jax.numpy as jnp
from jax import lax
import numpy as np

D_MODEL = 1024
BATCH = 1
SEQ = 256
DEPTH = 1

HEAD_DIM = 64
Q_BLOCK = 128
RMS_EPS = 1e-6
NEG_INF = -1e30
FORCE_SCORE = 1e9

N_BUCKETS = 32
BUCKET_EXACT = 16
BUCKET_MAX_DIST = 2048

A_HEADS = 4
A_CMP_LEN = 32
A_CMP_STRIDE = 16
A_PHI_HIDDEN = 128
A_SEL_BLOCK = 64
A_SEL_TOPK = 16
A_WINDOW = 512

B_GROUPS = ((128, 1), (512, 4), (2048, 16))
B_HEADS_PER_GROUP = 2
B_HEADS = B_HEADS_PER_GROUP * len(B_GROUPS)

C_HEADS = 4

D_HEADS = 4
D_Q_LORA = 256
D_KV_LORA = 128
D_NOPE = 64
D_ROPE = 32
D_VDIM = 64
ROPE_THETA = 10000.0

D_FF = 2816
FFN_CONV_WIDTH = 3

N_BRANCHES = 4
IN_SPLITS = (
    A_HEADS * HEAD_DIM,
    6 * HEAD_DIM,
    3 * A_HEADS,
    3 * B_HEADS * HEAD_DIM,
    3 * C_HEADS * HEAD_DIM,
    C_HEADS,
    D_Q_LORA,
    D_KV_LORA,
    D_ROPE,
)
D_IN = sum(IN_SPLITS)
A_OUT = A_HEADS * HEAD_DIM
B_OUT = B_HEADS_PER_GROUP * HEAD_DIM
C_OUT = C_HEADS * HEAD_DIM
D_OUT = D_HEADS * D_VDIM


def rms_norm(x, gain):
    xf = x.astype(jnp.float32)
    y = xf * lax.rsqrt(jnp.mean(xf * xf, axis=-1, keepdims=True) + RMS_EPS)
    return (y * gain.astype(jnp.float32)).astype(x.dtype)

def split_cols(a, sizes):
    return jnp.split(a, np.cumsum(sizes)[:-1].tolist(), axis=-1)

def rel_bucket(dist):
    dist = jnp.maximum(dist, 0)
    d = jnp.maximum(dist, 1).astype(jnp.float32)
    large = BUCKET_EXACT + (jnp.log(d / BUCKET_EXACT) / math.log(BUCKET_MAX_DIST / BUCKET_EXACT)
                            * (N_BUCKETS - BUCKET_EXACT)).astype(jnp.int32)
    large = jnp.minimum(large, N_BUCKETS - 1)
    return jnp.where(dist < BUCKET_EXACT, dist, large)

def masked_softmax(logits, mask):
    logits = jnp.where(mask, logits, NEG_INF)
    m = jnp.max(logits, axis=-1, keepdims=True)
    p = jnp.where(mask, jnp.exp(logits - m), 0.0)
    den = jnp.sum(p, axis=-1, keepdims=True)
    den_safe = jnp.maximum(den, 1e-30)
    return p / den_safe, m[..., 0] + jnp.log(den_safe[..., 0])

def sweep_query_blocks(fn, *q_arrays):
    b, s = q_arrays[0].shape[:2]
    nb = s // Q_BLOCK
    blocked = tuple(jnp.moveaxis(a.reshape((b, nb, Q_BLOCK) + a.shape[2:]), 1, 0) for a in q_arrays)
    out = lax.map(lambda args: fn(args[0], *args[1:]), (jnp.arange(nb, dtype=jnp.int32),) + blocked)
    return jnp.moveaxis(out, 0, 1).reshape((b, s) + out.shape[3:])

def rope(x, cos, sin):
    x1, x2 = jnp.split(x, 2, axis=-1)
    return jnp.concatenate([x1 * cos - x2 * sin, x2 * cos + x1 * sin], axis=-1)

def nsa_mixer(q, kv_a, gate_logits, cmp_pos, phi_k_w1, phi_k_w2, phi_v_w1, phi_v_w2, rel_table):
    b, s = q.shape[:2]
    k_cmp, v_cmp, k_slc, v_slc, k_win, v_win = jnp.split(kv_a, 6, axis=-1)
    scale = HEAD_DIM ** -0.5
    n_cmp = (s - A_CMP_LEN) // A_CMP_STRIDE + 1

    def compress(kv, w1, w2):
        ch = kv.reshape(b, s // A_CMP_STRIDE, A_CMP_STRIDE, HEAD_DIM)
        blocks = jnp.concatenate([ch[:, j:j + n_cmp] for j in range(A_CMP_LEN // A_CMP_STRIDE)], axis=2)
        blocks = (blocks + cmp_pos).reshape(b, n_cmp, A_CMP_LEN * HEAD_DIM)
        return jax.nn.gelu(blocks @ w1) @ w2

    kc = compress(k_cmp, phi_k_w1, phi_k_w2)
    vc = compress(v_cmp, phi_v_w1, phi_v_w2)
    cmp_start = jnp.arange(n_cmp) * A_CMP_STRIDE
    cmp_end = cmp_start + A_CMP_LEN - 1
    n_sel = s // A_SEL_BLOCK
    sel_start = jnp.arange(n_sel) * A_SEL_BLOCK
    overlap = ((cmp_start[:, None] <= sel_start[None, :] + A_SEL_BLOCK - 1)
               & (cmp_end[:, None] >= sel_start[None, :])).astype(jnp.float32)
    n_top = min(A_SEL_TOPK, n_sel)
    ks_blocks = k_slc.reshape(b, n_sel, A_SEL_BLOCK, HEAD_DIM)
    vs_blocks = v_slc.reshape(b, n_sel, A_SEL_BLOCK, HEAD_DIM)
    kw_pad = jnp.pad(k_win, ((0, 0), (A_WINDOW, 0), (0, 0)))
    vw_pad = jnp.pad(v_win, ((0, 0), (A_WINDOW, 0), (0, 0)))
    tab = rel_table[:, :A_HEADS]
    batch_ix = jnp.arange(b)[:, None, None]

    def block(bi, q_blk, g_blk):
        t = bi * Q_BLOCK + jnp.arange(Q_BLOCK)
        lc = jnp.einsum('bqhd,bcd->bhqc', q_blk, kc, preferred_element_type=jnp.float32) * scale
        p_c, _ = masked_softmax(lc, cmp_end[None, :] <= t[:, None])
        o_c = jnp.einsum('bhqc,bcd->bqhd', p_c.astype(vc.dtype), vc)
        imp = jnp.einsum('bhqc,cj->bqj', p_c, overlap)
        cur = (t // A_SEL_BLOCK)[:, None]
        j = jnp.arange(n_sel)[None, :]
        imp = jnp.where((j == 0) | (j == cur) | (j == cur - 1), FORCE_SCORE,
                        jnp.where(j > cur, -FORCE_SCORE, imp))
        _, sel = lax.top_k(imp, n_top)
        ks = ks_blocks[batch_ix, sel].reshape(b, Q_BLOCK, n_top * A_SEL_BLOCK, HEAD_DIM)
        vs = vs_blocks[batch_ix, sel].reshape(b, Q_BLOCK, n_top * A_SEL_BLOCK, HEAD_DIM)
        pos = (sel[..., None] * A_SEL_BLOCK + jnp.arange(A_SEL_BLOCK)).reshape(b, Q_BLOCK, n_top * A_SEL_BLOCK)
        dist = t[None, :, None] - pos
        ls = (jnp.einsum('bqhd,bqkd->bhqk', q_blk, ks, preferred_element_type=jnp.float32) * scale
              + jnp.moveaxis(tab[rel_bucket(dist)], -1, 1))
        p_s, _ = masked_softmax(ls, (dist >= 0)[:, None])
        o_s = jnp.einsum('bhqk,bqkd->bqhd', p_s.astype(vs.dtype), vs)
        kw = lax.dynamic_slice_in_dim(kw_pad, bi * Q_BLOCK, A_WINDOW + Q_BLOCK, axis=1)
        vw = lax.dynamic_slice_in_dim(vw_pad, bi * Q_BLOCK, A_WINDOW + Q_BLOCK, axis=1)
        kpos = bi * Q_BLOCK - A_WINDOW + jnp.arange(A_WINDOW + Q_BLOCK)
        dist_w = t[:, None] - kpos[None, :]
        mask_w = (kpos[None, :] >= 0) & (dist_w >= 0) & (dist_w < A_WINDOW)
        lw = (jnp.einsum('bqhd,bkd->bhqk', q_blk, kw, preferred_element_type=jnp.float32) * scale
              + jnp.moveaxis(tab[rel_bucket(dist_w)], -1, 0)[None])
        p_w, _ = masked_softmax(lw, mask_w)
        o_w = jnp.einsum('bhqk,bkd->bqhd', p_w.astype(vw.dtype), vw)
        g = jax.nn.sigmoid(g_blk.astype(jnp.float32)).astype(q_blk.dtype)
        return g[..., 0:1] * o_c + g[..., 1:2] * o_s + g[..., 2:3] * o_w

    return sweep_query_blocks(block, q, gate_logits)

def dilated_mixer(q, k, v, rel_table):
    scale = HEAD_DIM ** -0.5
    tab = rel_table[:, A_HEADS:]
    hsl = [slice(g * B_HEADS_PER_GROUP, (g + 1) * B_HEADS_PER_GROUP) for g in range(len(B_GROUPS))]
    k_groups = [k[:, :, hs] for hs in hsl]
    v_groups = [v[:, :, hs] for hs in hsl]

    def block(bi, q_blk):
        t = bi * Q_BLOCK + jnp.arange(Q_BLOCK)
        outs, lses = [], []
        for g, (window, dilation) in enumerate(B_GROUPS):
            offs = dilation * jnp.arange(window // dilation + 1)
            idx = t[:, None] - offs[None, :]
            safe = jnp.maximum(idx, 0)
            kg = k_groups[g][:, safe]
            vg = v_groups[g][:, safe]
            bias = jnp.moveaxis(tab[rel_bucket(offs), hsl[g]], -1, 0)
            logits = (jnp.einsum('bqhd,bqkhd->bhqk', q_blk[:, :, hsl[g]], kg, preferred_element_type=jnp.float32)
                      * scale + bias[None, :, None, :])
            p, lse = masked_softmax(logits, (idx >= 0)[None, None])
            outs.append(jnp.einsum('bhqk,bqkhd->bqhd', p.astype(vg.dtype), vg))
            lses.append(jnp.moveaxis(lse, -1, 1))
        wts = jax.nn.softmax(jnp.stack(lses), axis=0)
        return jnp.einsum('gbqh,gbqhd->bqhd', wts.astype(q_blk.dtype), jnp.stack(outs))

    return sweep_query_blocks(block, q)

def forgetting_mixer(q, k, v, f_logits, f_bias):
    s = q.shape[1]
    scale = HEAD_DIM ** -0.5
    log_f = jax.nn.log_sigmoid(f_logits.astype(jnp.float32) + f_bias.astype(jnp.float32))
    cum = jnp.cumsum(log_f, axis=1)
    cum_keys = jnp.moveaxis(cum, 1, 2)
    kpos = jnp.arange(s)

    def block(bi, q_blk, cum_blk):
        t = bi * Q_BLOCK + jnp.arange(Q_BLOCK)
        logits = (jnp.einsum('bqhd,bkhd->bhqk', q_blk, k, preferred_element_type=jnp.float32) * scale
                  + jnp.moveaxis(cum_blk, 1, 2)[..., None] - cum_keys[:, :, None, :])
        p, _ = masked_softmax(logits, kpos[None, :] <= t[:, None])
        return jnp.einsum('bhqk,bkhd->bqhd', p.astype(v.dtype), v)

    return sweep_query_blocks(block, q, cum)

def mla_mixer(q_lat, kv_lat, k_rope, q_norm, kv_norm, w_uq, w_ukv):
    b, s = q_lat.shape[:2]
    scale = (D_NOPE + D_ROPE) ** -0.5
    q = (rms_norm(q_lat, q_norm) @ w_uq).reshape(b, s, D_HEADS, D_NOPE + D_ROPE)
    kv = (rms_norm(kv_lat, kv_norm) @ w_ukv).reshape(b, s, D_HEADS, D_NOPE + D_VDIM)
    q_nope, q_rot = q[..., :D_NOPE], q[..., D_NOPE:]
    k_nope, v = kv[..., :D_NOPE], kv[..., D_NOPE:]
    inv_freq = ROPE_THETA ** (-jnp.arange(0, D_ROPE, 2, dtype=jnp.float32) / D_ROPE)
    ang = jnp.arange(s, dtype=jnp.float32)[:, None] * inv_freq[None, :]
    cos, sin = jnp.cos(ang).astype(q.dtype), jnp.sin(ang).astype(q.dtype)
    q_rot = rope(q_rot, cos[:, None], sin[:, None])
    k_rot = rope(k_rope, cos, sin)
    kpos = jnp.arange(s)

    def block(bi, qn_blk, qr_blk):
        t = bi * Q_BLOCK + jnp.arange(Q_BLOCK)
        logits = (jnp.einsum('bqhd,bkhd->bhqk', qn_blk, k_nope, preferred_element_type=jnp.float32)
                  + jnp.einsum('bqhr,bkr->bhqk', qr_blk, k_rot, preferred_element_type=jnp.float32)) * scale
        p, _ = masked_softmax(logits, kpos[None, :] <= t[:, None])
        return jnp.einsum('bhqk,bkhd->bqhd', p.astype(v.dtype), v)

    return sweep_query_blocks(block, q_nope, q_rot)

def first_inputs(seed: int = 0) -> dict:
    key = jax.random.key(seed)
    ks = iter(list(jax.random.split(key, 32)))
    f32 = jnp.float32

    def nrm(shape, fan_in, scale=1.0):
        return scale * jax.random.normal(next(ks), shape, f32) * fan_in ** -0.5

    def gain(shape):
        return 1.0 + 0.05 * jax.random.normal(next(ks), shape, f32)

    return {
        'x': jax.random.normal(next(ks), (BATCH, SEQ, D_MODEL), f32),
        'rel_bias_table': 0.5 * jax.random.normal(next(ks), (N_BUCKETS, A_HEADS + B_HEADS), f32),
        'norm_attn_pre': gain((DEPTH, D_MODEL)),
        'norm_attn_post': gain((DEPTH, D_MODEL)),
        'norm_ffn_pre': gain((DEPTH, D_MODEL)),
        'norm_ffn_post': gain((DEPTH, D_MODEL)),
        'w_in': nrm((DEPTH, D_MODEL, D_IN), D_MODEL),
        'nsa_cmp_pos': 0.1 * jax.random.normal(next(ks), (DEPTH, A_CMP_LEN, HEAD_DIM), f32),
        'nsa_phi_k_w1': nrm((DEPTH, A_CMP_LEN * HEAD_DIM, A_PHI_HIDDEN), A_CMP_LEN * HEAD_DIM),
        'nsa_phi_k_w2': nrm((DEPTH, A_PHI_HIDDEN, HEAD_DIM), A_PHI_HIDDEN),
        'nsa_phi_v_w1': nrm((DEPTH, A_CMP_LEN * HEAD_DIM, A_PHI_HIDDEN), A_CMP_LEN * HEAD_DIM),
        'nsa_phi_v_w2': nrm((DEPTH, A_PHI_HIDDEN, HEAD_DIM), A_PHI_HIDDEN),
        'fox_forget_bias': 2.0 + 0.5 * jax.random.normal(next(ks), (DEPTH, C_HEADS), f32),
        'mla_q_norm': gain((DEPTH, D_Q_LORA)),
        'mla_kv_norm': gain((DEPTH, D_KV_LORA)),
        'mla_w_uq': nrm((DEPTH, D_Q_LORA, D_HEADS * (D_NOPE + D_ROPE)), D_Q_LORA),
        'mla_w_ukv': nrm((DEPTH, D_KV_LORA, D_HEADS * (D_NOPE + D_VDIM)), D_KV_LORA),
        'w_branch_a': nrm((DEPTH, A_OUT, D_MODEL), A_OUT),
        'w_branch_b': nrm((DEPTH, B_OUT, D_MODEL), B_OUT),
        'w_branch_c': nrm((DEPTH, C_OUT, D_MODEL), C_OUT),
        'w_branch_d': nrm((DEPTH, D_OUT, D_MODEL), D_OUT),
        'w_merge_gate': nrm((DEPTH, N_BRANCHES, D_MODEL, D_MODEL), D_MODEL),
        'w_o': nrm((DEPTH, D_MODEL, D_MODEL), D_MODEL),
        'ffn_w_up': nrm((DEPTH, D_MODEL, 2 * D_FF), D_MODEL),
        'ffn_conv_w': nrm((DEPTH, FFN_CONV_WIDTH, 2 * D_FF), FFN_CONV_WIDTH),
        'ffn_conv_b': 0.02 * jax.random.normal(next(ks), (DEPTH, 2 * D_FF), f32),
        'ffn_w_down': nrm((DEPTH, D_FF, D_MODEL), D_FF),
    }

def first_block(x, rel_bias_table, norm_attn_pre, norm_attn_post, norm_ffn_pre, norm_ffn_post,
              w_in, nsa_cmp_pos, nsa_phi_k_w1, nsa_phi_k_w2, nsa_phi_v_w1, nsa_phi_v_w2,
              fox_forget_bias, mla_q_norm, mla_kv_norm, mla_w_uq, mla_w_ukv,
              w_branch_a, w_branch_b, w_branch_c, w_branch_d, w_merge_gate, w_o,
              ffn_w_up, ffn_conv_w, ffn_conv_b, ffn_w_down):
    batch, seq = x.shape[:2]
    for l in range(DEPTH):
        h = rms_norm(x, norm_attn_pre[l])
        (a_q, a_kv, a_g, b_qkv, c_qkv, c_f, d_qlat, d_kvlat, d_krope) = split_cols(h @ w_in[l], IN_SPLITS)
        o_a = nsa_mixer(a_q.reshape(batch, seq, A_HEADS, HEAD_DIM), a_kv,
                        a_g.reshape(batch, seq, A_HEADS, 3), nsa_cmp_pos[l],
                        nsa_phi_k_w1[l], nsa_phi_k_w2[l], nsa_phi_v_w1[l], nsa_phi_v_w2[l],
                        rel_bias_table)
        b_qkv = b_qkv.reshape(batch, seq, 3, B_HEADS, HEAD_DIM)
        o_b = dilated_mixer(b_qkv[:, :, 0], b_qkv[:, :, 1], b_qkv[:, :, 2], rel_bias_table)
        c_qkv = c_qkv.reshape(batch, seq, 3, C_HEADS, HEAD_DIM)
        o_c = forgetting_mixer(c_qkv[:, :, 0], c_qkv[:, :, 1], c_qkv[:, :, 2], c_f, fox_forget_bias[l])
        o_d = mla_mixer(d_qlat, d_kvlat, d_krope, mla_q_norm[l], mla_kv_norm[l], mla_w_uq[l], mla_w_ukv[l])
        branches = (
            (o_a.reshape(batch, seq, A_OUT), w_branch_a[l]),
            (o_b.reshape(batch, seq, B_OUT), w_branch_b[l]),
            (o_c.reshape(batch, seq, C_OUT), w_branch_c[l]),
            (o_d.reshape(batch, seq, D_OUT), w_branch_d[l]),
        )
        merged = None
        for i, (o_i, w_i) in enumerate(branches):
            term = jax.nn.sigmoid(h @ w_merge_gate[l, i]) * (o_i @ w_i)
            merged = term if i == 0 else merged + term
        x = x + rms_norm(merged @ w_o[l], norm_attn_post[l])
        h = rms_norm(x, norm_ffn_pre[l])
        u = h @ ffn_w_up[l]
        u_pad = jnp.pad(u, ((0, 0), (FFN_CONV_WIDTH - 1, 0), (0, 0)))
        conv = ffn_conv_b[l]
        for j in range(FFN_CONV_WIDTH):
            conv = conv + ffn_conv_w[l, j] * u_pad[:, j:j + seq]
        gate, val = jnp.split(conv, 2, axis=-1)
        y = (jax.nn.silu(gate) * val) @ ffn_w_down[l]
        x = x + rms_norm(y, norm_ffn_post[l])
    return x


DEPTH_2 = 2

CHUNK = 64
N_MEM = 256
EPS = 1e-6
A_HEADS_2 = D_MODEL // (2 * HEAD_DIM)
IDX_HEADS = 8
IDX_DIM = 64
TOPK_MAX = 256
B_VDIM = 2 * HEAD_DIM
B_HEADS_2 = D_MODEL // (2 * B_VDIM)
C_HEADS_2 = D_MODEL // HEAD_DIM
C_BAND = 9
REL_CLIP = 256
T5_BUCKETS = 32
T5_MAX_DIST = 128
T5_HEADS = A_HEADS_2 + B_HEADS_2
M_HEADS = 4
M_DIM = 128


def even_split_sizes():
    return [A_HEADS_2 * HEAD_DIM, A_HEADS_2 * HEAD_DIM, A_HEADS_2 * HEAD_DIM,
            IDX_HEADS * IDX_DIM, IDX_DIM, IDX_HEADS,
            B_HEADS_2 * 2 * HEAD_DIM, B_HEADS_2 * 2 * HEAD_DIM, B_HEADS_2 * B_VDIM]

def rmsnorm(x, g):
    xf = x.astype(jnp.float32)
    y = xf * lax.rsqrt(jnp.mean(xf * xf, axis=-1, keepdims=True) + EPS)
    return (y * g.astype(jnp.float32)).astype(x.dtype)

def swiglu(x, wg, wu, wd):
    return (jax.nn.silu(x @ wg) * (x @ wu)) @ wd

def t5_bucket(rel):
    nb = T5_BUCKETS // 2
    max_exact = nb // 2
    offset = (rel < 0).astype(jnp.int32) * nb
    n = jnp.abs(rel)
    nf = jnp.maximum(n, 1).astype(jnp.float32)
    large = max_exact + (jnp.log(nf / max_exact) / math.log(T5_MAX_DIST / max_exact)
                         * (nb - max_exact)).astype(jnp.int32)
    large = jnp.minimum(large, nb - 1)
    return offset + jnp.where(n < max_exact, n, large)

def dsa_attention(q, k, v, iq, ik, iw, bias_table):
    bsz, seq, heads, dh = q.shape
    top_k = min(TOPK_MAX, seq // 4)
    key_chunk = jnp.arange(seq, dtype=jnp.int32) // CHUNK
    bias_table = bias_table.astype(jnp.float32)

    def block(i):
        start = i * Q_BLOCK
        qpos = start + jnp.arange(Q_BLOCK, dtype=jnp.int32)
        qchunk = qpos // CHUNK
        qb = lax.dynamic_slice_in_dim(q, start, Q_BLOCK, axis=1)
        iqb = lax.dynamic_slice_in_dim(iq, start, Q_BLOCK, axis=1)
        iwb = lax.dynamic_slice_in_dim(iw, start, Q_BLOCK, axis=1).astype(jnp.float32) * IDX_HEADS ** -0.5
        idx_logits = jnp.einsum('bqhd,bsd->bqhs', iqb, ik).astype(jnp.float32) * IDX_DIM ** -0.5
        score = jnp.einsum('bqh,bqhs->bqs', iwb, jax.nn.relu(idx_logits))
        admissible = key_chunk[None, :] <= qchunk[:, None]
        score = jnp.where(admissible[None], score, -jnp.inf)
        _, sel = lax.top_k(score, top_k)
        valid = (sel // CHUNK) <= qchunk[None, :, None]
        kg = jax.vmap(lambda kk, ii: kk[ii])(k, sel)
        vg = jax.vmap(lambda vv, ii: vv[ii])(v, sel)
        logits = jnp.einsum('bqhd,bqkhd->bhqk', qb, kg).astype(jnp.float32) * dh ** -0.5
        bias = bias_table[t5_bucket(qpos[None, :, None] - sel)]
        logits = logits + jnp.transpose(bias, (0, 3, 1, 2))
        logits = jnp.where(valid[:, None], logits, -jnp.inf)
        p = jax.nn.softmax(logits, axis=-1).astype(v.dtype)
        return jnp.einsum('bhqk,bqkhd->bqhd', p, vg)

    out = lax.map(block, jnp.arange(seq // Q_BLOCK, dtype=jnp.int32))
    return jnp.transpose(out, (1, 0, 2, 3, 4)).reshape(bsz, seq, heads * dh)

def diff_attention(q, k, v, lam, subln_g, bias_table):
    bsz, seq, heads, _, dh = q.shape
    pos = jnp.arange(seq, dtype=jnp.int32)
    key_chunk = pos // CHUNK
    bias_table = bias_table.astype(jnp.float32)

    def block(i):
        start = i * Q_BLOCK
        qpos = start + jnp.arange(Q_BLOCK, dtype=jnp.int32)
        qb = lax.dynamic_slice_in_dim(q, start, Q_BLOCK, axis=1)
        logits = jnp.einsum('bqhmd,bshmd->bhmqs', qb, k).astype(jnp.float32) * dh ** -0.5
        bias = bias_table[t5_bucket(qpos[:, None] - pos[None, :])]
        logits = logits + jnp.transpose(bias, (2, 0, 1))[None, :, None]
        mask = key_chunk[None, :] <= (qpos // CHUNK)[:, None]
        logits = jnp.where(mask, logits, -jnp.inf)
        p = jax.nn.softmax(logits, axis=-1)
        attn = (p[:, :, 0] - lam * p[:, :, 1]).astype(v.dtype)
        o = jnp.einsum('bhqs,bshe->bqhe', attn, v)
        return rmsnorm(o, subln_g)

    out = lax.map(block, jnp.arange(seq // Q_BLOCK, dtype=jnp.int32))
    return jnp.transpose(out, (1, 0, 2, 3, 4)).reshape(bsz, seq, heads * v.shape[-1])

def chunk_band_attention(q, k, v, rel_bias):
    bsz, seq, heads, dh = q.shape
    pad = (C_BAND - 1) * CHUNK
    band = C_BAND * CHUNK
    kp = jnp.pad(k, ((0, 0), (pad, 0), (0, 0), (0, 0)))
    vp = jnp.pad(v, ((0, 0), (pad, 0), (0, 0), (0, 0)))
    qoff = jnp.arange(CHUNK, dtype=jnp.int32)
    koff = jnp.arange(band, dtype=jnp.int32)
    rel = (qoff[:, None] + pad) - koff[None, :]
    rel_idx = jnp.clip(rel, -REL_CLIP, REL_CLIP) + REL_CLIP
    bias = jnp.transpose(rel_bias.astype(jnp.float32)[rel_idx], (2, 0, 1))

    def one_chunk(c):
        qc = lax.dynamic_slice_in_dim(q, c * CHUNK, CHUNK, axis=1)
        kc = lax.dynamic_slice_in_dim(kp, c * CHUNK, band, axis=1)
        vc = lax.dynamic_slice_in_dim(vp, c * CHUNK, band, axis=1)
        valid = (c * CHUNK - pad + koff) >= 0
        logits = jnp.einsum('bqhd,bkhd->bhqk', qc, kc).astype(jnp.float32) * dh ** -0.5 + bias[None]
        logits = jnp.where(valid, logits, -jnp.inf)
        p = jax.nn.softmax(logits, axis=-1).astype(vc.dtype)
        return jnp.einsum('bhqk,bkhd->bqhd', p, vc)

    out = lax.map(one_chunk, jnp.arange(seq // CHUNK, dtype=jnp.int32))
    return jnp.transpose(out, (1, 0, 2, 3, 4)).reshape(bsz, seq, heads * dh)

def even_mixer(h, w_in, a_qg, a_kg, idx_kg, b_qg, b_kg, lq1, lk1, lq2, lk2, b_subln, w_out, t5_bias, layer_idx):
    bsz, seq, _ = h.shape
    cuts = [int(c) for c in np.cumsum(even_split_sizes())[:-1]]
    aq, ak, av, iq, ik, iw, bq, bk, bv = jnp.split(h @ w_in, cuts, axis=-1)
    aq = rmsnorm(aq.reshape(bsz, seq, A_HEADS_2, HEAD_DIM), a_qg)
    ak = rmsnorm(ak.reshape(bsz, seq, A_HEADS_2, HEAD_DIM), a_kg)
    av = av.reshape(bsz, seq, A_HEADS_2, HEAD_DIM)
    iq = iq.reshape(bsz, seq, IDX_HEADS, IDX_DIM)
    ik = rmsnorm(ik, idx_kg)
    out_a = dsa_attention(aq, ak, av, iq, ik, iw, t5_bias[:, :A_HEADS_2])
    bq = rmsnorm(bq.reshape(bsz, seq, B_HEADS_2, 2, HEAD_DIM), b_qg)
    bk = rmsnorm(bk.reshape(bsz, seq, B_HEADS_2, 2, HEAD_DIM), b_kg)
    bv = bv.reshape(bsz, seq, B_HEADS_2, B_VDIM)
    lambda_init = 0.8 - 0.6 * math.exp(-0.3 * layer_idx)
    lam = (jnp.exp(jnp.sum(lq1.astype(jnp.float32) * lk1.astype(jnp.float32)))
           - jnp.exp(jnp.sum(lq2.astype(jnp.float32) * lk2.astype(jnp.float32))) + lambda_init)
    out_b = diff_attention(bq, bk, bv, lam, b_subln, t5_bias[:, A_HEADS_2:]) * (1.0 - lambda_init)
    return jnp.concatenate([out_a, out_b], axis=-1) @ w_out

def odd_mixer(h, w_in, c_qg, c_kg, rel_bias, w_out):
    bsz, seq, _ = h.shape
    q, k, v = jnp.split(h @ w_in, 3, axis=-1)
    q = rmsnorm(q.reshape(bsz, seq, C_HEADS_2, HEAD_DIM), c_qg)
    k = rmsnorm(k.reshape(bsz, seq, C_HEADS_2, HEAD_DIM), c_kg)
    v = v.reshape(bsz, seq, C_HEADS_2, HEAD_DIM)
    return chunk_band_attention(q, k, v, rel_bias) @ w_out

def memory_xattn(h, m, wq, wkv, qg, kg, wo):
    bsz, seq, _ = h.shape
    q = rmsnorm((h @ wq).reshape(bsz, seq, M_HEADS, M_DIM), qg)
    k, v = jnp.split(m @ wkv, 2, axis=-1)
    k = rmsnorm(k.reshape(bsz, -1, M_HEADS, M_DIM), kg)
    v = v.reshape(bsz, -1, M_HEADS, M_DIM)
    logits = jnp.einsum('bshd,bmhd->bhsm', q, k).astype(jnp.float32) * M_DIM ** -0.5
    p = jax.nn.softmax(logits, axis=-1).astype(v.dtype)
    o = jnp.einsum('bhsm,bmhd->bshd', p, v).reshape(bsz, seq, M_HEADS * M_DIM)
    return o @ wo

def second_inputs(seed: int = 0) -> dict:
    key = jax.random.key(seed)
    counter = [0]

    def nk():
        counter[0] += 1
        return jax.random.fold_in(key, counter[0])

    def dense(fan_in, fan_out):
        return jax.random.normal(nk(), (fan_in, fan_out), jnp.float32) * fan_in ** -0.5

    def gain(n):
        return 1.0 + 0.02 * jax.random.normal(nk(), (n,), jnp.float32)

    def small(shape, scale):
        return scale * jax.random.normal(nk(), shape, jnp.float32)

    p = {}
    p['x'] = jax.random.normal(nk(), (BATCH, SEQ, D_MODEL), jnp.float32)
    p['mem'] = jax.random.normal(nk(), (BATCH, N_MEM, D_MODEL), jnp.float32)
    p['t5_bias'] = small((T5_BUCKETS, T5_HEADS), 0.2)
    for layer in range(DEPTH_2):
        pre = 'l%d_' % layer
        p[pre + 'ffn1_norm'] = gain(D_MODEL)
        p[pre + 'ffn1_wg'] = dense(D_MODEL, D_FF)
        p[pre + 'ffn1_wu'] = dense(D_MODEL, D_FF)
        p[pre + 'ffn1_wd'] = dense(D_FF, D_MODEL)
        p[pre + 'mix_norm'] = gain(D_MODEL)
        if layer % 2 == 0:
            p[pre + 'w_in'] = dense(D_MODEL, sum(even_split_sizes()))
            p[pre + 'a_q_norm'] = gain(HEAD_DIM)
            p[pre + 'a_k_norm'] = gain(HEAD_DIM)
            p[pre + 'idx_k_norm'] = gain(IDX_DIM)
            p[pre + 'b_q_norm'] = gain(HEAD_DIM)
            p[pre + 'b_k_norm'] = gain(HEAD_DIM)
            p[pre + 'b_lq1'] = small((HEAD_DIM,), 0.1)
            p[pre + 'b_lk1'] = small((HEAD_DIM,), 0.1)
            p[pre + 'b_lq2'] = small((HEAD_DIM,), 0.1)
            p[pre + 'b_lk2'] = small((HEAD_DIM,), 0.1)
            p[pre + 'b_subln'] = gain(B_VDIM)
            p[pre + 'w_out'] = dense(A_HEADS_2 * HEAD_DIM + B_HEADS_2 * B_VDIM, D_MODEL)
        else:
            p[pre + 'w_in'] = dense(D_MODEL, 3 * C_HEADS_2 * HEAD_DIM)
            p[pre + 'c_q_norm'] = gain(HEAD_DIM)
            p[pre + 'c_k_norm'] = gain(HEAD_DIM)
            p[pre + 'c_rel_bias'] = small((2 * REL_CLIP + 1, C_HEADS_2), 0.2)
            p[pre + 'w_out'] = dense(C_HEADS_2 * HEAD_DIM, D_MODEL)
        p[pre + 'mem_norm'] = gain(D_MODEL)
        p[pre + 'mem_src_norm'] = gain(D_MODEL)
        p[pre + 'mem_wq'] = dense(D_MODEL, M_HEADS * M_DIM)
        p[pre + 'mem_wkv'] = dense(D_MODEL, 2 * M_HEADS * M_DIM)
        p[pre + 'mem_q_norm'] = gain(M_DIM)
        p[pre + 'mem_k_norm'] = gain(M_DIM)
        p[pre + 'mem_wo'] = dense(M_HEADS * M_DIM, D_MODEL)
        p[pre + 'ffn2_norm'] = gain(D_MODEL)
        p[pre + 'ffn2_wg'] = dense(D_MODEL, D_FF)
        p[pre + 'ffn2_wu'] = dense(D_MODEL, D_FF)
        p[pre + 'ffn2_wd'] = dense(D_FF, D_MODEL)
    return p

def second_block(x, mem, t5_bias,
              l0_ffn1_norm, l0_ffn1_wg, l0_ffn1_wu, l0_ffn1_wd,
              l0_mix_norm, l0_w_in, l0_a_q_norm, l0_a_k_norm, l0_idx_k_norm,
              l0_b_q_norm, l0_b_k_norm, l0_b_lq1, l0_b_lk1, l0_b_lq2, l0_b_lk2, l0_b_subln, l0_w_out,
              l0_mem_norm, l0_mem_src_norm, l0_mem_wq, l0_mem_wkv, l0_mem_q_norm, l0_mem_k_norm, l0_mem_wo,
              l0_ffn2_norm, l0_ffn2_wg, l0_ffn2_wu, l0_ffn2_wd,
              l1_ffn1_norm, l1_ffn1_wg, l1_ffn1_wu, l1_ffn1_wd,
              l1_mix_norm, l1_w_in, l1_c_q_norm, l1_c_k_norm, l1_c_rel_bias, l1_w_out,
              l1_mem_norm, l1_mem_src_norm, l1_mem_wq, l1_mem_wkv, l1_mem_q_norm, l1_mem_k_norm, l1_mem_wo,
              l1_ffn2_norm, l1_ffn2_wg, l1_ffn2_wu, l1_ffn2_wd):
    ffn1 = [(l0_ffn1_norm, l0_ffn1_wg, l0_ffn1_wu, l0_ffn1_wd),
            (l1_ffn1_norm, l1_ffn1_wg, l1_ffn1_wu, l1_ffn1_wd)]
    mix = [(l0_mix_norm, (l0_w_in, l0_a_q_norm, l0_a_k_norm, l0_idx_k_norm, l0_b_q_norm, l0_b_k_norm,
                          l0_b_lq1, l0_b_lk1, l0_b_lq2, l0_b_lk2, l0_b_subln, l0_w_out)),
           (l1_mix_norm, (l1_w_in, l1_c_q_norm, l1_c_k_norm, l1_c_rel_bias, l1_w_out))]
    memx = [(l0_mem_norm, l0_mem_src_norm, l0_mem_wq, l0_mem_wkv, l0_mem_q_norm, l0_mem_k_norm, l0_mem_wo),
            (l1_mem_norm, l1_mem_src_norm, l1_mem_wq, l1_mem_wkv, l1_mem_q_norm, l1_mem_k_norm, l1_mem_wo)]
    ffn2 = [(l0_ffn2_norm, l0_ffn2_wg, l0_ffn2_wu, l0_ffn2_wd),
            (l1_ffn2_norm, l1_ffn2_wg, l1_ffn2_wu, l1_ffn2_wd)]
    h = x
    for layer in range(DEPTH_2):
        g, wg, wu, wd = ffn1[layer]
        h = h + 0.5 * swiglu(rmsnorm(h, g), wg, wu, wd)
        mix_g, mix_params = mix[layer]
        if layer % 2 == 0:
            h = h + even_mixer(rmsnorm(h, mix_g), *mix_params, t5_bias, layer)
        else:
            h = h + odd_mixer(rmsnorm(h, mix_g), *mix_params)
        mg, sg, wq, wkv, qg, kg, wo = memx[layer]
        h = h + memory_xattn(rmsnorm(h, mg), rmsnorm(mem, sg), wq, wkv, qg, kg, wo)
        g, wg, wu, wd = ffn2[layer]
        h = h + 0.5 * swiglu(rmsnorm(h, g), wg, wu, wd)
    return h


def setup_inputs(seed=0):
    out = dict(first_inputs(seed))
    for name, value in second_inputs(seed + 1).items():
        if name != "x":
            out[name + "_2"] = value
    return out


def reference(
    x, rel_bias_table, norm_attn_pre, norm_attn_post, norm_ffn_pre, norm_ffn_post, w_in,
    nsa_cmp_pos, nsa_phi_k_w1, nsa_phi_k_w2, nsa_phi_v_w1, nsa_phi_v_w2, fox_forget_bias,
    mla_q_norm, mla_kv_norm, mla_w_uq, mla_w_ukv, w_branch_a, w_branch_b, w_branch_c,
    w_branch_d, w_merge_gate, w_o, ffn_w_up, ffn_conv_w, ffn_conv_b, ffn_w_down, mem_2,
    t5_bias_2, l0_ffn1_norm_2, l0_ffn1_wg_2, l0_ffn1_wu_2, l0_ffn1_wd_2, l0_mix_norm_2,
    l0_w_in_2, l0_a_q_norm_2, l0_a_k_norm_2, l0_idx_k_norm_2, l0_b_q_norm_2, l0_b_k_norm_2,
    l0_b_lq1_2, l0_b_lk1_2, l0_b_lq2_2, l0_b_lk2_2, l0_b_subln_2, l0_w_out_2, l0_mem_norm_2,
    l0_mem_src_norm_2, l0_mem_wq_2, l0_mem_wkv_2, l0_mem_q_norm_2, l0_mem_k_norm_2, l0_mem_wo_2,
    l0_ffn2_norm_2, l0_ffn2_wg_2, l0_ffn2_wu_2, l0_ffn2_wd_2, l1_ffn1_norm_2, l1_ffn1_wg_2,
    l1_ffn1_wu_2, l1_ffn1_wd_2, l1_mix_norm_2, l1_w_in_2, l1_c_q_norm_2, l1_c_k_norm_2,
    l1_c_rel_bias_2, l1_w_out_2, l1_mem_norm_2, l1_mem_src_norm_2, l1_mem_wq_2, l1_mem_wkv_2,
    l1_mem_q_norm_2, l1_mem_k_norm_2, l1_mem_wo_2, l1_ffn2_norm_2, l1_ffn2_wg_2, l1_ffn2_wu_2,
    l1_ffn2_wd_2,
):
    x = first_block(
        x, rel_bias_table, norm_attn_pre, norm_attn_post, norm_ffn_pre, norm_ffn_post, w_in,
        nsa_cmp_pos, nsa_phi_k_w1, nsa_phi_k_w2, nsa_phi_v_w1, nsa_phi_v_w2, fox_forget_bias,
        mla_q_norm, mla_kv_norm, mla_w_uq, mla_w_ukv, w_branch_a, w_branch_b, w_branch_c,
        w_branch_d, w_merge_gate, w_o, ffn_w_up, ffn_conv_w, ffn_conv_b, ffn_w_down,
    )
    return second_block(
        x, mem_2, t5_bias_2, l0_ffn1_norm_2, l0_ffn1_wg_2, l0_ffn1_wu_2, l0_ffn1_wd_2,
        l0_mix_norm_2, l0_w_in_2, l0_a_q_norm_2, l0_a_k_norm_2, l0_idx_k_norm_2, l0_b_q_norm_2,
        l0_b_k_norm_2, l0_b_lq1_2, l0_b_lk1_2, l0_b_lq2_2, l0_b_lk2_2, l0_b_subln_2, l0_w_out_2,
        l0_mem_norm_2, l0_mem_src_norm_2, l0_mem_wq_2, l0_mem_wkv_2, l0_mem_q_norm_2,
        l0_mem_k_norm_2, l0_mem_wo_2, l0_ffn2_norm_2, l0_ffn2_wg_2, l0_ffn2_wu_2, l0_ffn2_wd_2,
        l1_ffn1_norm_2, l1_ffn1_wg_2, l1_ffn1_wu_2, l1_ffn1_wd_2, l1_mix_norm_2, l1_w_in_2,
        l1_c_q_norm_2, l1_c_k_norm_2, l1_c_rel_bias_2, l1_w_out_2, l1_mem_norm_2,
        l1_mem_src_norm_2, l1_mem_wq_2, l1_mem_wkv_2, l1_mem_q_norm_2, l1_mem_k_norm_2,
        l1_mem_wo_2, l1_ffn2_norm_2, l1_ffn2_wg_2, l1_ffn2_wu_2, l1_ffn2_wd_2,
    )


_drawn_inputs = setup_inputs


def setup_inputs(seed=0):
    import zlib

    import numpy as np

    out = dict(_drawn_inputs(seed))
    spreads = {}
    factors = {'mla_q_norm': 3.219,
     'l0_ffn1_norm_2': 7.658,
     'l0_mix_norm_2': 3.895,
     'l0_a_q_norm_2': 8.0,
     'l0_a_k_norm_2': 8.0,
     'l0_idx_k_norm_2': 6.261,
     'l0_b_q_norm_2': 8.0,
     'l0_b_k_norm_2': 8.0,
     'l0_b_lq1_2': 8.0,
     'l0_b_lk1_2': 8.0,
     'l0_b_lq2_2': 21.416,
     'l0_b_subln_2': 8.0,
     'l0_mem_norm_2': 8.0,
     'l0_mem_src_norm_2': 8.0,
     'l0_mem_q_norm_2': 8.0,
     'l0_mem_k_norm_2': 8.0,
     'l0_ffn2_norm_2': 8.0,
     'l1_ffn1_norm_2': 8.0,
     'l1_mix_norm_2': 8.0,
     'l1_c_q_norm_2': 8.0,
     'l1_c_k_norm_2': 8.0,
     'l1_c_rel_bias_2': 4.272,
     'l1_mem_norm_2': 8.0,
     'l1_mem_src_norm_2': 8.0,
     'l1_mem_q_norm_2': 8.0,
     'l1_mem_k_norm_2': 8.0,
     'l1_ffn2_norm_2': 32.293,
     'l0_b_lk2_2': 8.0}
    for name, (base, spread) in spreads.items():
        noise = np.random.default_rng([zlib.crc32(name.encode()), seed]).standard_normal(out[name].shape)
        drawn = base * np.exp(spread * noise) if base else spread * noise
        out[name] = jnp.asarray(drawn.astype(out[name].dtype))
    for name, factor in factors.items():
        out[name] = (out[name] * factor).astype(out[name].dtype)
    return out
```

```python
import math

import numpy as np

import concourse.bass as bass
from concourse import mybir

F32 = mybir.dt.float32
F32R = mybir.dt.float32r
ACT = mybir.ActivationFunctionType
ALU = mybir.AluOpType
AX = mybir.AxisListType

P = 128
S = 256
NB = S // P
D = 1024
KT = D // P
DH = 64
FF = 2816
FT = FF // P
EPS = 1e-6
NEG = -1e30
TAKEN = -3e38
HALF = 512

SLOT = 2048
RING = 4
LEAD = 2
TOE = 384
TOP_K = S // 4



def rel_bucket(dist):
    dist = np.maximum(dist, 0)
    d = np.maximum(dist, 1).astype(np.float32)
    large = 16 + (np.log(d / np.float32(16)) / np.float32(math.log(128)) * np.float32(16)).astype(np.int32)
    return np.where(dist < 16, dist, np.minimum(large, 31))


def t5_bucket(rel):
    off = (rel < 0).astype(np.int32) * 16
    n = np.abs(rel)
    nf = np.maximum(n, 1).astype(np.float32)
    large = 8 + (np.log(nf / np.float32(8)) / np.float32(math.log(16)) * np.float32(8)).astype(np.int32)
    return off + np.where(n < 8, n, np.minimum(large, 15))


class Columns:

    def __init__(self, **widths):
        self.at, self.n = {}, 0
        for name, w in widths.items():
            self.at[name] = (self.n, w)
            self.n += w

    def __call__(self, tile, name):
        a, w = self.at[name]
        return tile[:, a:a + w]


CONST = Columns(ident=P, upto=P, ones=P, causal=S, cmp_mask=30, cmp_valid=2, cos=2 * 16, sin=2 * 16)
TABLE = Columns(hot_rel=TOE, hot_t5=TOE, rel_mask=TOE)
PARAM = Columns(mla_q=2, mla_kv=1, a_q=1, a_k=1, idx_k=1, b_q=1, b_k=1, subln=1, c_q=1, c_k=1,
                mq0=1, mk0=1, mq1=1, mk1=1, conv_w=3 * 2 * FT, conv_b=2 * FT, cmp_pos=32,
                w2k=P, w2v=DH, lam=4 * DH, f_bias=4, rel=10, t5=12)
ROWS = ["attn_pre", "ffn_pre", "attn_post", "ffn_post", "l0_ffn1", "l0_mix", "l0_src", "l0_mem", "l0_ffn2",
        "l1_ffn1", "l1_mix", "l1_src", "l1_mem", "l1_ffn2"]


def constants():
    c = np.zeros((P, CONST.n), np.float32)
    p = np.arange(P)
    CONST(c, "ident")[:] = np.eye(P)
    CONST(c, "upto")[:] = p[:, None] <= p[None, :]
    CONST(c, "ones")[:] = 1
    k = np.arange(S)
    CONST(c, "causal")[:] = np.where(P + p[:, None] - k[None, :] >= 0, 0, NEG)
    end = np.arange(15) * 16 + 31
    for b in range(NB):
        t = b * P + p
        CONST(c, "cmp_mask")[:, 15 * b:15 * b + 15] = np.where(end[None, :] <= t[:, None], 0, NEG)
        CONST(c, "cmp_valid")[:, b] = t >= end[0]
        freq = (np.float32(10000.0) ** (-np.arange(0, 32, 2, dtype=np.float32) / np.float32(32))).astype(np.float32)
        angle = t.astype(np.float32)[:, None] * freq[None, :]
        CONST(c, "cos")[:, 16 * b:16 * b + 16] = np.cos(angle)
        CONST(c, "sin")[:, 16 * b:16 * b + 16] = np.sin(angle)
    return c


def tables():
    t = np.zeros((P, TABLE.n), np.float32)
    j = np.arange(TOE)
    dist = 255 - j
    for name, bucket in (("hot_rel", rel_bucket(dist)), ("hot_t5", t5_bucket(dist))):
        TABLE(t, name)[bucket, j] = 1
    for h in range(10):
        ok = dist >= 0
        if h >= 4:
            window, dilation = ((128, 1), (512, 4), (2048, 16))[(h - 4) // 2]
            ok = ok & (dist <= window) & (dist % dilation == 0)
        TABLE(t, "rel_mask")[h] = np.where(ok, 0, NEG)
    return t



class Matrix:

    def __init__(self, first, count, width):
        self.first, self.count, self.width = first, count, width
        self.per = SLOT // width
        self.slots = -(-count // self.per)

    def slot(self, i):
        return self.first + i // self.per

    def offset(self, i):
        return i % self.per * self.width

    def ends_slot(self, i):
        return i == self.count - 1 or i % self.per == self.per - 1


def by_chunk(w, width, chunks=None):
    k = w.shape[0] // P
    return [w[t * P:(t + 1) * P, c * width:(c + 1) * width]
            for c in range(chunks or -(-w.shape[1] // width)) for t in range(k)]


def by_tile(w, width):
    return [w[t * P:(t + 1) * P, c * width:(c + 1) * width]
            for t in range(w.shape[0] // P) for c in range(w.shape[1] // width)]


def first_in_columns():
    h64 = lambda base, i: list(range(base + 64 * i, base + 64 * i + 64))
    a_q, kv, b, c = 0, 256, 652, 1804
    tiles = []
    for t in range(2):
        tiles += h64(a_q, 2 * t) + h64(a_q, 2 * t + 1)
    tiles += h64(kv, 2) * 2 + h64(kv, 4) * 2 + h64(kv, 0) + h64(kv, 1)
    for base in (b, b + 384):
        for t in range(3):
            tiles += h64(base, 2 * t) + h64(base, 2 * t + 1)
    for base in (c, c + 256):
        for t in range(2):
            tiles += h64(base, 2 * t) + h64(base, 2 * t + 1)
    rows = (h64(kv, 3) + h64(kv, 5) + list(range(640, 652)) + list(range(b + 768, b + 1152))
            + list(range(c + 512, c + 768)) + list(range(2572, 2576)) + list(range(2576, 2992)))
    return tiles, rows


def even_in_columns():
    r = lambda a, n: list(range(a, a + n))
    main = r(0, 512) + r(512, 512) + r(1536, 512) + r(2120, 512) + r(2632, 512) + r(1024, 512) + r(3144, 512)
    return main, r(2048, 64) * 2 + r(2112, 8)


def stream_plan():
    plan = [("in_t", 15 * KT, P), ("in_n", 3 * KT, HALF), ("mla", 3, HALF), ("phi", 32, P)]
    for i in range(4):
        plan += [(f"branch{i}", 2 if i == 1 else 4, HALF), (f"gate{i}", 2 * KT, HALF)]
    plan += [("w_o", 2 * KT, HALF), ("up", FT * 2 * KT, P), ("down", 2 * FT, HALF)]
    for layer in range(2):
        plan += [(f"up1_{layer}", FT * 2 * KT, P), (f"down1_{layer}", 2 * FT, HALF)]
        if layer == 0:
            plan += [("even", 7 * KT, HALF), ("even_tail", KT, S), ("even_out", 2 * KT, HALF)]
        else:
            plan += [("odd", 6 * KT, HALF), ("odd_out", 2 * KT, HALF)]
        plan += [(f"wkv{layer}", 2 * KT, HALF), (f"wq{layer}", KT, HALF), (f"wo{layer}", 8, HALF)]
        plan += [(f"up2_{layer}", FT * 2 * KT, P), (f"down2_{layer}", 2 * FT, HALF)]
    out, first = {}, 0
    for name, count, width in plan:
        out[name] = Matrix(first, count, width)
        first += out[name].slots
    return out, first


def pack_stream(x):
    plan, slots = stream_plan()
    out = np.zeros((slots, P, SLOT), np.float32)

    def pairs(g, u):
        g, u = by_chunk(g, P), by_chunk(u, P)
        return [piece for f in range(FT) for piece in g[f * KT:(f + 1) * KT] + u[f * KT:(f + 1) * KT]]

    w_in = x["w_in"][0]
    tiles, rows = first_in_columns()
    pieces = {"in_t": by_chunk(w_in[:, tiles], P), "in_n": by_chunk(w_in[:, rows], HALF)}
    w1 = [x[n][0].reshape(32, DH, P) for n in ("nsa_phi_k_w1", "nsa_phi_v_w1")]
    pieces["phi"] = [np.concatenate([w[i] for w in w1], 0) for i in range(32)]
    pieces["mla"] = by_chunk(x["mla_w_uq"][0], HALF) + by_chunk(x["mla_w_ukv"][0], HALF)
    for i, n in enumerate("abcd"):
        pieces[f"branch{i}"] = by_chunk(x["w_branch_" + n][0], HALF)
        pieces[f"gate{i}"] = by_chunk(x["w_merge_gate"][0, i], HALF)
    pieces["w_o"] = by_tile(x["w_o"][0], HALF)
    up = x["ffn_w_up"][0]
    pieces["up"] = pairs(up[:, :FF], up[:, FF:])
    pieces["down"] = by_tile(x["ffn_w_down"][0], HALF)
    for layer in range(2):
        g = lambda n: x[f"l{layer}_{n}_2"]
        for n in (1, 2):
            pieces[f"up{n}_{layer}"] = pairs(g(f"ffn{n}_wg"), g(f"ffn{n}_wu"))
            pieces[f"down{n}_{layer}"] = by_tile(g(f"ffn{n}_wd"), HALF)
        pieces[f"wkv{layer}"] = by_chunk(g("mem_wkv"), HALF)
        pieces[f"wq{layer}"] = by_chunk(g("mem_wq"), HALF)
        pieces[f"wo{layer}"] = by_tile(g("mem_wo"), HALF)
        if layer == 0:
            main, tail = even_in_columns()
            pieces["even"] = by_chunk(g("w_in")[:, main], HALF)
            pieces["even_tail"] = by_chunk(g("w_in")[:, tail], S)
            pieces["even_out"] = by_tile(g("w_out"), HALF)
        else:
            pieces["odd"] = by_chunk(g("w_in"), HALF)
            pieces["odd_out"] = by_tile(g("w_out"), HALF)
    for name, m in plan.items():
        assert len(pieces[name]) == m.count, name
        for i, piece in enumerate(pieces[name]):
            at = m.offset(i)
            out[m.slot(i), :, at:at + piece.shape[1]] = piece
    return out


def pack_params(x):
    a = np.zeros((P, PARAM.n), np.float32)
    put = lambda n, v: PARAM(a, n).__setitem__(slice(None), v)
    twice = lambda v: np.concatenate([v, v])[:, None]
    put("mla_q", x["mla_q_norm"][0].reshape(2, P).T)
    put("mla_kv", x["mla_kv_norm"][0][:, None])
    for n, k in (("a_q", "l0_a_q_norm_2"), ("a_k", "l0_a_k_norm_2"), ("idx_k", "l0_idx_k_norm_2"),
                 ("b_q", "l0_b_q_norm_2"), ("b_k", "l0_b_k_norm_2"), ("c_q", "l1_c_q_norm_2"), ("c_k", "l1_c_k_norm_2")):
        put(n, twice(x[k]))
    put("subln", x["l0_b_subln_2"][:, None])
    for layer in range(2):
        put(f"mq{layer}", x[f"l{layer}_mem_q_norm_2"][:, None])
        put(f"mk{layer}", x[f"l{layer}_mem_k_norm_2"][:, None])
    put("conv_w", x["ffn_conv_w"][0].reshape(3 * 2 * FT, P).T)
    put("conv_b", x["ffn_conv_b"][0].reshape(2 * FT, P).T)
    pos = x["nsa_cmp_pos"][0].T
    put("cmp_pos", np.concatenate([pos, pos], 0))
    put("w2k", np.concatenate([x["nsa_phi_k_w2"][0]] * 2, 1))
    put("w2v", x["nsa_phi_v_w2"][0])
    put("lam", np.concatenate([x[f"l0_b_{n}_2"] for n in ("lq1", "lk1", "lq2", "lk2")])[None, :])
    put("f_bias", x["fox_forget_bias"][0][None, :])
    PARAM(a, "rel")[:32] = x["rel_bias_table"]
    PARAM(a, "t5")[:32] = x["t5_bias_2"]
    return a


def pack_rows(x):
    first = [x[n][0] for n in ("norm_attn_pre", "norm_ffn_pre", "norm_attn_post", "norm_ffn_post")]
    rest = [x[f"l{layer}_{n}_2"] for layer in range(2)
            for n in ("ffn1_norm", "mix_norm", "mem_src_norm", "mem_norm", "ffn2_norm")]
    return np.stack(first + rest)


def pack_band_bias(x):
    table = x["l1_c_rel_bias_2"]
    return np.ascontiguousarray(table[511 - np.arange(TOE)].T)



NAMES = ["squares_ready", "sums_ready", "means_ready", "roots_ready", "rows_scaled", "tiles_turned",
         "turned_by_act", "turned_by_dve", "highs_ready", "banks_filled", "drained_by_act", "drained_by_dve",
         "gates_ready", "hidden_ready", "convolved", "scores_ready", "logits_ready", "probs_ready",
         "probs_turned", "probs_copied", "out_ready", "out_taken", "inputs_ready", "partial_ready",
         "act_step", "dve_step", "pool_step"]


class Steps:

    def __init__(self, engine, sem):
        self.engine, self.sem, self.n = engine, sem, 0

    def __call__(self, instruction):
        self.n += 1
        instruction.then_inc(self.sem, 1)
        self.engine.wait_ge(self.sem, self.n)


class Core:

    def __init__(self, nc, stream):
        self.nc = nc
        self.plan, self.slots = stream_plan()
        self.stream = stream
        phi = self.plan["phi"]
        self.unsplit = range(phi.first, phi.first + phi.slots)
        self.top = -(-nc.sbuf_base // 64) * 64
        self.limit = nc.sbuf_usable_end
        t = self.tile
        raw_at = self.top
        self.raw = t("raw", [P, RING, SLOT])
        self.low = self.over("low", [P, RING, SLOT], F32R, raw_at)
        self.high = t("high", [P, RING, SLOT], F32R)
        self.h = t("h", [P, NB, D])
        self.xh = t("xh", [P, KT, S], F32R)
        self.xl = t("xl", [P, KT, S], F32R)
        arena = self.top
        self.u = t("u", [P, NB, 3720])
        self.o = t("o", [P, NB, D])
        self.small_rows = self.over("small_rows", [P, 2, TOE], F32, self.top - NB * D * 4)
        self.top = max(self.top, arena + 2 * FT * S * 4)
        self.hh = self.over("hh", [P, FT, S], F32R, arena)
        self.hl = self.over("hl", [P, FT, S], F32R, arena + FT * S * 4)
        turned = self.top
        self.t = t("t", [P, 24, S])
        self.oh = self.over("oh", [P, KT, S], F32R, turned)
        self.ol = self.over("ol", [P, KT, S], F32R, turned + KT * S * 4)
        xn = self.xn_at = self.top
        self.xn = t("xn", [P, NB, D])
        self.latent_h = self.over("latent_h", [P, 3, S], F32R, xn)
        self.latent_l = self.over("latent_l", [P, 3, S], F32R, xn + 3 * S * 4)
        self.forget = self.over("forget", [P, NB, 4, S], F32, xn)
        self.taken = self.over("taken", [P, NB, S], F32, xn)
        work = self.top
        self.prob = t("prob", [P, 4, 2, S])
        self.prob_t = t("prob_t", [P, 2, 4, P])
        self.square = self.over("square", [P, 3, D], F32, work)
        self.bias = t("bias", [P, 16, S])
        self.gain = t("gain", [P, D])
        self.gain2 = t("gain2", [P, D])
        self.const = t("const", [P, CONST.n])
        self.param = t("param", [P, PARAM.n])
        self.stat = t("stat", [P, 80])
        self.nmax = t("nmax", [P, 64])
        self.den = t("den", [P, 64])
        self.rden = t("rden", [P, 64])
        self.small = t("small", [P, 192])
        self.ident = CONST(self.const, "ident")
        self.products = self.u[:, 1, 2600:3368].rearrange("p (b g h d) -> p b g h d", b=NB, g=3, h=2)
        self.bank = [nc.alloc_psum_tensor(f"bank{i}", [P, HALF], F32) for i in range(8)]
        sem = nc.alloc_semaphore
        self.slot_loaded = [sem(f"slot_loaded{i}") for i in range(RING)]
        self.high_split, self.low_split, self.slot_used = sem("high_split"), sem("low_split"), sem("slot_used")
        self.stage_done, self.loaded, self.stored = sem("stage_done"), sem("loaded"), sem("stored")
        self.bounced = sem("bounced")
        self.sets = [{n: sem(f"{n}_{'even' if i == 0 else 'odd'}") for n in NAMES} for i in range(2)]
        self.act_next = self.dve_next = 0
        self.loads = 0

    def tile(self, name, shape, dtype=F32):
        size = int(np.prod(shape[1:])) * 4
        out = self.nc.alloc_sbuf_tensor_at(name, shape, dtype, offset=self.top)
        self.top += -(-size // 64) * 64
        assert self.top <= self.limit, (name, self.top, self.limit)
        return out

    def over(self, name, shape, dtype, at):
        return self.nc.alloc_sbuf_tensor_at(name, shape, dtype, offset=at)

    def split_high(self, act, last):
        for n in range(self.act_next, min(last + LEAD, self.slots - 1) + 1):
            act.wait_ge(self.slot_loaded[n % RING], 16 * (n // RING + 1))
            act.activation(self.high[:, n % RING, :], self.raw[:, n % RING, :], ACT.Copy).then_inc(self.high_split, 1)
            self.act_next = n + 1

    def split_low(self, dve, last):
        for n in range(self.dve_next, min(last + LEAD, self.slots - 1) + 1):
            dve.wait_ge(self.high_split, n + 1)
            if n in self.unsplit:
                dve.drain().then_inc(self.low_split, 1)
                self.dve_next = n + 1
                continue
            dve.tensor_tensor(self.low[:, n % RING, :], self.raw[:, n % RING, :],
                              self.high[:, n % RING, :].bitcast(F32), ALU.subtract).then_inc(self.low_split, 1)
            self.dve_next = n + 1

    def piece(self, pe, m, i, width=None):
        if i % m.per == 0:
            pe.wait_ge(self.low_split, m.slot(i) + 1)
        at, r = m.offset(i), m.slot(i) % RING
        cut = slice(at, at + (width or m.width))
        return self.high[:, r, cut], self.low[:, r, cut]

    def release(self, instruction, m, i):
        if m.ends_slot(i):
            instruction.then_inc(self.slot_used, 1)

    def finish_output(self, instruction, m, i, s):
        instruction.then_inc(self.slot_used if m.ends_slot(i) else s["banks_filled"], 1)

    def wait_output(self, engine, m, i, s, others):
        if m.ends_slot(i):
            engine.wait_ge(self.slot_used, m.slot(i) + 1)
        else:
            engine.wait_ge(s["banks_filled"], others)


def mm3(pe, out, left, right, start, stop):
    (lh, ll), (rh, rl) = left, right
    pe.matmul(out, lh, rh, start=start, stop=False)
    pe.matmul(out, lh, rl, start=False, stop=False)
    return pe.matmul(out, ll, rh, start=False, stop=stop)


def mm(pe, out, left, right, start, stop):
    return pe.matmul(out, left, right, start=start, stop=stop)


class Stage:
    def __init__(self, core):
        self.core = core

    def tensor(self, pe, s):
        pass

    def scalar(self, act, s):
        pass

    def vector(self, dve, s):
        pass

    def gpsimd(self, pool, s):
        pass


class Setup(Stage):

    def __init__(self, core, dram):
        super().__init__(core)
        self.dram = dram
        self.table = core.u[:, 0, 0:TABLE.n]

    def gpsimd(self, pool, s):
        c = self.core
        pool.dma_start(c.const[:, :], self.dram["const"]).then_inc(c.loaded, 16)
        pool.dma_start(c.param[:, :], self.dram["param"]).then_inc(c.loaded, 16)
        pool.dma_start(self.table, self.dram["table"]).then_inc(c.loaded, 16)
        pool.dma_start(c.h[:, :, :], self.dram["x"].rearrange("(b p) d -> p b d", p=P)).then_inc(c.loaded, 16)
        pool.dma_start(c.gain[:, :], self.dram["rows"][0:1, :].to_broadcast([P, D])).then_inc(c.loaded, 16)
        c.loads += 5
        pool.wait_ge(c.loaded, 16 * c.loads)
        pool.wait_ge(s["out_taken"], 2)
        pool.dma_start(self.dram["rel_rows"], c.small_rows[0:10, 0, :]).then_inc(c.bounced, 16)
        pool.dma_start(self.dram["t5_rows"], c.small_rows[0:12, 1, :]).then_inc(c.bounced, 16)
        pool.wait_ge(c.bounced, 32)

    def tensor(self, pe, s):
        c = self.core
        pe.wait_ge(c.loaded, 80)
        mm(pe, c.bank[0][0:10, 0:TOE], PARAM(c.param, "rel")[0:32], TABLE(self.table, "hot_rel")[0:32],
           True, True).then_inc(s["out_ready"], 1)
        mm(pe, c.bank[1][0:12, 0:TOE], PARAM(c.param, "t5")[0:32], TABLE(self.table, "hot_t5")[0:32],
           True, True).then_inc(s["out_ready"], 1)

    def scalar(self, act, s):
        c = self.core
        act.wait_ge(c.loaded, 80)
        c.split_high(act, 0)

    def vector(self, dve, s):
        c = self.core
        dve.wait_ge(c.loaded, 80)
        dve.wait_ge(s["out_ready"], 2)
        dve.tensor_tensor(c.small_rows[0:10, 0, :], c.bank[0][0:10, 0:TOE], TABLE(self.table, "rel_mask")[0:10],
                          ALU.add).then_inc(s["out_taken"], 1)
        dve.tensor_copy(c.small_rows[0:12, 1, :], c.bank[1][0:12, 0:TOE]).then_inc(s["out_taken"], 1)
        c.split_low(dve, 0)


class Loads:

    def __init__(self, *pairs):
        self.pairs = pairs

    def start(self, core, pool):
        for dst, src in self.pairs:
            pool.dma_start(dst, src).then_inc(core.loaded, 16)
            core.loads += 1

    def finish(self, core, pool):
        pool.wait_ge(core.loaded, 16 * core.loads)


def spread(rows, wide):
    heads = rows.shape[0]
    return wide[0:heads], bass.AP(tensor=rows.tensor, offset=rows.offset, ap=[[TOE, heads], [0, P], [1, TOE]])


def toeplitz(wide, heads):
    return bass.AP(tensor=wide.tensor, offset=wide.offset + P - 1, ap=[[TOE - 1, P], [P * TOE, heads], [1, S]])


class Turn(Stage):

    def __init__(self, core, segments, groups, loads=None):
        super().__init__(core)
        self.segments, self.groups, self.loads = segments, groups, loads
        cols, self.at = 0, []
        for src, *_ in segments:
            self.at.append(cols)
            cols += src.shape[1]
        self.cols = cols
        assert cols <= 80
        self.by = [("act", "dve") if g[3] == "pair" else (("act",) if i % 2 == 0 else ("dve",))
                   for i, g in enumerate(groups)]

    def drained(self, engine, g):
        return sum(engine in b for b in self.by[:g + 1])

    def gpsimd(self, pool, s):
        if self.loads:
            self.loads.start(self.core, pool)
            self.loads.finish(self.core, pool)

    def tensor(self, pe, s):
        c = self.core
        for g, (need, sources, width, kind, dst, gain) in enumerate(self.groups):
            if need:
                pe.wait_ge(s["rows_scaled"], need)
            if g >= 4:
                if self.drained("act", g - 4):
                    pe.wait_ge(s["turned_by_act"], self.drained("act", g - 4))
                if self.drained("dve", g - 4):
                    pe.wait_ge(s["turned_by_dve"], self.drained("dve", g - 4))
            for j, src in enumerate(sources):
                last = pe.transpose(c.bank[g % 4][0:width, j * P:(j + 1) * P], src, self.core.ident)
            last.then_inc(s["tiles_turned"], 1)

    def scalar(self, act, s):
        c = self.core
        for i, (src, dst, gain, factor) in enumerate(self.segments):
            if i >= 3:
                act.wait_ge(s["sums_ready"], i - 2)
            h, w = src.shape[1], src.shape[2]
            sq = c.square[:, i % 3, 0:h * w].rearrange("p (h w) -> p h w", w=w)
            act.activation(sq, src, ACT.Square).then_inc(s["squares_ready"], 1)
        if self.segments:
            act.wait_ge(s["means_ready"], 1)
            act.activation(c.stat[:, 0:self.cols], c.stat[:, 0:self.cols], ACT.Sqrt).then_inc(s["roots_ready"], 1)
        for g, (need, sources, width, kind, dst, gain) in enumerate(self.groups):
            if "act" not in self.by[g]:
                continue
            act.wait_ge(s["tiles_turned"], g + 1)
            ps = c.bank[g % 4][0:width, 0:len(sources) * P].rearrange("p (n q) -> p n q", q=P)
            out = dst[0] if kind == "pair" else dst
            if gain is None:
                i = act.activation(out, ps, ACT.Copy)
            else:
                i = act.activation(out, ps, ACT.Copy, scale=gain)
            i.then_inc(s["turned_by_act"], 1)

    def vector(self, dve, s):
        c = self.core
        step = Steps(dve, s["dve_step"])
        for i, (src, dst, gain, factor) in enumerate(self.segments):
            h, w = src.shape[1], src.shape[2]
            dve.wait_ge(s["squares_ready"], i + 1)
            sq = c.square[:, i % 3, 0:h * w].rearrange("p (h w) -> p h w", w=w)
            dve.tensor_reduce(c.stat[:, self.at[i]:self.at[i] + h], sq, AX.X, ALU.add).then_inc(s["sums_ready"], 1)
        if self.segments:
            dve.wait_ge(s["sums_ready"], len(self.segments))
        for i, (src, dst, gain, factor) in enumerate(self.segments):
            h, w = src.shape[1], src.shape[2]
            f2 = factor * factor
            m = dve.tensor_scalar(c.stat[:, self.at[i]:self.at[i] + h], c.stat[:, self.at[i]:self.at[i] + h],
                                  1.0 / (w * f2), EPS / f2, ALU.mult, ALU.add)
            step(m)
        if self.segments:
            dve.sem_inc(s["means_ready"], 1)
            dve.wait_ge(s["roots_ready"], 1)
            step(dve.reciprocal(c.stat[:, 0:self.cols], c.stat[:, 0:self.cols]))
        for i, (src, dst, gain, factor) in enumerate(self.segments):
            h, w = src.shape[1], src.shape[2]
            dst = src if dst is None else dst
            r = c.stat[:, self.at[i]:self.at[i] + h]
            if gain is not None:
                m = dve.scalar_tensor_tensor(dst[:, 0, :], src[:, 0, :], r, gain, ALU.mult, ALU.mult)
            elif h == 1:
                m = dve.tensor_scalar(dst[:, 0, :], src[:, 0, :], r, None, ALU.mult)
            else:
                m = dve.tensor_tensor(dst, src, r.unsqueeze(2).to_broadcast([P, h, w]), ALU.mult)
            m.then_inc(s["rows_scaled"], 1)
        for g, (need, sources, width, kind, dst, gain) in enumerate(self.groups):
            if "dve" not in self.by[g]:
                continue
            ps = c.bank[g % 4][0:width, 0:len(sources) * P].rearrange("p (n q) -> p n q", q=P)
            dve.wait_ge(s["tiles_turned"], g + 1)
            if kind == "pair":
                dve.wait_ge(s["turned_by_act"], self.drained("act", g))
                hi = dst[0].bitcast(F32)
                if gain is None:
                    i = dve.tensor_tensor(dst[1], ps, hi, ALU.subtract)
                else:
                    i = dve.scalar_tensor_tensor(dst[1], ps, gain, hi, ALU.mult, ALU.subtract)
            elif gain is None:
                i = dve.tensor_copy(dst, ps)
            else:
                i = dve.tensor_scalar(dst, ps, gain, None, ALU.mult)
            i.then_inc(s["turned_by_dve"], 1)


def norm_turn(core, src, gain, dst_h, dst_l, loads=None, norm=True):
    segments, groups = [], []
    for b in range(NB):
        rows = src[:, b:b + 1, :]
        if norm:
            segments.append((rows, core.xn[:, b:b + 1, :], gain, 1.0))
        rows = core.xn[:, b, :] if norm else src[:, b, :]
        for q in range(KT // 4):
            tiles = [rows[:, (4 * q + j) * P:(4 * q + j + 1) * P] for j in range(4)]
            cut = (slice(None), slice(4 * q, 4 * q + 4), slice(b * P, (b + 1) * P))
            groups.append((b + 1 if norm else 0, tiles, P, "pair", (dst_h[cut], dst_l[cut]), None))
    return Turn(core, segments, groups, loads)


class ProjectTurned(Stage):

    def __init__(self, core, name, tiles, loads=None):
        super().__init__(core)
        self.m, self.tiles, self.loads = core.plan[name], tiles, loads
        self.last = [(t + 1) * KT - 1 for t in range(tiles)]
        self.others = [sum(not self.m.ends_slot(i) for i in self.last[:t + 1]) for t in range(tiles)]

    def gpsimd(self, pool, s):
        if self.loads:
            self.loads.start(self.core, pool)
            self.loads.finish(self.core, pool)

    def tensor(self, pe, s):
        c = self.core
        for t in range(self.tiles):
            if t >= 4:
                pe.wait_ge(s["drained_by_act" if t % 2 == 0 else "drained_by_dve"], (t - 4) // 2 + 1)
            for k in range(KT):
                i = t * KT + k
                last = mm3(pe, c.bank[t % 4][:, 0:S], c.piece(pe, self.m, i), (c.xh[:, k, :], c.xl[:, k, :]),
                           k == 0, k == KT - 1)
            c.finish_output(last, self.m, i, s)

    def scalar(self, act, s):
        c = self.core
        for t in range(self.tiles):
            c.split_high(act, self.m.slot(self.last[t]))
            if t % 2 == 0:
                c.wait_output(act, self.m, self.last[t], s, self.others[t])
                act.activation(c.t[:, t, :], c.bank[t % 4][:, 0:S], ACT.Copy).then_inc(s["drained_by_act"], 1)

    def vector(self, dve, s):
        c = self.core
        for t in range(self.tiles):
            c.split_low(dve, self.m.slot(self.last[t]))
            if t % 2 == 1:
                c.wait_output(dve, self.m, self.last[t], s, self.others[t])
                dve.tensor_copy(c.t[:, t, :], c.bank[t % 4][:, 0:S]).then_inc(s["drained_by_dve"], 1)


class Project(Stage):

    def __init__(self, core, x, jobs, loads=None):
        super().__init__(core)
        self.x, self.jobs, self.loads = x, jobs, loads
        ends = [j[0].ends_slot(j[1] + len(j[2]) - 1) for j in jobs]
        self.others = [sum(not e for e in ends[:n + 1]) for n in range(len(jobs))]

    def gpsimd(self, pool, s):
        if self.loads:
            self.loads.start(self.core, pool)
            self.loads.finish(self.core, pool)

    def tensor(self, pe, s):
        c = self.core
        xh, xl = self.x
        for n, (m, i0, kts, width, dst) in enumerate(self.jobs):
            if n >= 2:
                pe.wait_ge(s["drained_by_act"], n - 1)
                pe.wait_ge(s["drained_by_dve"], n - 1)
            for j, k in enumerate(kts):
                w = c.piece(pe, m, i0 + j, width)
                for b in range(NB):
                    cut = slice(b * P, (b + 1) * P)
                    last = mm3(pe, c.bank[2 * (n % 2) + b][:, 0:width], (xh[:, k, cut], xl[:, k, cut]), w,
                               j == 0, j == len(kts) - 1)
                if j == len(kts) - 1:
                    c.finish_output(last, m, i0 + j, s)
                else:
                    c.release(last, m, i0 + j)

    def scalar(self, act, s):
        c = self.core
        for n, (m, i0, kts, width, dst) in enumerate(self.jobs):
            c.split_high(act, m.slot(i0 + len(kts) - 1))
            c.wait_output(act, m, i0 + len(kts) - 1, s, self.others[n])
            act.activation(dst[0], c.bank[2 * (n % 2)][:, 0:width], ACT.Copy).then_inc(s["drained_by_act"], 1)

    def vector(self, dve, s):
        c = self.core
        for n, (m, i0, kts, width, dst) in enumerate(self.jobs):
            c.split_low(dve, m.slot(i0 + len(kts) - 1))
            c.wait_output(dve, m, i0 + len(kts) - 1, s, self.others[n])
            dve.tensor_copy(dst[1], c.bank[2 * (n % 2) + 1][:, 0:width]).then_inc(s["drained_by_dve"], 1)


class Residual(Stage):

    def __init__(self, core, name, x, kts, factor=1.0, gain=None, loads=None):
        super().__init__(core)
        self.m, self.x, self.kts, self.factor, self.gain, self.loads = core.plan[name], x, kts, factor, gain, loads

    def gpsimd(self, pool, s):
        if self.loads:
            self.loads.start(self.core, pool)
            self.loads.finish(self.core, pool)

    def tensor(self, pe, s):
        c, m = self.core, self.m
        xh, xl = self.x
        for k in range(self.kts):
            self.input_wait(pe, s, k)
            for half in range(2):
                i = 2 * k + half
                w = c.piece(pe, m, i)
                for b in range(NB):
                    cut = slice(b * P, (b + 1) * P)
                    last = mm3(pe, c.bank[4 + 2 * b + half][:, :], (xh[:, k, cut], xl[:, k, cut]), w,
                               k == 0, k == self.kts - 1)
                c.release(last, m, i)

    def input_wait(self, pe, s, k):
        pass

    def scalar(self, act, s):
        c = self.core
        c.split_high(act, self.m.slot(self.m.count - 1))
        if self.gain is None:
            return
        act.wait_ge(c.slot_used, self.m.slot(self.m.count - 1) + 1)
        for b in range(NB):
            for half in range(2):
                act.activation(c.square[:, b, half * HALF:(half + 1) * HALF], c.bank[4 + 2 * b + half][:, :], ACT.Square,
                               accum_out=c.stat[:, 2 * b + half:2 * b + half + 1]).then_inc(s["squares_ready"], 1)
        act.wait_ge(s["means_ready"], 1)
        act.activation(c.stat[:, 4:6], c.stat[:, 4:6], ACT.Sqrt).then_inc(s["roots_ready"], 1)

    def vector(self, dve, s):
        c = self.core
        c.split_low(dve, self.m.slot(self.m.count - 1))
        step = Steps(dve, s["dve_step"])
        dve.wait_ge(c.slot_used, self.m.slot(self.m.count - 1) + 1)
        if self.gain is not None:
            dve.wait_ge(s["squares_ready"], 4)
            sums = c.stat[:, 0:4].rearrange("p (b f) -> p b f", f=2)
            step(dve.tensor_reduce(c.stat[:, 4:6], sums, AX.X, ALU.add))
            dve.tensor_scalar(c.stat[:, 4:6], c.stat[:, 4:6], 1.0 / D, EPS, ALU.mult, ALU.add)\
               .then_inc(s["means_ready"], 1)
            dve.wait_ge(s["roots_ready"], 1)
            step(dve.reciprocal(c.stat[:, 4:6], c.stat[:, 4:6]))
        for b in range(NB):
            for half in range(2):
                ps = c.bank[4 + 2 * b + half][:, :]
                cut = slice(half * HALF, (half + 1) * HALF)
                if self.gain is None:
                    dve.scalar_tensor_tensor(c.h[:, b, cut], ps, self.factor, c.h[:, b, cut], ALU.mult, ALU.add)
                else:
                    step(dve.scalar_tensor_tensor(c.xn[:, b, cut], ps, c.stat[:, 4 + b:5 + b],
                                                  self.gain[:, cut], ALU.mult, ALU.mult))
                    dve.tensor_tensor(c.h[:, b, cut], c.h[:, b, cut], c.xn[:, b, cut], ALU.add)


class Ffn(Residual):

    def __init__(self, core, up, down, factor=1.0, gain=None, conv=False, loads=None):
        super().__init__(core, down, (core.hh, core.hl), FT, factor, gain, loads)
        self.up, self.conv = core.plan[up], conv

    def tensor(self, pe, s):
        c = self.core
        for f in range(FT):
            if f >= 4:
                pe.wait_ge(s["hidden_ready"], f - 3)
            for part in range(2):
                for k in range(KT):
                    i = (2 * f + part) * KT + k
                    last = mm3(pe, c.bank[f % 4][:, part * S:(part + 1) * S], c.piece(pe, self.up, i),
                               (c.xh[:, k, :], c.xl[:, k, :]), k == 0, k == KT - 1)
                    c.release(last, self.up, i)
        super().tensor(pe, s)

    def input_wait(self, pe, s, k):
        pe.wait_ge(s["hidden_ready"], k + 1)

    def buffers(self, f):
        c = self.core
        gate, value = c.square[:, 0, (f % 2) * HALF:(f % 2) * HALF + S], c.square[:, 0, (f % 2) * HALF + S:(f % 2 + 1) * HALF]
        return gate, value, c.square[:, 1, (f % 2) * S:(f % 2 + 1) * S], c.square[:, 2, (f % 2) * S:(f % 2 + 1) * S]

    def scalar(self, act, s):
        c = self.core
        w = PARAM(c.param, "conv_w").rearrange("p (j f) -> p j f", j=3)
        bias = PARAM(c.param, "conv_b")
        for f in range(FT):
            c.split_high(act, self.up.first + f)
            ps = c.bank[f % 4]
            gate, value, silu, product = self.buffers(f)
            act.wait_ge(c.slot_used, self.up.first + f + 1)
            if f >= 2:
                act.wait_ge(s["gates_ready"], f - 1)
            if self.conv:
                act.activation(gate, ps[:, 0:S], ACT.Identity, bias=bias[:, f:f + 1], scale=w[:, 2, f:f + 1])
                act.activation(value, ps[:, S:HALF], ACT.Identity, bias=bias[:, FT + f:FT + f + 1],
                               scale=w[:, 2, FT + f:FT + f + 1]).then_inc(s["partial_ready"], 1)
                act.wait_ge(s["convolved"], f + 1)
                act.activation(silu, gate, ACT.Silu).then_inc(s["inputs_ready"], 1)
            else:
                act.activation(silu, ps[:, 0:S], ACT.Silu).then_inc(s["inputs_ready"], 1)
            act.wait_ge(s["gates_ready"], f + 1)
            act.activation(c.hh[:, f, :], product, ACT.Copy).then_inc(s["highs_ready"], 1)
        super().scalar(act, s)

    def vector(self, dve, s):
        c = self.core
        step = Steps(dve, s["pool_step"])
        w = PARAM(c.param, "conv_w").rearrange("p (j f) -> p j f", j=3)
        for f in range(FT):
            c.split_low(dve, self.up.first + f)
            ps = c.bank[f % 4]
            gate, value, silu, product = self.buffers(f)
            if self.conv:
                dve.wait_ge(s["partial_ready"], f + 1)
                for j in (1, 0):
                    back = 2 - j
                    for part, buf, col in ((0, gate, f), (1, value, FT + f)):
                        i = dve.scalar_tensor_tensor(buf[:, back:S], ps[:, part * S:(part + 1) * S - back],
                                                     w[:, j, col:col + 1], buf[:, back:S], ALU.mult, ALU.add)
                        if j == 1 or part == 0:
                            step(i)
                        else:
                            i.then_inc(s["convolved"], 1)
                dve.wait_ge(s["convolved"], f + 1)
            dve.wait_ge(s["inputs_ready"], f + 1)
            if f >= 2:
                dve.wait_ge(s["highs_ready"], f - 1)
            dve.tensor_tensor(product, silu, value if self.conv else ps[:, S:HALF], ALU.mult)\
               .then_inc(s["gates_ready"], 1)
            dve.wait_ge(s["highs_ready"], f + 1)
            dve.tensor_tensor(c.hl[:, f, :], product, c.hh[:, f, :].bitcast(F32), ALU.subtract)\
               .then_inc(s["hidden_ready"], 1)
        super().vector(dve, s)


class Merge(Stage):

    TILES = ((0, 1), (2,), (3, 4), (5, 6))

    def tensor(self, pe, s):
        c = self.core
        for n in range(4):
            branch, gate = c.plan[f"branch{n}"], c.plan[f"gate{n}"]
            kts = self.TILES[n]
            if n:
                pe.wait_ge(s["out_taken"], 4 * n)
            for half in range(2):
                for j, k in enumerate(kts):
                    i = half * len(kts) + j
                    w = c.piece(pe, branch, i)
                    for b in range(NB):
                        cut = slice(b * P, (b + 1) * P)
                        last = mm3(pe, c.bank[4 + 2 * half + b][:, :], (c.oh[:, k, cut], c.ol[:, k, cut]), w,
                                   j == 0, j == len(kts) - 1)
                    c.release(last, branch, i)
            for half in range(2):
                for k in range(KT):
                    i = half * KT + k
                    w = c.piece(pe, gate, i)
                    for b in range(NB):
                        cut = slice(b * P, (b + 1) * P)
                        last = mm3(pe, c.bank[2 * half + b][:, :], (c.xh[:, k, cut], c.xl[:, k, cut]), w,
                                   k == 0, k == KT - 1)
                    c.release(last, gate, i)

    def scalar(self, act, s):
        c = self.core
        for n in range(4):
            gate = c.plan[f"gate{n}"]
            for half in range(2):
                c.split_high(act, gate.first + 2 * half + 1)
                act.wait_ge(c.slot_used, gate.first + 2 * half + 2)
                for b in range(NB):
                    q = 2 * half + b
                    if n:
                        act.wait_ge(s["out_taken"], 4 * (n - 1) + q + 1)
                    act.activation(c.square[:, q // 2, (q % 2) * HALF:(q % 2 + 1) * HALF], c.bank[q][:, :],
                                   ACT.Sigmoid).then_inc(s["gates_ready"], 1)

    def vector(self, dve, s):
        c = self.core
        step = Steps(dve, s["dve_step"])
        for n in range(4):
            gate = c.plan[f"gate{n}"]
            for half in range(2):
                c.split_low(dve, gate.first + 2 * half + 1)
                for b in range(NB):
                    q = 2 * half + b
                    dve.wait_ge(s["gates_ready"], 4 * n + q + 1)
                    g = c.square[:, q // 2, (q % 2) * HALF:(q % 2 + 1) * HALF]
                    out = c.xn[:, b, half * HALF:(half + 1) * HALF]
                    if n == 0:
                        dve.tensor_tensor(out, g, c.bank[4 + q][:, :], ALU.mult).then_inc(s["out_taken"], 1)
                    else:
                        dve.wait_ge(s["out_taken"], 4 * n + q)
                        step(dve.tensor_tensor(c.square[:, 2, 0:HALF], g, c.bank[4 + q][:, :], ALU.mult))
                        dve.tensor_tensor(out, out, c.square[:, 2, 0:HALF], ALU.add).then_inc(s["out_taken"], 1)


class Unit:

    def __init__(self, q, k, v, parts, scale, dv, finish, cols, bias=None, minus=False, extra=None):
        self.q, self.k, self.v, self.parts, self.scale, self.dv = q, k, v, parts, scale, dv
        self.finish, self.cols, self.bias, self.minus, self.extra = finish, cols, bias, minus, extra
        self.n, self.nk = len(q), sum(parts)


class Attention(Stage):
    def __init__(self, core, units, before=None, loads=None):
        super().__init__(core)
        self.units, self.before, self.loads = units, before, loads

    def gpsimd(self, pool, s):
        if self.loads:
            self.loads.start(self.core, pool)
            self.loads.finish(self.core, pool)

    SCORE_BANKS = (0, 1, 6)

    def scores(self, i):
        u = self.units[i]
        bank = self.core.bank[self.SCORE_BANKS[i % 3]]
        return bank[:, :].rearrange("p (n k) -> p n k", n=2)[:, 0:u.n, 0:u.nk]

    def tensor(self, pe, s):
        c, units = self.core, self.units

        def score(i):
            u = units[i]
            if i >= 3:
                pe.wait_ge(s["logits_ready" if units[i - 3].bias is not None else "probs_ready"], i - 2)
            ps = self.scores(i)
            for j in range(u.n):
                last = mm(pe, ps[:, j, :], u.q[j], u.k[j], True, True)
            last.then_inc(s["scores_ready"], 1)

        def turn(i):
            u = units[i]
            pe.wait_ge(s["probs_ready"], i + 1)
            if i >= 2:
                pe.wait_ge(s["probs_copied"], i - 1)
            for j in range(u.n):
                for t, size in enumerate(u.parts):
                    at = (j * len(u.parts) + t) * P
                    last = pe.transpose(c.bank[2 + i % 2][0:size, at:at + P],
                                        c.prob[:, i % 4, j, t * P:t * P + size], c.ident)
            last.then_inc(s["probs_turned"], 1)

        def value(i):
            u = units[i]
            pe.wait_ge(s["probs_copied"], i + 1)
            if i >= 2:
                pe.wait_ge(s["out_taken"], i - 1)
            for j in range(u.n):
                for t, size in enumerate(u.parts):
                    last = mm(pe, c.bank[4 + i % 2][:, j * u.dv:(j + 1) * u.dv],
                              c.prob_t[0:size, i % 2, j * len(u.parts) + t, :], u.v[j][t],
                              t == 0, t == len(u.parts) - 1)
            last.then_inc(s["out_ready"], 1)

        for i in range(min(3, len(units))):
            score(i)
        for i in range(len(units) + 1):
            if i < len(units):
                turn(i)
            if i + 3 < len(units):
                score(i + 3)
            if i:
                value(i - 1)

    def scalar(self, act, s):
        c, units = self.core, self.units
        c.split_high(act, -LEAD)

        def exp(i):
            u = units[i]
            act.wait_ge(s["logits_ready"], i + 1)
            if i >= 4:
                act.wait_ge(s["probs_turned"], i - 3)
            for j in range(u.n):
                dst = c.prob[:, i % 4, j, 0:u.nk]
                src, scale = (dst, 1.0) if u.bias is not None else (self.scores(i)[:, j, :], u.scale)
                col = u.cols.start + j * (u.cols.step or 1)
                last = act.activation(dst, src, ACT.Exp, bias=c.nmax[:, col:col + 1],
                                      scale=scale, accum_out=c.den[:, col:col + 1])
            last.then_inc(s["probs_ready"], 1)

        exp(0)
        for i, u in enumerate(units):
            if i + 1 < len(units):
                exp(i + 1)
            act.wait_ge(s["probs_turned"], i + 1)
            if i >= 2:
                act.wait_ge(s["out_ready"], i - 1)
            size, tiles = u.parts[0], u.n * len(u.parts)
            act.activation(c.prob_t[0:size, i % 2, 0:tiles, :],
                           c.bank[2 + i % 2][0:size, 0:tiles * P].rearrange("p (n q) -> p n q", q=P),
                           ACT.Copy).then_inc(s["probs_copied"], 1)

    def vector(self, dve, s):
        c, units = self.core, self.units
        step = Steps(dve, s["dve_step"])

        def logits(i):
            u = units[i]
            dve.wait_ge(s["scores_ready"], i + 1)
            if i >= 4:
                dve.wait_ge(s["probs_turned"], i - 3)
            ps = self.scores(i)
            if u.bias is None:
                step(dve.tensor_reduce(c.nmax[:, u.cols], ps, AX.X, ALU.max, negate=True))
                dve.tensor_scalar(c.nmax[:, u.cols], c.nmax[:, u.cols], u.scale, None, ALU.mult)\
                   .then_inc(s["logits_ready"], 1)
                return
            t = c.prob[:, i % 4, 0:u.n, 0:u.nk]
            step(dve.scalar_tensor_tensor(t, ps, u.scale, u.bias, ALU.mult, ALU.subtract if u.minus else ALU.add))
            if u.extra is not None:
                step(dve.tensor_tensor(t, t, u.extra, ALU.add))
            dve.tensor_reduce(c.nmax[:, u.cols], t, AX.X, ALU.max, negate=True).then_inc(s["logits_ready"], 1)

        def finish(i):
            u = units[i]
            dve.wait_ge(s["out_ready"], i + 1)
            if i:
                dve.wait_ge(s["out_taken"], i)
            ps = c.bank[4 + i % 2][:, 0:u.n * u.dv].rearrange("p (n d) -> p n d", n=u.n)
            u.finish(dve, step, u, ps).then_inc(s["out_taken"], 1)

        logits(0)
        logits(1)
        for i in range(len(units) + 2):
            if i + 2 < len(units):
                logits(i + 2)
            if i >= 2:
                finish(i - 2)


def scaled(core, dst, factor=None, add=False):

    def finish(dve, step, u, ps):
        r = core.rden[:, u.cols]
        step(dve.reciprocal(r, core.den[:, u.cols]))
        if factor is not None:
            step(dve.tensor_tensor(r, r, factor, ALU.mult))
        if not add:
            return dve.tensor_tensor(dst, ps, r.unsqueeze(2).to_broadcast([P, u.n, u.dv]), ALU.mult)
        for j in range(u.n):
            col = u.cols.start + j * (u.cols.step or 1)
            last = dve.scalar_tensor_tensor(dst[:, j, :], ps[:, j, :], core.rden[:, col:col + 1], dst[:, j, :],
                                            ALU.mult, ALU.add)
        return last

    return finish


def kept(core, dst):
    return lambda dve, step, u, ps: dve.tensor_copy(dst, ps)


class Compress(Stage):

    def __init__(self, core):
        super().__init__(core)
        c = core
        self.m = c.plan["phi"]
        free = c.u[:, 0, 2600:3720]
        self.x = free[:, 0:512].rearrange("p (l c) -> p l c", c=16)
        self.xh = c.over("blocks_h", [P, 32, 16], F32R, c.xn_at)
        self.xl = c.over("blocks_l", [P, 32, 16], F32R, c.xn_at + 512 * 4)
        self.g = free[:, 512:544].rearrange("p (a c) -> p a c", a=2)
        self.v = core.small[:, 0:DH]
        self.k = core.small[:, DH:DH + 16]
        self.lf = free[:, 560:568].rearrange("p (b h) -> p b h", b=NB)
        self.t1 = free[:, 576:584].rearrange("p (b h) -> p b h", b=NB)
        self.t2 = free[:, 592:600].rearrange("p (b h) -> p b h", b=NB)
        self.cq = free[:, 608:616].rearrange("p (b h) -> p b h", b=NB)
        self.spread = c.square[:, 0, :].rearrange("p (b h q) -> p b h q", b=NB, h=4)
        self.gates = core.small[:, 96:96 + 24].rearrange("p (b g) -> p b g", b=NB)
        self.cmp_gates = core.small[:, 128:136].rearrange("p (b h) -> p b h", b=NB)

    def tensor(self, pe, s):
        c = self.core
        pe.wait_ge(s["inputs_ready"], 1)
        for l in range(32):
            c.piece(pe, self.m, l)
            w = c.raw[:, self.m.slot(l) % RING, self.m.offset(l):self.m.offset(l) + P]
            for part, rows in ((0, slice(0, DH)), (1, slice(DH, P))):
                last = mm(pe, c.bank[part][:, 0:16], w[rows], self.x[rows, l, :],
                           l == 0, l == 31)
            c.release(last, self.m, l)
        pe.wait_ge(s["partial_ready"], 1)
        upto, ones = CONST(c.const, "upto"), CONST(c.const, "ones")
        mm(pe, c.bank[2][:, 0:4], upto, self.lf[:, 0, :], True, True)
        mm(pe, c.bank[2][:, 4:8], ones, self.lf[:, 0, :], True, False)
        mm(pe, c.bank[2][:, 4:8], upto, self.lf[:, 1, :], False, True).then_inc(s["scores_ready"], 1)
        for h in range(4):
            ps = c.bank[3 + h // 2][:, (h % 2) * S:(h % 2 + 1) * S]
            mm(pe, ps[:, 0:P], self.spread[:, 0, h, :], upto, True, True)
            mm(pe, ps[:, P:S], self.spread[:, 0, h, :], ones, True, False)
            last = mm(pe, ps[:, P:S], self.spread[:, 1, h, :], upto, False, True)
        last.then_inc(s["scores_ready"], 1)
        pe.wait_ge(s["gates_ready"], 1)
        mm(pe, c.bank[5][:, 0:16], PARAM(c.param, "w2k"), self.g[:, 0, :], True, True)
        mm(pe, c.bank[6][0:16, 0:DH], self.g[:, 1, :], PARAM(c.param, "w2v"), True, True).then_inc(s["out_ready"], 1)

    def scalar(self, act, s):
        c = self.core
        act.wait_ge(s["convolved"], 1)
        act.activation(self.xh[:, :, :], self.x, ACT.Copy).then_inc(s["highs_ready"], 1)
        c.split_high(act, self.m.first + self.m.slots - 1)
        step = Steps(act, s["act_step"])
        act.wait_ge(s["sums_ready"], 1)
        step(act.activation(self.t2, self.t1, ACT.Abs))
        step(act.activation(self.t2, self.t2, ACT.Exp, scale=-1.0))
        act.activation(self.t2, self.t2, ACT.Ln, bias=1.0).then_inc(s["means_ready"], 1)
        for b in range(NB):
            last = act.activation(self.gates[:, b, :], c.u[:, b, 128:140], ACT.Sigmoid)
        last.then_inc(s["roots_ready"], 1)
        act.wait_ge(c.slot_used, self.m.first + self.m.slots)
        act.activation(self.g[:, 0, :], c.bank[0][:, 0:16], ACT.Gelu_apprx_tanh)
        act.activation(self.g[:, 1, :], c.bank[1][:, 0:16], ACT.Gelu_apprx_tanh).then_inc(s["gates_ready"], 1)

    def vector(self, dve, s):
        c = self.core
        step = Steps(dve, s["dve_step"])
        step(dve.memset(self.x[:, :, 15:16], 0.0))
        tok = c.t[:, 4, :].rearrange("p (c l) -> p l c", l=16)
        pos = PARAM(c.param, "cmp_pos")
        for part in range(2):
            cut = slice(16 * part, 16 * part + 16)
            last = dve.tensor_tensor(self.x[:, cut, 0:15], tok[:, :, part:part + 15],
                                     pos[:, cut].unsqueeze(2).to_broadcast([P, 16, 15]), ALU.add)
        last.then_inc(s["convolved"], 1)
        dve.wait_ge(s["highs_ready"], 1)
        dve.tensor_tensor(self.xl[:, :, :], self.x, self.xh[:, :, :].bitcast(F32), ALU.subtract)\
           .then_inc(s["inputs_ready"], 1)
        bias = PARAM(c.param, "f_bias")
        for b in range(NB):
            last = dve.tensor_tensor(self.t1[:, b, :], c.u[:, b, 780:784], bias, ALU.add)
        last.then_inc(s["sums_ready"], 1)
        c.split_low(dve, self.m.first + self.m.slots - 1)
        dve.wait_ge(s["means_ready"], 1)
        step(dve.scalar_tensor_tensor(self.lf, self.t1, 0.0, self.t2, ALU.min, ALU.subtract))
        dve.tensor_copy(self.spread, self.lf.unsqueeze(3).to_broadcast([P, NB, 4, P]))\
           .then_inc(s["partial_ready"], 1)
        dve.wait_ge(s["roots_ready"], 1)
        gates = self.gates.rearrange("p b (h r) -> p b h r", r=3)
        for b in range(NB):
            dve.tensor_scalar(self.cmp_gates[:, b, :], gates[:, b, :, 0], CONST(c.const, "cmp_valid")[:, b:b + 1],
                              None, ALU.mult)
        dve.wait_ge(s["scores_ready"], 2)
        step(dve.tensor_copy(self.cq, c.bank[2][:, 0:8].rearrange("p (b h) -> p b h", b=NB)))
        causal = CONST(c.const, "causal")
        for b in range(NB):
            nk = (b + 1) * P
            for h in range(4):
                ps = c.bank[3 + h // 2][:, (h % 2) * S:(h % 2) * S + nk]
                dve.scalar_tensor_tensor(c.forget[:, b, h, 0:nk], ps, self.cq[:, b, h:h + 1], causal[:, S - nk:S],
                                         ALU.subtract, ALU.subtract)
        dve.wait_ge(s["out_ready"], 1)
        dve.tensor_copy(self.k[:, 0:15], c.bank[5][:, 0:15])
        dve.tensor_copy(self.v[0:15, :], c.bank[6][0:15, 0:DH])


class Rope(Stage):

    def __init__(self, core, q, kv, rope, k):
        super().__init__(core)
        self.q, self.kv, self.rope, self.k = q, kv, rope, k

    def vector(self, dve, s):
        c = self.core
        step = Steps(dve, s["dve_step"])
        for b in range(NB):
            cos = CONST(c.const, "cos")[:, 16 * b:16 * b + 16]
            sin = CONST(c.const, "sin")[:, 16 * b:16 * b + 16]
            q = self.q(b).rearrange("p (h d) -> p h d", h=4)
            k = self.k(b).rearrange("p (h d) -> p h d", h=4)
            kv = self.kv(b).rearrange("p (h d) -> p h d", h=4)
            rope = self.rope(b).unsqueeze(1)
            for n, x in ((4, q[:, :, DH:96]), (1, rope)):
                t = c.square[:, b, 0:4 * n * 16].rearrange("p (a h d) -> p a h d", a=4, h=n)
                w = lambda a: a.unsqueeze(1).to_broadcast([P, n, 16])
                x1, x2 = x[:, :, 0:16], x[:, :, 16:32]
                dve.tensor_tensor(t[:, 0], x1, w(cos), ALU.mult)
                dve.tensor_tensor(t[:, 1], x2, w(sin), ALU.mult)
                dve.tensor_tensor(t[:, 2], x2, w(cos), ALU.mult)
                step(dve.tensor_tensor(t[:, 3], x1, w(sin), ALU.mult))
                dve.tensor_tensor(x1, t[:, 0], t[:, 1], ALU.subtract)
                step(dve.tensor_tensor(x2, t[:, 2], t[:, 3], ALU.add))
            dve.tensor_copy(k[:, :, 0:DH], kv[:, :, 0:DH])
            dve.tensor_copy(k[:, :, DH:96], rope.to_broadcast([P, 4, 32]))


class Dilated(Stage):

    def __init__(self, core, kept_products, base):
        super().__init__(core)
        c = core
        cut = slice(base, base + 12)
        shape = lambda a: a.rearrange("p (b g h) -> p b g h", b=NB, g=3)
        self.nm, self.den = shape(c.nmax[:, cut]), shape(c.den[:, cut])
        self.e = shape(c.rden[:, cut])
        self.m = c.stat[:, 0:4].rearrange("p (b h) -> p b h", b=NB)
        self.sum = c.stat[:, 4:8].rearrange("p (b h) -> p b h", b=NB)
        self.products = kept_products
        self.t = c.square[:, 0, 0:768].rearrange("p (b g h d) -> p b g h d", b=NB, g=3, h=2)

    def scalar(self, act, s):
        act.wait_ge(s["inputs_ready"], 1)
        for b in range(NB):
            last = act.activation(self.e[:, b], self.e[:, b], ACT.Exp)
        last.then_inc(s["probs_ready"], 1)

    def vector(self, dve, s):
        step = Steps(dve, s["dve_step"])
        nm, den, e, m, total = self.nm, self.den, self.e, self.m, self.sum
        step(dve.tensor_tensor(m, nm[:, :, 0], nm[:, :, 1], ALU.min))
        step(dve.tensor_tensor(m, m, nm[:, :, 2], ALU.min))
        for g in range(3):
            last = dve.tensor_tensor(e[:, :, g], m, nm[:, :, g], ALU.subtract)
        last.then_inc(s["inputs_ready"], 1)
        dve.wait_ge(s["probs_ready"], 1)
        flat = lambda a: a.rearrange("p b g h -> p (b g h)")
        step(dve.tensor_tensor(self.core.stat[:, 16:28], flat(e), flat(den), ALU.mult))
        ed = self.core.stat[:, 16:28].rearrange("p (b g h) -> p b g h", b=NB, g=3)
        step(dve.tensor_tensor(total, ed[:, :, 0], ed[:, :, 1], ALU.add))
        step(dve.tensor_tensor(total, total, ed[:, :, 2], ALU.add))
        step(dve.reciprocal(total, total))
        for g in range(3):
            last = dve.tensor_tensor(e[:, :, g], e[:, :, g], total, ALU.mult)
        step(last)
        for b in range(NB):
            x = self.products[:, b].rearrange("p g h d -> p (g h) d")
            w = e[:, b].rearrange("p g h -> p (g h)").unsqueeze(2).to_broadcast([P, 6, DH])
            last = dve.tensor_tensor(self.t[:, b].rearrange("p g h d -> p (g h) d"), x, w, ALU.mult)
        step(last)
        for b in range(NB):
            out = self.core.o[:, b, 256:384].rearrange("p (h d) -> p h d", h=2)
            step(dve.tensor_tensor(out, self.t[:, b, 0], self.t[:, b, 1], ALU.add))
            dve.tensor_tensor(out, out, self.t[:, b, 2], ALU.add)


class Select(Stage):

    def __init__(self, core, q, k, weights):
        super().__init__(core)
        self.q, self.k, self.weights = q, k, weights
        c = core
        self.relu = c.square[:, 0, :].rearrange("p (n j k) -> p n j k", n=2, j=2)
        self.score = c.square[:, 1, 0:HALF].rearrange("p (b k) -> p b k", b=NB)
        self.best = c.square[:, 1, HALF:HALF + 16].rearrange("p (b k) -> p b k", b=NB)
        self.w = c.square[:, 2, 0:16].rearrange("p (b h) -> p b h", b=NB)
        self.units = [(b, pair) for b in range(NB) for pair in ((0, 2), (1, 3), (4, 6), (5, 7))]

    def tensor(self, pe, s):
        c = self.core
        for i, (b, pair) in enumerate(self.units):
            nk = (b + 1) * P
            if i >= 2:
                pe.wait_ge(s["probs_ready"], i - 1)
            for j, h in enumerate(pair):
                last = mm(pe, c.bank[i % 2][:, j * S:j * S + nk], self.q(h)[:, b * P:(b + 1) * P],
                          self.k(h)[:, 0:nk], True, True)
            last.then_inc(s["scores_ready"], 1)

    def scalar(self, act, s):
        c = self.core
        for i, (b, pair) in enumerate(self.units):
            nk = (b + 1) * P
            act.wait_ge(s["scores_ready"], i + 1)
            if i >= 2:
                act.wait_ge(s["out_taken"], i - 1)
            ps = c.bank[i % 2][:, :].rearrange("p (j k) -> p j k", j=2)[:, :, 0:nk]
            act.activation(self.relu[:, i % 2, :, 0:nk], ps, ACT.Relu, scale=DH ** -0.5)\
               .then_inc(s["probs_ready"], 1)

    def vector(self, dve, s):
        c = self.core
        step = Steps(dve, s["dve_step"])
        for b in range(NB):
            step(dve.tensor_scalar(self.w[:, b, :], self.weights(b), 8 ** -0.5, None, ALU.mult))
        for i, (b, pair) in enumerate(self.units):
            nk = (b + 1) * P
            dve.wait_ge(s["probs_ready"], i + 1)
            for j, h in enumerate(pair):
                r, score, w = self.relu[:, i % 2, j, 0:nk], self.score[:, b, 0:nk], self.w[:, b, h:h + 1]
                if i % 4 == 0 and j == 0:
                    step(dve.tensor_scalar(score, r, w, None, ALU.mult))
                else:
                    m = dve.scalar_tensor_tensor(score, r, w, score, ALU.mult, ALU.add)
                    if j == 0:
                        step(m)
            m.then_inc(s["out_taken"], 1)
            dve.wait_ge(s["out_taken"], i + 1)
        for b in range(NB):
            nk = (b + 1) * P
            score = self.score[:, b, 0:nk]
            step(dve.memset(score[0:DH, nk - DH:nk], NEG))
            for n in range(TOP_K // 8):
                step(dve.max(self.best[:, b, :], score))
                step(dve.match_replace(score, self.best[:, b, :], score, TAKEN))
            dve.tensor_scalar(c.taken[:, b, 0:nk], score, TAKEN, NEG, ALU.not_equal, ALU.mult)


class Lambda(Stage):

    def vector(self, dve, s):
        c = self.core
        step = Steps(dve, s["dve_step"])
        lam = PARAM(c.param, "lam").rearrange("p (n d) -> p n d", n=4)
        for n in range(2):
            step(dve.tensor_tensor(c.square[:, 0, n * DH:(n + 1) * DH], lam[:, 2 * n, :], lam[:, 2 * n + 1, :], ALU.mult))
        dve.tensor_reduce(c.small[:, 144:146], c.square[:, 0, 0:2 * DH].rearrange("p (n d) -> p n d", n=2),
                          AX.X, ALU.add).then_inc(s["sums_ready"], 1)
        dve.wait_ge(s["probs_ready"], 1)
        step(dve.tensor_tensor(c.small[:, 140:141], c.small[:, 147:148], c.small[:, 146:147], ALU.subtract))
        step(dve.tensor_scalar(c.small[:, 140:141], c.small[:, 140:141], -LAMBDA_INIT, None, ALU.add))
        dve.tensor_copy(c.small[:, 141:142], c.small[:, 140:141])
        dve.memset(c.bias[0:DH, 0:12, S - DH:S], NEG)

    def scalar(self, act, s):
        c = self.core
        act.wait_ge(s["sums_ready"], 1)
        act.activation(c.small[:, 146:148], c.small[:, 144:146], ACT.Exp).then_inc(s["probs_ready"], 1)


class MaskBand(Stage):

    def vector(self, dve, s):
        dve.memset(self.core.bias[0:DH, 0:16, S - DH:S], NEG)


LAMBDA_INIT = 0.8 - 0.6 * math.exp(0.0)


class Store(Stage):
    def __init__(self, core, out):
        super().__init__(core)
        self.out = out

    def gpsimd(self, pool, s):
        c = self.core
        pool.dma_start(self.out, c.h[:, :, :]).then_inc(c.stored, 16)
        pool.wait_ge(c.stored, 16)



def half(tile, h, cols=slice(None)):
    return tile[(h % 2) * DH:(h % 2 + 1) * DH, h // 2, cols]


def block_cut(b):
    return slice(b * P, (b + 1) * P)


def first_units(c, compress):
    units = []
    rel = c.bias
    pairs = ((0, 2), (1, 3))
    for b in range(NB):
        nk, parts = (b + 1) * P, [P] * (b + 1)
        keys, qs = slice(0, nk), block_cut(b)
        for pair in pairs:
            q = [half(c.t, h, qs) for h in pair]
            rows = slice((pair[0] % 2) * DH, (pair[0] % 2 + 1) * DH)
            heads = slice(pair[0], 4, 2)
            dst = c.o[:, b, 0:256].rearrange("p (h d) -> p h d", d=DH)[:, heads, :]
            gates = compress.gates[:, b, :].rearrange("p (h r) -> p h r", r=3)
            at = 2 * len(units)
            mask = CONST(c.const, "cmp_mask")[:, 15 * b:15 * b + 15].unsqueeze(1).to_broadcast([P, 2, 15])
            units.append(Unit(q, [compress.k[rows, 0:15]] * 2, [[compress.v[0:15, :]]] * 2, [15], DH ** -0.5, DH,
                              scaled(c, dst, compress.cmp_gates[:, b, heads]), slice(at, at + 2), mask))
            for r, (kt, v0) in enumerate(((2, 0), (3, DH)), 1):
                at = 2 * len(units)
                k = c.t[rows, kt, keys]
                v = [c.u[:, t, v0:v0 + DH] for t in range(b + 1)]
                units.append(Unit(q, [k, k], [v, v], parts, DH ** -0.5, DH, scaled(c, dst, gates[:, heads, r], add=True),
                                  slice(at, at + 2), rel[:, heads, S - nk:S]))
    base = 2 * len(units)
    for b in range(NB):
        nk, parts = (b + 1) * P, [P] * (b + 1)
        keys, qs = slice(0, nk), block_cut(b)
        for heads in ((0, 2), (1, 3), (4,), (5,)):
            q = [half(c.t[:, 5:8, :], h, qs) for h in heads]
            k = [half(c.t[:, 8:11, :], h, keys) for h in heads]
            v = [[c.u[:, t, 140 + h * DH:140 + (h + 1) * DH] for t in range(b + 1)] for h in heads]
            cut = slice(heads[0], heads[-1] + 1, 2)
            dst = c.products[:, b].rearrange("p g h d -> p (g h) d")[:, cut, :]
            units.append(Unit(q, k, v, parts, DH ** -0.5, DH, kept(c, dst),
                              slice(base + 6 * b + heads[0], base + 6 * b + heads[-1] + 1, 2),
                              rel[:, slice(4 + heads[0], 4 + heads[-1] + 1, 2), S - nk:S]))
    at = base + 12
    for b in range(NB):
        nk, parts = (b + 1) * P, [P] * (b + 1)
        keys, qs = slice(0, nk), block_cut(b)
        for pair in pairs:
            heads = slice(pair[0], 4, 2)
            v = [[c.u[:, t, 524 + h * DH:524 + (h + 1) * DH] for t in range(b + 1)] for h in pair]
            dst = c.o[:, b, 384:640].rearrange("p (h d) -> p h d", d=DH)[:, heads, :]
            units.append(Unit([half(c.t[:, 11:13, :], h, qs) for h in pair], [half(c.t[:, 13:15, :], h, keys) for h in pair],
                              v, parts, DH ** -0.5, DH, scaled(c, dst), slice(at, at + 2),
                              c.forget[:, b, heads, 0:nk], minus=True))
            at += 2
        for pair in ((0, 1), (2, 3)):
            heads = slice(pair[0], pair[0] + 2)
            v = [[c.u[:, t, 1584 + h * P + DH:1584 + (h + 1) * P] for t in range(b + 1)] for h in pair]
            dst = c.o[:, b, 640:896].rearrange("p (h d) -> p h d", d=DH)[:, heads, :]
            mask = CONST(c.const, "causal")[:, S - nk:S].unsqueeze(1).to_broadcast([P, 2, nk])
            units.append(Unit([c.t[0:96, 15 + h, qs] for h in pair], [c.t[0:96, 19 + h, keys] for h in pair], v, parts,
                              96 ** -0.5, DH, scaled(c, dst), slice(at, at + 2), mask))
            at += 2
    return units, base


def turn_groups(rows, tiles, dst, gain, need, t0, cut):
    return [(need, [rows[:, (q + j) * P:(q + j + 1) * P] for j in range(min(4, tiles - q))], P, "f32",
             dst[:, t0 + q:t0 + min(q + 4, tiles), cut], gain) for q in range(0, tiles, 4)]


def memory_stages(c, layer, dram, next_gain):
    u, t, heads = c.u, c.t, 4
    wkv, wq, wo = c.plan[f"wkv{layer}"], c.plan[f"wq{layer}"], c.plan[f"wo{layer}"]
    mem = c.u[:, :, 2048:3072]
    gain = lambda n: PARAM(c.param, f"{n}{layer}")
    out = [norm_turn(c, mem, c.gain[:, :], c.xh, c.xl,
                     Loads((c.gain2[:, :], dram_row(dram, f"l{layer}_mem"))))]
    out.append(Project(c, (c.xh, c.xl), [(wkv, n * KT, range(KT), HALF, [u[:, b, n * HALF:(n + 1) * HALF] for b in range(NB)])
                                         for n in range(2)]))
    out.append(norm_turn(c, c.h, c.gain2[:, :], c.xh, c.xl, Loads((c.gain[:, :], dram_row(dram, next_gain)))))
    out.append(Project(c, (c.xh, c.xl), [(wq, 0, range(KT), HALF, [u[:, b, D:D + HALF] for b in range(NB)])]))
    segments, groups = [], []
    for b in range(NB):
        for n, at in enumerate((0, D)):
            rows = u[:, b, at:at + HALF]
            segments.append((rows.rearrange("p (h d) -> p h d", h=heads), None, None, 1.0))
            groups += turn_groups(rows, heads, t, gain("mk" if n == 0 else "mq"), 2 * b + n + 1, 4 * n, block_cut(b))
    out.append(Turn(c, segments, groups))
    units = []
    for b in range(NB):
        for pair in ((0, 1), (2, 3)):
            at = 2 * len(units)
            dst = c.o[:, b, 0:HALF].rearrange("p (h d) -> p h d", h=heads)[:, pair[0]:pair[0] + 2, :]
            v = [[u[:, k, HALF + h * P:HALF + (h + 1) * P] for k in range(NB)] for h in pair]
            units.append(Unit([t[:, 4 + h, block_cut(b)] for h in pair], [t[:, h, :] for h in pair], v, [P, P],
                              P ** -0.5, P, scaled(c, dst), slice(at, at + 2)))
    out.append(Attention(c, units))
    out.append(out_turn(c, 4))
    out.append(Residual(c, f"wo{layer}", (c.oh, c.ol), heads))
    return out


def out_turn(c, tiles, gain=None, segments=()):
    groups = []
    for b in range(NB):
        for q in range(0, tiles, 4):
            n = min(4, tiles - q)
            cut = (slice(None), slice(q, q + n), block_cut(b))
            groups.append((len(segments), [c.o[:, b, (q + j) * P:(q + j + 1) * P] for j in range(n)], P, "pair",
                           (c.oh[cut], c.ol[cut]), gain if q >= 4 else None))
    return Turn(c, list(segments), groups)


def dram_row(dram, name):
    n = ROWS.index(name)
    return dram["rows"][n:n + 1, :].to_broadcast([P, D])


def first_mixer(c, dram):
    x, u = (c.xh, c.xl), c.u
    m = c.plan["in_n"]
    widths = [HALF, HALF, 1200 - 2 * HALF]
    st = [norm_turn(c, c.h, c.gain[:, :], *x),
          ProjectTurned(c, "in_t", 15, Loads(*[spread(dram[n + "_rows"], dram[n + "_wide"]) for n in ("rel", "t5", "band")])),
          Project(c, x, [(m, n * KT, range(KT), w, [u[:, b, n * HALF:n * HALF + w] for b in range(NB)])
                         for n, w in enumerate(widths)],
                  Loads((c.bias[:, 0:10, :], toeplitz(dram["rel_wide"], 10)),
                        (c.gain[:, :], dram_row(dram, "attn_post")), (c.gain2[:, :], dram_row(dram, "ffn_pre"))))]
    segments, groups = [], []
    for b in range(NB):
        q, kv = u[:, b, 784:1040], u[:, b, 1040:1168]
        segments += [(q.unsqueeze(1), None, None, 1.0), (kv.unsqueeze(1), None, None, 1.0)]
        for tile, rows, g in ((0, q[:, 0:P], "mla_q"), (1, q[:, P:2 * P], "mla_q"), (2, kv, "mla_kv")):
            col = PARAM(c.param, g)[:, tile % 2:tile % 2 + 1]
            cut = (slice(None), slice(tile, tile + 1), block_cut(b))
            groups.append((2 * b + (2 if tile == 2 else 1), [rows], P, "pair", (c.latent_h[cut], c.latent_l[cut]), col))
    m = c.plan["mla"]
    st += [Turn(c, segments, groups),
           Project(c, (c.latent_h, c.latent_l),
                   [(m, 0, (0, 1), 384, [u[:, b, 1200:1584] for b in range(NB)]),
                    (m, 2, (2,), HALF, [u[:, b, 1584:2096] for b in range(NB)])]),
           Rope(c, lambda b: u[:, b, 1200:1584], lambda b: u[:, b, 1584:2096], lambda b: u[:, b, 1168:1200],
                lambda b: u[:, b, 2096:2480])]
    groups = []
    for b in range(NB):
        for n, at in enumerate((1200, 2096)):
            groups.append((0, [u[:, b, at + 96 * h:at + 96 * (h + 1)] for h in range(4)], 96, "f32",
                           c.t[0:96, 15 + 4 * n:19 + 4 * n, block_cut(b)], None))
    compress = Compress(c)
    units, base = first_units(c, compress)
    st += [Turn(c, [], groups), compress, Attention(c, units), Dilated(c, c.products, base),
           out_turn(c, 7), Merge(c), norm_turn(c, c.xn, None, *x, norm=False),
           Residual(c, "w_o", x, KT, gain=c.gain[:, :])]
    return st


def even_mixer(c, dram):
    x, u, t = (c.xh, c.xl), c.u, c.t
    m, tail = c.plan["even"], c.plan["even_tail"]
    jobs = [(m, n * KT, range(KT), HALF, [u[:, b, n * HALF:(n + 1) * HALF] for b in range(NB)]) for n in range(7)]
    jobs.append((tail, 0, range(KT), 136, [u[:, b, 3584:3720] for b in range(NB)]))
    st = [Project(c, x, jobs)]
    segments, groups = [], []
    for b in range(NB):
        by_head = lambda a, n: u[:, b, a:a + n].rearrange("p (h d) -> p h d", d=DH)
        segments += [(by_head(0, D), None, None, 1.0), (by_head(3584, P), None, None, 1.0),
                     (by_head(1536, D), None, None, 1.0)]
        for at, tiles, t0, gain, need in ((0, 4, 0, "a_q", 1), (512, 4, 4, "a_k", 1), (1024, 4, 8, None, 1),
                                          (3584, 1, 12, "idx_k", 2), (1536, 4, 13, "b_q", 3), (2048, 4, 17, "b_k", 3)):
            col = PARAM(c.param, gain) if gain else None
            groups += turn_groups(u[:, b, at:at + tiles * P], tiles, t, col, 3 * b + need, t0, block_cut(b))
    st += [Turn(c, segments, groups), Lambda(c),
           Select(c, lambda h: half(t[:, 8:12, :], h), lambda h: t[(h % 2) * DH:(h % 2 + 1) * DH, 12, :],
                  lambda b: u[:, b, 3712:3720])]
    units = []
    for b in range(NB):
        nk, parts = (b + 1) * P, [P] * (b + 1)
        keys, qs = slice(0, nk), block_cut(b)
        for pair in ((0, 2), (1, 3), (4, 6), (5, 7)):
            at, heads = 2 * len(units), slice(pair[0], pair[1] + 1, 2)
            dst = c.o[:, b, 0:HALF].rearrange("p (h d) -> p h d", d=DH)[:, heads, :]
            v = [[u[:, k, 2560 + h * DH:2560 + (h + 1) * DH] for k in range(b + 1)] for h in pair]
            units.append(Unit([half(t, h, qs) for h in pair], [half(t[:, 4:8, :], h, keys) for h in pair], v, parts,
                              DH ** -0.5, DH, scaled(c, dst), slice(at, at + 2), c.bias[:, heads, S - nk:S],
                              extra=c.taken[:, b, 0:nk].unsqueeze(1).to_broadcast([P, 2, nk])))
        for pair in ((0, 1), (2, 3)):
            for part in range(2):
                at, heads = 2 * len(units), slice(pair[0], pair[0] + 2)
                rows = slice(part * DH, (part + 1) * DH)
                dst = c.o[:, b, HALF:D].rearrange("p (h d) -> p h d", d=P)[:, heads, :]
                v = [[u[:, k, 3072 + h * P:3072 + (h + 1) * P] for k in range(b + 1)] for h in pair]
                fin = scaled(c, dst, c.small[:, 140:142], add=True) if part else scaled(c, dst)
                units.append(Unit([t[rows, 13 + h, qs] for h in pair], [t[rows, 17 + h, keys] for h in pair], v, parts,
                                  DH ** -0.5, P, fin, slice(at, at + 2), c.bias[:, slice(8 + pair[0], 10 + pair[0]), S - nk:S]))
    st.append(Attention(c, units))
    norms = [(c.o[:, b, HALF:D].rearrange("p (h d) -> p h d", d=P), None, None, 1.0 - LAMBDA_INIT) for b in range(NB)]
    st.append(out_turn(c, 8, PARAM(c.param, "subln"), norms))
    return st


def odd_mixer(c, dram):
    x, u, t, m = (c.xh, c.xl), c.u, c.t, c.plan["odd"]
    st = [Project(c, x, [(m, n * KT, range(KT), HALF, [u[:, b, n * HALF:(n + 1) * HALF] for b in range(NB)])
                         for n in range(6)])]
    segments, groups = [], []
    for b in range(NB):
        for n, gain in enumerate(("c_q", "c_k")):
            rows = u[:, b, n * D:(n + 1) * D]
            segments.append((rows.rearrange("p (h d) -> p h d", d=DH), None, None, 1.0))
            groups += turn_groups(rows, 8, t, PARAM(c.param, gain), 2 * b + n + 1, 8 * n, block_cut(b))
    st += [Turn(c, segments, groups), MaskBand(c)]
    units = []
    for b in range(NB):
        nk, parts = (b + 1) * P, [P] * (b + 1)
        keys, qs = slice(0, nk), block_cut(b)
        for q in range(4):
            for r in range(2):
                pair = (4 * q + r, 4 * q + r + 2)
                at, heads = 2 * len(units), slice(pair[0], pair[1] + 1, 2)
                dst = c.o[:, b, :].rearrange("p (h d) -> p h d", d=DH)[:, heads, :]
                v = [[u[:, k, 2 * D + h * DH:2 * D + (h + 1) * DH] for k in range(b + 1)] for h in pair]
                units.append(Unit([half(t, h, qs) for h in pair], [half(t[:, 8:16, :], h, keys) for h in pair], v,
                                  parts, DH ** -0.5, DH, scaled(c, dst), slice(at, at + 2), c.bias[:, heads, S - nk:S]))
    st += [Attention(c, units), out_turn(c, 8)]
    return st


def stages_of(c, dram, out):
    x = (c.xh, c.xl)
    row = lambda n: dram_row(dram, n)
    g1, g2 = c.gain[:, :], c.gain2[:, :]
    st = [Setup(c, dram)]
    st += first_mixer(c, dram)
    st += [norm_turn(c, c.h, g2, *x, loads=Loads((g1, row("ffn_post")))),
           Ffn(c, "up", "down", gain=g1, conv=True,
               loads=Loads((g2, row("l0_ffn1")), (c.bias[:, 0:12, :], toeplitz(dram["t5_wide"], 12))))]
    for layer in range(2):
        l = f"l{layer}"
        st += [norm_turn(c, c.h, g2, *x, loads=Loads((g1, row(l + "_mix")))),
               Ffn(c, f"up1_{layer}", f"down1_{layer}", factor=0.5),
               norm_turn(c, c.h, g1, *x)]
        st += even_mixer(c, dram) if layer == 0 else odd_mixer(c, dram)
        mem = dram["mem"].rearrange("(b p) d -> p b d", p=P)
        st += [Residual(c, "even_out" if layer == 0 else "odd_out", (c.oh, c.ol), KT,
                        loads=Loads((g1, row(l + "_src")), (c.u[:, :, 2048:3072], mem)))]
        st += memory_stages(c, layer, dram, l + "_ffn2")
        after = [(g2, row("l1_ffn1")), (c.bias[:, 0:16, :], toeplitz(dram["band_wide"], 16))] if layer == 0 else []
        st += [norm_turn(c, c.h, g1, *x, loads=Loads(*after)),
               Ffn(c, f"up2_{layer}", f"down2_{layer}", factor=0.5)]
    st.append(Store(c, out.rearrange("a (b p) d -> p (a b) d", p=P)))
    return st


STOP = None


def program(nc, dram, out):
    core = Core(nc, dram["stream"])
    stages = stages_of(core, dram, out)
    if STOP is not None:
        stages = stages[:STOP] + stages[-1:]
    numbers = [sorted(x.num for x in s.values()) for s in core.sets]

    def meet(engine, n):
        engine.drain().then_inc(core.stage_done, 1)
        engine.wait_ge(core.stage_done, 4 * (n + 1))
        engine.nop(nofuse=True)

    with nc.Block() as block:

        @block.tensor
        def _(pe):
            for n, stage in enumerate(stages):
                stage.tensor(pe, core.sets[n % 2])
                meet(pe, n)

        @block.scalar
        def _(act):
            for n, stage in enumerate(stages):
                stage.scalar(act, core.sets[n % 2])
                meet(act, n)

        @block.vector
        def _(dve):
            for n, stage in enumerate(stages):
                stage.vector(dve, core.sets[n % 2])
                meet(dve, n)

        @block.gpsimd
        def _(pool):
            for n, stage in enumerate(stages):
                if n:
                    other = numbers[(n + 1) % 2]
                    pool.sem_clear(range(other[0], other[-1] + 1))
                stage.gpsimd(pool, core.sets[n % 2])
                meet(pool, n)

        @block.sync
        def _(sp):
            for n in range(core.act_next):
                if n >= RING:
                    sp.wait_ge(core.slot_used, n - RING + 1)
                sp.dma_start(core.raw[:, n % RING, :], core.stream[n]).then_inc(core.slot_loaded[n % RING], 16)


def kernel(**inputs):
    from concourse import bacc
    from concourse.bass_utils import run_bass_kernel_spmd as run

    x = {k: np.ascontiguousarray(v) for k, v in inputs.items()}
    nc = bacc.Bacc("TRN2", target_bir_lowering=False, num_devices=1)
    arrays = {
        "stream": pack_stream(x), "param": pack_params(x), "rows": pack_rows(x), "band_rows": pack_band_bias(x),
        "const": constants(), "table": tables(), "x": x["x"][0], "mem": x["mem_2"][0],
    }
    arrays = {k: np.ascontiguousarray(v) for k, v in arrays.items()}
    dram = {k: nc.dram_tensor(k + "_dram", v.shape, F32, kind="ExternalInput").ap() for k, v in arrays.items()}
    for name, heads in (("rel_rows", 10), ("t5_rows", 12)):
        dram[name] = nc.dram_tensor(name + "_dram", (heads, TOE), F32, kind="Internal").ap()
    for name, heads in (("rel_wide", 10), ("t5_wide", 12), ("band_wide", 16)):
        dram[name] = nc.dram_tensor(name + "_dram", (heads, P, TOE), F32, kind="Internal").ap()
    out = nc.dram_tensor("out_dram", (1, S, D), F32, kind="ExternalOutput").ap()
    program(nc, dram, out)
    r = run(nc, [{k + "_dram": v for k, v in arrays.items()}], core_ids=[0])
    return r.results[0]["out_dram"]
```

```python
import math

import numpy as np

import concourse.bass as bass
from concourse import mybir

F32 = mybir.dt.float32
F32R = mybir.dt.float32r
ACT = mybir.ActivationFunctionType
ALU = mybir.AluOpType
AX = mybir.AxisListType

P = 128
S = 256
NB = S // P
D = 1024
KT = D // P
DH = 64
FF = 2816
FT = FF // P
EPS = 1e-6
NEG = -1e30
TAKEN = -3e38
HALF = 512

SLOT = 2048
RING = 4
LEAD = 2
TOE = 384
TOP_K = S // 4



def rel_bucket(dist):
    dist = np.maximum(dist, 0)
    d = np.maximum(dist, 1).astype(np.float32)
    large = 16 + (np.log(d / np.float32(16)) / np.float32(math.log(128)) * np.float32(16)).astype(np.int32)
    return np.where(dist < 16, dist, np.minimum(large, 31))


def t5_bucket(rel):
    off = (rel < 0).astype(np.int32) * 16
    n = np.abs(rel)
    nf = np.maximum(n, 1).astype(np.float32)
    large = 8 + (np.log(nf / np.float32(8)) / np.float32(math.log(16)) * np.float32(8)).astype(np.int32)
    return off + np.where(n < 8, n, np.minimum(large, 15))


class Columns:

    def __init__(self, **widths):
        self.at, self.n = {}, 0
        for name, w in widths.items():
            self.at[name] = (self.n, w)
            self.n += w

    def __call__(self, tile, name):
        a, w = self.at[name]
        return tile[:, a:a + w]


CONST = Columns(ident=P, upto=P, ones=P, causal=S, cmp_mask=30, cmp_valid=2, cos=2 * 16, sin=2 * 16)
TABLE = Columns(hot_rel=TOE, hot_t5=TOE, rel_mask=TOE)
PARAM = Columns(mla_q=2, mla_kv=1, a_q=1, a_k=1, idx_k=1, b_q=1, b_k=1, subln=1, c_q=1, c_k=1,
                mq0=1, mk0=1, mq1=1, mk1=1, conv_w=3 * 2 * FT, conv_b=2 * FT, cmp_pos=32,
                gains=14 * KT, w2k=P, w2v=DH, lam=4 * DH, f_bias=4, rel=10, t5=12)
ROWS = ["attn_pre", "ffn_pre", "attn_post", "ffn_post", "l0_ffn1", "l0_mix", "l0_src", "l0_mem", "l0_ffn2",
        "l1_ffn1", "l1_mix", "l1_src", "l1_mem", "l1_ffn2"]


def constants():
    c = np.zeros((P, CONST.n), np.float32)
    p = np.arange(P)
    CONST(c, "ident")[:] = np.eye(P)
    CONST(c, "upto")[:] = p[:, None] <= p[None, :]
    CONST(c, "ones")[:] = 1
    k = np.arange(S)
    CONST(c, "causal")[:] = np.where(P + p[:, None] - k[None, :] >= 0, 0, NEG)
    end = np.arange(15) * 16 + 31
    for b in range(NB):
        t = b * P + p
        CONST(c, "cmp_mask")[:, 15 * b:15 * b + 15] = np.where(end[None, :] <= t[:, None], 0, NEG)
        CONST(c, "cmp_valid")[:, b] = t >= end[0]
        freq = (np.float32(10000.0) ** (-np.arange(0, 32, 2, dtype=np.float32) / np.float32(32))).astype(np.float32)
        angle = t.astype(np.float32)[:, None] * freq[None, :]
        CONST(c, "cos")[:, 16 * b:16 * b + 16] = np.cos(angle)
        CONST(c, "sin")[:, 16 * b:16 * b + 16] = np.sin(angle)
    return c


def tables():
    t = np.zeros((P, TABLE.n), np.float32)
    j = np.arange(TOE)
    dist = 255 - j
    for name, bucket in (("hot_rel", rel_bucket(dist)), ("hot_t5", t5_bucket(dist))):
        TABLE(t, name)[bucket, j] = 1
    for h in range(10):
        ok = dist >= 0
        if h >= 4:
            window, dilation = ((128, 1), (512, 4), (2048, 16))[(h - 4) // 2]
            ok = ok & (dist <= window) & (dist % dilation == 0)
        TABLE(t, "rel_mask")[h] = np.where(ok, 0, NEG)
    return t



class Matrix:

    def __init__(self, first, count, width):
        self.first, self.count, self.width = first, count, width
        self.per = SLOT // width
        self.slots = -(-count // self.per)

    def slot(self, i):
        return self.first + i // self.per

    def offset(self, i):
        return i % self.per * self.width

    def ends_slot(self, i):
        return i == self.count - 1 or i % self.per == self.per - 1


def by_chunk(w, width, chunks=None):
    k = w.shape[0] // P
    return [w[t * P:(t + 1) * P, c * width:(c + 1) * width]
            for c in range(chunks or -(-w.shape[1] // width)) for t in range(k)]


def by_tile(w, width):
    return [w[t * P:(t + 1) * P, c * width:(c + 1) * width]
            for t in range(w.shape[0] // P) for c in range(w.shape[1] // width)]


def first_in_columns():
    h64 = lambda base, i: list(range(base + 64 * i, base + 64 * i + 64))
    a_q, kv, b, c = 0, 256, 652, 1804
    tiles = []
    for t in range(2):
        tiles += h64(a_q, 2 * t) + h64(a_q, 2 * t + 1)
    tiles += h64(kv, 2) * 2 + h64(kv, 4) * 2 + h64(kv, 0) + h64(kv, 1)
    for base in (b, b + 384):
        for t in range(3):
            tiles += h64(base, 2 * t) + h64(base, 2 * t + 1)
    for base in (c, c + 256):
        for t in range(2):
            tiles += h64(base, 2 * t) + h64(base, 2 * t + 1)
    rows = (h64(kv, 3) + h64(kv, 5) + list(range(640, 652)) + list(range(b + 768, b + 1152))
            + list(range(c + 512, c + 768)) + list(range(2572, 2576)) + list(range(2576, 2992)))
    return tiles, rows


def even_in_columns():
    r = lambda a, n: list(range(a, a + n))
    main = r(0, 512) + r(512, 512) + r(1536, 512) + r(2120, 512) + r(2632, 512) + r(1024, 512) + r(3144, 512)
    return main, r(2048, 64) * 2 + r(2112, 8)


def stream_plan():
    plan = [("in_t", 15 * KT, P), ("in_n", 3 * KT, HALF), ("mla", 3, HALF), ("phi", 32, P)]
    for i in range(4):
        plan += [(f"branch{i}", 2 if i == 1 else 4, HALF), (f"gate{i}", 2 * KT, HALF)]
    plan += [("w_o", 2 * KT, HALF), ("up", FT * 2 * KT, P), ("down", 2 * FT, HALF)]
    for layer in range(2):
        plan += [(f"up1_{layer}", FT * 2 * KT, P), (f"down1_{layer}", 2 * FT, HALF)]
        if layer == 0:
            plan += [("even", 7 * KT, HALF), ("even_tail", KT, S), ("even_out", 2 * KT, HALF)]
        else:
            plan += [("odd", 6 * KT, HALF), ("odd_out", 2 * KT, HALF)]
        plan += [(f"wkv{layer}", 2 * KT, HALF), (f"wq{layer}", KT, HALF), (f"wo{layer}", 8, HALF)]
        plan += [(f"up2_{layer}", FT * 2 * KT, P), (f"down2_{layer}", 2 * FT, HALF)]
    out, first = {}, 0
    for name, count, width in plan:
        out[name] = Matrix(first, count, width)
        first += out[name].slots
    return out, first


def pack_stream(x):
    plan, slots = stream_plan()
    out = np.zeros((slots, P, SLOT), np.float32)

    def pairs(g, u):
        g, u = by_chunk(g, P), by_chunk(u, P)
        return [piece for f in range(FT) for piece in g[f * KT:(f + 1) * KT] + u[f * KT:(f + 1) * KT]]

    w_in = x["w_in"][0]
    tiles, rows = first_in_columns()
    pieces = {"in_t": by_chunk(w_in[:, tiles], P), "in_n": by_chunk(w_in[:, rows], HALF)}
    w1 = [x[n][0].reshape(32, DH, P) for n in ("nsa_phi_k_w1", "nsa_phi_v_w1")]
    pieces["phi"] = [np.concatenate([w[i] for w in w1], 0) for i in range(32)]
    pieces["mla"] = by_chunk(x["mla_w_uq"][0], HALF) + by_chunk(x["mla_w_ukv"][0], HALF)
    for i, n in enumerate("abcd"):
        pieces[f"branch{i}"] = by_chunk(x["w_branch_" + n][0], HALF)
        pieces[f"gate{i}"] = by_chunk(x["w_merge_gate"][0, i], HALF)
    pieces["w_o"] = by_tile(x["w_o"][0], HALF)
    up = x["ffn_w_up"][0]
    pieces["up"] = pairs(up[:, :FF], up[:, FF:])
    pieces["down"] = by_tile(x["ffn_w_down"][0], HALF)
    for layer in range(2):
        g = lambda n: x[f"l{layer}_{n}_2"]
        for n in (1, 2):
            pieces[f"up{n}_{layer}"] = pairs(g(f"ffn{n}_wg"), g(f"ffn{n}_wu"))
            pieces[f"down{n}_{layer}"] = by_tile(g(f"ffn{n}_wd"), HALF)
        pieces[f"wkv{layer}"] = by_chunk(g("mem_wkv"), HALF)
        pieces[f"wq{layer}"] = by_chunk(g("mem_wq"), HALF)
        pieces[f"wo{layer}"] = by_tile(g("mem_wo"), HALF)
        if layer == 0:
            main, tail = even_in_columns()
            pieces["even"] = by_chunk(g("w_in")[:, main], HALF)
            pieces["even_tail"] = by_chunk(g("w_in")[:, tail], S)
            pieces["even_out"] = by_tile(g("w_out"), HALF)
        else:
            pieces["odd"] = by_chunk(g("w_in"), HALF)
            pieces["odd_out"] = by_tile(g("w_out"), HALF)
    for name, m in plan.items():
        assert len(pieces[name]) == m.count, name
        for i, piece in enumerate(pieces[name]):
            at = m.offset(i)
            out[m.slot(i), :, at:at + piece.shape[1]] = piece
    return out


def pack_params(x):
    a = np.zeros((P, PARAM.n), np.float32)
    put = lambda n, v: PARAM(a, n).__setitem__(slice(None), v)
    twice = lambda v: np.concatenate([v, v])[:, None]
    put("mla_q", x["mla_q_norm"][0].reshape(2, P).T)
    put("mla_kv", x["mla_kv_norm"][0][:, None])
    for n, k in (("a_q", "l0_a_q_norm_2"), ("a_k", "l0_a_k_norm_2"), ("idx_k", "l0_idx_k_norm_2"),
                 ("b_q", "l0_b_q_norm_2"), ("b_k", "l0_b_k_norm_2"), ("c_q", "l1_c_q_norm_2"), ("c_k", "l1_c_k_norm_2")):
        put(n, twice(x[k]))
    put("subln", x["l0_b_subln_2"][:, None])
    for layer in range(2):
        put(f"mq{layer}", x[f"l{layer}_mem_q_norm_2"][:, None])
        put(f"mk{layer}", x[f"l{layer}_mem_k_norm_2"][:, None])
    put("conv_w", x["ffn_conv_w"][0].reshape(3 * 2 * FT, P).T)
    put("conv_b", x["ffn_conv_b"][0].reshape(2 * FT, P).T)
    put("gains", pack_rows(x).reshape(len(ROWS) * KT, P).T)
    pos = x["nsa_cmp_pos"][0].T
    put("cmp_pos", np.concatenate([pos, pos], 0))
    put("w2k", np.concatenate([x["nsa_phi_k_w2"][0]] * 2, 1))
    put("w2v", x["nsa_phi_v_w2"][0])
    put("lam", np.concatenate([x[f"l0_b_{n}_2"] for n in ("lq1", "lk1", "lq2", "lk2")])[None, :])
    put("f_bias", x["fox_forget_bias"][0][None, :])
    PARAM(a, "rel")[:32] = x["rel_bias_table"]
    PARAM(a, "t5")[:32] = x["t5_bias_2"]
    return a


def pack_rows(x):
    first = [x[n][0] for n in ("norm_attn_pre", "norm_ffn_pre", "norm_attn_post", "norm_ffn_post")]
    rest = [x[f"l{layer}_{n}_2"] for layer in range(2)
            for n in ("ffn1_norm", "mix_norm", "mem_src_norm", "mem_norm", "ffn2_norm")]
    return np.stack(first + rest)


def pack_band_bias(x):
    table = x["l1_c_rel_bias_2"]
    return np.ascontiguousarray(table[511 - np.arange(TOE)].T)



NAMES = ["squares_ready", "sums_ready", "means_ready", "roots_ready", "rows_scaled", "tiles_turned",
         "turned_by_act", "turned_by_dve", "highs_ready", "banks_filled", "drained_by_act", "drained_by_dve",
         "gates_ready", "hidden_ready", "convolved", "scores_ready", "logits_ready", "probs_ready",
         "probs_turned", "probs_copied", "out_ready", "out_taken", "inputs_ready", "partial_ready",
         "act_step", "dve_step", "sum_step", "rows_turned", "high_turned", "low_turned", "norm_squares",
         "norm_means", "norm_roots", "inverse_ready", "wide_ready", "wide_turned", "row_ready", "scaled_ready"]


class Steps:

    def __init__(self, engine, sem):
        self.engine, self.sem, self.n = engine, sem, 0

    def __call__(self, instruction):
        self.n += 1
        instruction.then_inc(self.sem, 1)
        self.engine.wait_ge(self.sem, self.n)


class Core:

    def __init__(self, nc, stream):
        self.nc = nc
        self.plan, self.slots = stream_plan()
        self.stream = stream
        phi = self.plan["phi"]
        self.unsplit = range(phi.first, phi.first + phi.slots)
        self.top = -(-nc.sbuf_base // 64) * 64
        self.limit = nc.sbuf_usable_end
        t = self.tile
        raw_at = self.top
        self.raw = t("raw", [P, RING, SLOT])
        self.low = self.over("low", [P, RING, SLOT], F32R, raw_at)
        self.high = t("high", [P, RING, SLOT], F32R)
        self.h = t("h", [P, NB, D])
        self.xh = t("xh", [P, KT, S], F32R)
        self.xl = t("xl", [P, KT, S], F32R)
        arena = self.top
        self.u = t("u", [P, NB, 3720])
        self.o = t("o", [P, NB, D])
        self.small_rows = self.over("small_rows", [P, 2, TOE], F32, self.top - NB * D * 4)
        self.top = max(self.top, arena + 2 * FT * S * 4)
        self.hh = self.over("hh", [P, FT, S], F32R, arena)
        self.hl = self.over("hl", [P, FT, S], F32R, arena + FT * S * 4)
        turned = self.top
        self.t = t("t", [P, 23, S])
        self.oh = self.over("oh", [P, KT, S], F32R, turned)
        self.ol = self.over("ol", [P, KT, S], F32R, turned + KT * S * 4)
        xn = self.xn_at = self.top
        self.xn = t("xn", [P, NB, D])
        self.latent_h = self.over("latent_h", [P, 3, S], F32R, xn)
        self.latent_l = self.over("latent_l", [P, 3, S], F32R, xn + 3 * S * 4)
        self.forget = self.over("forget", [P, NB, 4, S], F32, xn)
        self.taken = self.over("taken", [P, NB, S], F32, xn)
        work = self.top
        self.prob = t("prob", [P, 4, 2, S])
        self.prob_t = t("prob_t", [P, 2, 4, P])
        self.square = self.over("square", [P, 3, D], F32, work)
        self.bias = t("bias", [P, 16, S])
        self.gain = t("gain", [P, 2, D])
        self.inv = t("inv", [P, 8])
        self.inv_wide = self.xn[:, 0, 0:S].rearrange("p (b q) -> p b q", b=NB)
        self.inv_row = t("inv_row", [P, S])
        self.const = t("const", [P, CONST.n])
        self.param = t("param", [P, PARAM.n])
        self.stat = t("stat", [P, 80])
        self.nmax = t("nmax", [P, 64])
        self.den = t("den", [P, 64])
        self.rden = t("rden", [P, 64])
        self.small = t("small", [P, 148])
        self.ident = CONST(self.const, "ident")
        self.products = self.u[:, 1, 2600:3368].rearrange("p (b g h d) -> p b g h d", b=NB, g=3, h=2)
        self.bank = [nc.alloc_psum_tensor(f"bank{i}", [P, HALF], F32) for i in range(8)]
        sem = nc.alloc_semaphore
        self.slot_loaded = [sem(f"slot_loaded{i}") for i in range(RING)]
        self.high_split, self.low_split, self.slot_used = sem("high_split"), sem("low_split"), sem("slot_used")
        self.stage_done, self.loaded, self.stored = sem("stage_done"), sem("loaded"), sem("stored")
        self.bounced = sem("bounced")
        self.sets = [{n: sem(f"{n}_{'even' if i == 0 else 'odd'}") for n in NAMES} for i in range(2)]
        self.act_next = self.dve_next = 0
        self.loads_of_setup = 4
        self.loads = 0

    def tile(self, name, shape, dtype=F32):
        size = int(np.prod(shape[1:])) * 4
        out = self.nc.alloc_sbuf_tensor_at(name, shape, dtype, offset=self.top)
        self.top += -(-size // 64) * 64
        assert self.top <= self.limit, (name, self.top, self.limit)
        return out

    def over(self, name, shape, dtype, at):
        return self.nc.alloc_sbuf_tensor_at(name, shape, dtype, offset=at)

    def split_high(self, act, last):
        for n in range(self.act_next, min(last + LEAD, self.slots - 1) + 1):
            act.wait_ge(self.slot_loaded[n % RING], 16 * (n // RING + 1))
            act.activation(self.high[:, n % RING, :], self.raw[:, n % RING, :], ACT.Copy).then_inc(self.high_split, 1)
            self.act_next = n + 1

    def split_low(self, dve, last):
        for n in range(self.dve_next, min(last + LEAD, self.slots - 1) + 1):
            dve.wait_ge(self.high_split, n + 1)
            if n in self.unsplit:
                dve.drain().then_inc(self.low_split, 1)
                self.dve_next = n + 1
                continue
            dve.tensor_tensor(self.low[:, n % RING, :], self.raw[:, n % RING, :],
                              self.high[:, n % RING, :].bitcast(F32), ALU.subtract).then_inc(self.low_split, 1)
            self.dve_next = n + 1

    def piece(self, pe, m, i, width=None):
        if i % m.per == 0:
            pe.wait_ge(self.low_split, m.slot(i) + 1)
        at, r = m.offset(i), m.slot(i) % RING
        cut = slice(at, at + (width or m.width))
        return self.high[:, r, cut], self.low[:, r, cut]

    def release(self, instruction, m, i):
        if m.ends_slot(i):
            instruction.then_inc(self.slot_used, 1)

    def finish_output(self, instruction, m, i, s):
        instruction.then_inc(self.slot_used if m.ends_slot(i) else s["banks_filled"], 1)

    def wait_output(self, engine, m, i, s, others):
        if m.ends_slot(i):
            engine.wait_ge(self.slot_used, m.slot(i) + 1)
        else:
            engine.wait_ge(s["banks_filled"], others)


def mm3(pe, out, left, right, start, stop):
    (lh, ll), (rh, rl) = left, right
    pe.matmul(out, lh, rh, start=start, stop=False)
    pe.matmul(out, lh, rl, start=False, stop=False)
    return pe.matmul(out, ll, rh, start=False, stop=stop)


def mm(pe, out, left, right, start, stop):
    return pe.matmul(out, left, right, start=start, stop=stop)


class Stage:
    def __init__(self, core):
        self.core = core

    def tensor(self, pe, s):
        pass

    def scalar(self, act, s):
        pass

    def vector(self, dve, s):
        pass

    def gpsimd(self, pool, s):
        pass


class Setup(Stage):

    def __init__(self, core, dram):
        super().__init__(core)
        self.dram = dram
        self.table = core.u[:, 0, 0:TABLE.n]

    def gpsimd(self, pool, s):
        c = self.core
        pool.dma_start(c.const[:, :], self.dram["const"]).then_inc(c.loaded, 16)
        pool.dma_start(c.param[:, :], self.dram["param"]).then_inc(c.loaded, 16)
        pool.dma_start(self.table, self.dram["table"]).then_inc(c.loaded, 16)
        pool.dma_start(c.h[:, :, :], self.dram["x"].rearrange("(b p) d -> p b d", p=P)).then_inc(c.loaded, 16)
        c.loads += 4
        pool.wait_ge(c.loaded, 16 * c.loads)
        pool.wait_ge(s["out_taken"], 2)
        pool.dma_start(self.dram["rel_rows"], c.small_rows[0:10, 0, :]).then_inc(c.bounced, 16)
        pool.dma_start(self.dram["t5_rows"], c.small_rows[0:12, 1, :]).then_inc(c.bounced, 16)
        pool.wait_ge(c.bounced, 32)

    def tensor(self, pe, s):
        c = self.core
        pe.wait_ge(c.loaded, 16 * c.loads_of_setup)
        mm(pe, c.bank[0][0:10, 0:TOE], PARAM(c.param, "rel")[0:32], TABLE(self.table, "hot_rel")[0:32],
           True, True).then_inc(s["out_ready"], 1)
        mm(pe, c.bank[1][0:12, 0:TOE], PARAM(c.param, "t5")[0:32], TABLE(self.table, "hot_t5")[0:32],
           True, True).then_inc(s["out_ready"], 1)

    def scalar(self, act, s):
        c = self.core
        act.wait_ge(c.loaded, 16 * c.loads_of_setup)
        c.split_high(act, 0)

    def vector(self, dve, s):
        c = self.core
        dve.wait_ge(c.loaded, 16 * c.loads_of_setup)
        dve.wait_ge(s["out_ready"], 2)
        dve.tensor_tensor(c.small_rows[0:10, 0, :], c.bank[0][0:10, 0:TOE], TABLE(self.table, "rel_mask")[0:10],
                          ALU.add).then_inc(s["out_taken"], 1)
        dve.tensor_copy(c.small_rows[0:12, 1, :], c.bank[1][0:12, 0:TOE]).then_inc(s["out_taken"], 1)
        c.split_low(dve, 0)


class Loads:

    def __init__(self, *pairs):
        self.pairs = pairs

    def start(self, core, pool):
        for dst, src in self.pairs:
            pool.dma_start(dst, src).then_inc(core.loaded, 16)
            core.loads += 1

    def finish(self, core, pool):
        pool.wait_ge(core.loaded, 16 * core.loads)


def spread(rows, wide):
    heads = rows.shape[0]
    return wide[0:heads], bass.AP(tensor=rows.tensor, offset=rows.offset, ap=[[TOE, heads], [0, P], [1, TOE]])


def toeplitz(wide, heads):
    return bass.AP(tensor=wide.tensor, offset=wide.offset + P - 1, ap=[[TOE - 1, P], [P * TOE, heads], [1, S]])


class Turn(Stage):

    def __init__(self, core, segments, groups, loads=None):
        super().__init__(core)
        self.segments, self.groups, self.loads = segments, groups, loads
        cols, self.at = 0, []
        for src, *_ in segments:
            self.at.append(cols)
            cols += src.shape[1]
        self.cols = cols
        assert cols <= 80
        self.by = [("act", "dve") if g[3] == "pair" else (("act",) if i % 2 == 0 else ("dve",))
                   for i, g in enumerate(groups)]

    def drained(self, engine, g):
        return sum(engine in b for b in self.by[:g + 1])

    def gpsimd(self, pool, s):
        if self.loads:
            self.loads.start(self.core, pool)
            self.loads.finish(self.core, pool)

    def tensor(self, pe, s):
        c = self.core
        for g, (need, sources, width, kind, dst, gain) in enumerate(self.groups):
            if need:
                pe.wait_ge(s["rows_scaled"], need)
            if g >= 4:
                if self.drained("act", g - 4):
                    pe.wait_ge(s["turned_by_act"], self.drained("act", g - 4))
                if self.drained("dve", g - 4):
                    pe.wait_ge(s["turned_by_dve"], self.drained("dve", g - 4))
            for j, src in enumerate(sources):
                last = pe.transpose(c.bank[g % 4][0:width, j * P:(j + 1) * P], src, self.core.ident)
            last.then_inc(s["tiles_turned"], 1)

    def scalar(self, act, s):
        c = self.core
        for i, (src, dst, gain, factor) in enumerate(self.segments):
            if i >= 3:
                act.wait_ge(s["sums_ready"], i - 2)
            h, w = src.shape[1], src.shape[2]
            sq = c.square[:, i % 3, 0:h * w].rearrange("p (h w) -> p h w", w=w)
            act.activation(sq, src, ACT.Square).then_inc(s["squares_ready"], 1)
        if self.segments:
            act.wait_ge(s["means_ready"], 1)
            act.activation(c.stat[:, 0:self.cols], c.stat[:, 0:self.cols], ACT.Sqrt).then_inc(s["roots_ready"], 1)
        for g, (need, sources, width, kind, dst, gain) in enumerate(self.groups):
            if "act" not in self.by[g]:
                continue
            act.wait_ge(s["tiles_turned"], g + 1)
            ps = c.bank[g % 4][0:width, 0:len(sources) * P].rearrange("p (n q) -> p n q", q=P)
            out = dst[0] if kind == "pair" else dst
            if gain is None:
                i = act.activation(out, ps, ACT.Copy)
            else:
                i = act.activation(out, ps, ACT.Copy, scale=gain)
            i.then_inc(s["turned_by_act"], 1)

    def vector(self, dve, s):
        c = self.core
        step = Steps(dve, s["dve_step"])
        for i, (src, dst, gain, factor) in enumerate(self.segments):
            h, w = src.shape[1], src.shape[2]
            dve.wait_ge(s["squares_ready"], i + 1)
            sq = c.square[:, i % 3, 0:h * w].rearrange("p (h w) -> p h w", w=w)
            dve.tensor_reduce(c.stat[:, self.at[i]:self.at[i] + h], sq, AX.X, ALU.add).then_inc(s["sums_ready"], 1)
        if self.segments:
            dve.wait_ge(s["sums_ready"], len(self.segments))
        for i, (src, dst, gain, factor) in enumerate(self.segments):
            h, w = src.shape[1], src.shape[2]
            f2 = factor * factor
            m = dve.tensor_scalar(c.stat[:, self.at[i]:self.at[i] + h], c.stat[:, self.at[i]:self.at[i] + h],
                                  1.0 / (w * f2), EPS / f2, ALU.mult, ALU.add)
            step(m)
        if self.segments:
            dve.sem_inc(s["means_ready"], 1)
            dve.wait_ge(s["roots_ready"], 1)
            step(dve.reciprocal(c.stat[:, 0:self.cols], c.stat[:, 0:self.cols]))
        for i, (src, dst, gain, factor) in enumerate(self.segments):
            h, w = src.shape[1], src.shape[2]
            dst = src if dst is None else dst
            r = c.stat[:, self.at[i]:self.at[i] + h]
            if gain is not None:
                m = dve.scalar_tensor_tensor(dst[:, 0, :], src[:, 0, :], r, gain, ALU.mult, ALU.mult)
            elif h == 1:
                m = dve.tensor_scalar(dst[:, 0, :], src[:, 0, :], r, None, ALU.mult)
            else:
                m = dve.tensor_tensor(dst, src, r.unsqueeze(2).to_broadcast([P, h, w]), ALU.mult)
            m.then_inc(s["rows_scaled"], 1)
        for g, (need, sources, width, kind, dst, gain) in enumerate(self.groups):
            if "dve" not in self.by[g]:
                continue
            ps = c.bank[g % 4][0:width, 0:len(sources) * P].rearrange("p (n q) -> p n q", q=P)
            dve.wait_ge(s["tiles_turned"], g + 1)
            if kind == "pair":
                dve.wait_ge(s["turned_by_act"], self.drained("act", g))
                hi = dst[0].bitcast(F32)
                if gain is None:
                    i = dve.tensor_tensor(dst[1], ps, hi, ALU.subtract)
                else:
                    i = dve.scalar_tensor_tensor(dst[1], ps, gain, hi, ALU.mult, ALU.subtract)
            elif gain is None:
                i = dve.tensor_copy(dst, ps)
            else:
                i = dve.tensor_scalar(dst, ps, gain, None, ALU.mult)
            i.then_inc(s["turned_by_dve"], 1)


class Source:

    def __init__(self, core, rows, dst, tiles=KT, gain=None, norm=False, base=4):
        self.core, self.rows, self.dst, self.tiles, self.norm, self.base = core, rows, dst, tiles, norm, base
        n = ROWS.index(gain) * KT if gain else None
        self.gain = PARAM(core.param, "gains")[:, n:n + KT] if gain else None

    def bank(self, k):
        return self.core.bank[self.base + k // 2][:, (k % 2) * S:(k % 2 + 1) * S]

    def tensor(self, pe, s):
        for k in range(self.tiles):
            for b in range(NB):
                last = pe.transpose(self.bank(k)[:, b * P:(b + 1) * P], self.rows[:, b, k * P:(k + 1) * P],
                                    self.core.ident)
            if k % 2 == 1:
                last.then_inc(s["rows_turned"], 1)

    def row(self, pe, s):
        if not self.norm:
            return
        c = self.core
        pe.wait_ge(s["low_turned"], self.tiles)
        pe.wait_ge(s["wide_ready"], 1)
        for b in range(NB):
            last = pe.transpose(c.bank[7][:, b * P:(b + 1) * P], c.inv_wide[:, b, :], c.ident)
        last.then_inc(s["wide_turned"], 1)

    def scalar(self, act, s):
        c = self.core
        for k in range(self.tiles):
            act.wait_ge(s["rows_turned"], k // 2 + 1)
            scale = 1.0 if self.gain is None else self.gain[:, k:k + 1]
            i = act.activation(self.dst[0][:, k, :], self.bank(k), ACT.Copy, scale=scale)
            if k % 2 == 1:
                i.then_inc(s["high_turned"], 1)
        if not self.norm:
            return
        for b in range(NB):
            act.activation(c.xn[:, b, :], self.rows[:, b, :], ACT.Square, accum_out=c.inv[:, b:b + 1])\
               .then_inc(s["norm_squares"], 1)
        act.wait_ge(s["norm_means"], 1)
        act.activation(c.inv[:, 0:2], c.inv[:, 0:2], ACT.Sqrt).then_inc(s["norm_roots"], 1)

    def vector(self, dve, s, factor=1.0, row=False):
        c = self.core
        for k in range(self.tiles):
            dve.wait_ge(s["high_turned"], k // 2 + 1)
            high, low = self.dst[0][:, k, :].bitcast(F32), self.dst[1][:, k, :]
            if self.gain is None:
                i = dve.tensor_tensor(low, self.bank(k), high, ALU.subtract)
            else:
                i = dve.scalar_tensor_tensor(low, self.bank(k), self.gain[:, k:k + 1], high, ALU.mult, ALU.subtract)
            i.then_inc(s["low_turned"], 1)
        if not self.norm:
            return
        dve.wait_ge(s["norm_squares"], NB)
        dve.tensor_scalar(c.inv[:, 0:2], c.inv[:, 0:2], 1.0 / D, EPS, ALU.mult, ALU.add).then_inc(s["norm_means"], 1)
        dve.wait_ge(s["norm_roots"], 1)
        dve.reciprocal(c.inv[:, 2:4], c.inv[:, 0:2]).then_inc(s["inverse_ready"], 1)
        dve.wait_ge(s["inverse_ready"], 1)
        dve.tensor_scalar(c.inv[:, 4:6], c.inv[:, 2:4], factor, None, ALU.mult).then_inc(s["scaled_ready"], 1)
        if row:
            dve.tensor_copy(c.inv_wide[:, :, :], c.inv[:, 2:4].unsqueeze(2).to_broadcast([P, NB, P]))\
               .then_inc(s["wide_ready"], 1)

    def take_row(self, dve, s):
        c = self.core
        dve.wait_ge(s["wide_turned"], 1)
        dve.tensor_copy(c.inv_row[:, :], c.bank[7][:, 0:S]).then_inc(s["row_ready"], 1)
        dve.wait_ge(s["row_ready"], 1)


class ProjectTurned(Stage):

    def __init__(self, core, name, tiles, source, loads=None):
        super().__init__(core)
        self.m, self.tiles, self.source, self.loads = core.plan[name], tiles, source, loads
        self.last = [(t + 1) * KT - 1 for t in range(tiles)]
        self.others = [sum(not self.m.ends_slot(i) for i in self.last[:t + 1]) for t in range(tiles)]

    def gpsimd(self, pool, s):
        if self.loads:
            self.loads.start(self.core, pool)
            self.loads.finish(self.core, pool)

    def tensor(self, pe, s):
        c = self.core
        self.source.tensor(pe, s)
        for t in range(self.tiles):
            if t == 2:
                self.source.row(pe, s)
            if t >= 4:
                pe.wait_ge(s["drained_by_dve"], t - 3)
            for k in range(KT):
                if t == 0:
                    pe.wait_ge(s["low_turned"], k + 1)
                i = t * KT + k
                last = mm3(pe, c.bank[t % 4][:, 0:S], c.piece(pe, self.m, i), (c.xh[:, k, :], c.xl[:, k, :]),
                           k == 0, k == KT - 1)
            c.finish_output(last, self.m, i, s)

    def scalar(self, act, s):
        self.source.scalar(act, s)
        self.core.split_high(act, self.m.slot(self.last[-1]))

    def vector(self, dve, s):
        c = self.core
        self.source.vector(dve, s, row=True)
        for t in range(self.tiles):
            c.split_low(dve, self.m.slot(self.last[t]))
            if t == 0:
                self.source.take_row(dve, s)
            c.wait_output(dve, self.m, self.last[t], s, self.others[t])
            dve.tensor_tensor(c.t[:, t, :], c.bank[t % 4][:, 0:S], c.inv_row[:, :], ALU.mult)\
               .then_inc(s["drained_by_dve"], 1)


class Project(Stage):

    def __init__(self, core, x, jobs, loads=None, source=None, scale=False):
        super().__init__(core)
        self.source, self.scale = source, scale
        self.x, self.jobs, self.loads = x, jobs, loads
        ends = [j[0].ends_slot(j[1] + len(j[2]) - 1) for j in jobs]
        self.others = [sum(not e for e in ends[:n + 1]) for n in range(len(jobs))]

    def gpsimd(self, pool, s):
        if self.loads:
            self.loads.start(self.core, pool)
            self.loads.finish(self.core, pool)

    def tensor(self, pe, s):
        c = self.core
        xh, xl = self.x
        if self.source:
            self.source.tensor(pe, s)
        for n, (m, i0, kts, width, dst) in enumerate(self.jobs):
            if n >= 2:
                pe.wait_ge(s["drained_by_act"], n - 1)
                pe.wait_ge(s["drained_by_dve"], n - 1)
            for j, k in enumerate(kts):
                if self.source and n == 0:
                    pe.wait_ge(s["low_turned"], k + 1)
                w = c.piece(pe, m, i0 + j, width)
                for b in range(NB):
                    cut = slice(b * P, (b + 1) * P)
                    last = mm3(pe, c.bank[2 * (n % 2) + b][:, 0:width], (xh[:, k, cut], xl[:, k, cut]), w,
                               j == 0, j == len(kts) - 1)
                if j == len(kts) - 1:
                    c.finish_output(last, m, i0 + j, s)
                else:
                    c.release(last, m, i0 + j)

    def scalar(self, act, s):
        c = self.core
        if self.source:
            self.source.scalar(act, s)
            act.wait_ge(s["inverse_ready"], 1)
        for n, (m, i0, kts, width, dst) in enumerate(self.jobs):
            c.split_high(act, m.slot(i0 + len(kts) - 1))
            c.wait_output(act, m, i0 + len(kts) - 1, s, self.others[n])
            act.activation(dst[0], c.bank[2 * (n % 2)][:, 0:width], ACT.Copy,
                           scale=c.inv[:, 2:3] if self.scale else 1.0).then_inc(s["drained_by_act"], 1)

    def vector(self, dve, s):
        c = self.core
        if self.source:
            self.source.vector(dve, s)
        for n, (m, i0, kts, width, dst) in enumerate(self.jobs):
            c.split_low(dve, m.slot(i0 + len(kts) - 1))
            c.wait_output(dve, m, i0 + len(kts) - 1, s, self.others[n])
            ps = c.bank[2 * (n % 2) + 1][:, 0:width]
            if self.scale:
                i = dve.tensor_scalar(dst[1], ps, c.inv[:, 3:4], None, ALU.mult)
            else:
                i = dve.tensor_copy(dst[1], ps)
            i.then_inc(s["drained_by_dve"], 1)


class Residual(Stage):

    def __init__(self, core, name, x, kts, factor=1.0, gain=None, loads=None, source=None):
        super().__init__(core)
        self.source = source
        self.m, self.x, self.kts, self.factor, self.gain, self.loads = core.plan[name], x, kts, factor, gain, loads

    def gpsimd(self, pool, s):
        if self.loads:
            self.loads.start(self.core, pool)
            self.loads.finish(self.core, pool)

    def tensor(self, pe, s):
        c, m = self.core, self.m
        xh, xl = self.x
        if self.source:
            self.source.tensor(pe, s)
        for k in range(self.kts):
            self.input_wait(pe, s, k)
            for half in range(2):
                i = 2 * k + half
                w = c.piece(pe, m, i)
                for b in range(NB):
                    cut = slice(b * P, (b + 1) * P)
                    last = mm3(pe, c.bank[4 + 2 * b + half][:, :], (xh[:, k, cut], xl[:, k, cut]), w,
                               k == 0, k == self.kts - 1)
                c.release(last, m, i)

    def row_factor(self, b):
        return self.factor

    def input_wait(self, pe, s, k):
        if self.source:
            pe.wait_ge(s["low_turned"], k + 1)

    def scalar(self, act, s):
        c = self.core
        if self.source:
            self.source.scalar(act, s)
        c.split_high(act, self.m.slot(self.m.count - 1))
        if self.gain is None:
            return
        act.wait_ge(c.slot_used, self.m.slot(self.m.count - 1) + 1)
        for b in range(NB):
            for half in range(2):
                act.activation(c.square[:, b, half * HALF:(half + 1) * HALF], c.bank[4 + 2 * b + half][:, :], ACT.Square,
                               accum_out=c.stat[:, 2 * b + half:2 * b + half + 1]).then_inc(s["squares_ready"], 1)
        act.wait_ge(s["means_ready"], 1)
        act.activation(c.stat[:, 4:6], c.stat[:, 4:6], ACT.Sqrt).then_inc(s["roots_ready"], 1)

    def vector(self, dve, s):
        c = self.core
        if self.source:
            self.source.vector(dve, s)
        c.split_low(dve, self.m.slot(self.m.count - 1))
        step = Steps(dve, s["sum_step"])
        dve.wait_ge(c.slot_used, self.m.slot(self.m.count - 1) + 1)
        if self.gain is not None:
            dve.wait_ge(s["squares_ready"], 4)
            sums = c.stat[:, 0:4].rearrange("p (b f) -> p b f", f=2)
            step(dve.tensor_reduce(c.stat[:, 4:6], sums, AX.X, ALU.add))
            dve.tensor_scalar(c.stat[:, 4:6], c.stat[:, 4:6], 1.0 / D, EPS, ALU.mult, ALU.add)\
               .then_inc(s["means_ready"], 1)
            dve.wait_ge(s["roots_ready"], 1)
            step(dve.reciprocal(c.stat[:, 4:6], c.stat[:, 4:6]))
        for b in range(NB):
            for half in range(2):
                ps = c.bank[4 + 2 * b + half][:, :]
                cut = slice(half * HALF, (half + 1) * HALF)
                if self.gain is None:
                    dve.scalar_tensor_tensor(c.h[:, b, cut], ps, self.row_factor(b), c.h[:, b, cut], ALU.mult, ALU.add)
                else:
                    step(dve.scalar_tensor_tensor(c.xn[:, b, cut], ps, c.stat[:, 4 + b:5 + b],
                                                  self.gain[:, cut], ALU.mult, ALU.mult))
                    dve.tensor_tensor(c.h[:, b, cut], c.h[:, b, cut], c.xn[:, b, cut], ALU.add)


class Ffn(Residual):

    def __init__(self, core, up, down, source, factor=1.0, gain=None, conv=False, loads=None):
        super().__init__(core, down, (core.hh, core.hl), FT, factor, gain, loads)
        self.up, self.conv, self.rows = core.plan[up], conv, source
        work = core.square[:, :, :].rearrange("p a b -> p (a b)")
        part = lambda at, n, w: work[:, at:at + n * w].rearrange("p (n w) -> p n w", n=n)
        self.product = part(0, 2, S)
        self.silu = part(2 * S, 3, S)
        self.mixed = part(2 * S, 3, HALF)
        self.scaled_in = part(2 * S + 3 * HALF, 2, HALF)

    def row_factor(self, b):
        return self.core.inv[:, 4 + b:5 + b]

    def tensor(self, pe, s):
        c = self.core
        self.rows.tensor(pe, s)
        for f in range(FT):
            if f == 1:
                self.rows.row(pe, s)
            if f >= 4:
                pe.wait_ge(s["partial_ready" if self.conv else "gates_ready"], f - 3)
            for part in range(2):
                for k in range(KT):
                    if f == 0 and part == 0:
                        pe.wait_ge(s["low_turned"], k + 1)
                    i = (2 * f + part) * KT + k
                    last = mm3(pe, c.bank[f % 4][:, part * S:(part + 1) * S], c.piece(pe, self.up, i),
                               (c.xh[:, k, :], c.xl[:, k, :]), k == 0, k == KT - 1)
                    c.release(last, self.up, i)
        super().tensor(pe, s)

    def input_wait(self, pe, s, k):
        pe.wait_ge(s["hidden_ready"], k + 1)

    def scalar(self, act, s):
        c = self.core
        self.rows.scalar(act, s)
        w = PARAM(c.param, "conv_w").rearrange("p (j f) -> p j f", j=3)
        bias = PARAM(c.param, "conv_b")
        late = 1 if self.conv else 0

        for step in range(FT + 1 + late):
            if step < FT:
                c.split_high(act, self.up.first + step)
            if step < FT and self.conv:
                f = step
                act.wait_ge(s["partial_ready"], f + 1)
                if f >= 3:
                    act.wait_ge(s["gates_ready"], f - 2)
                for part, col in ((0, f), (1, FT + f)):
                    last = act.activation(self.mixed[:, f % 3, part * S:(part + 1) * S],
                                          self.scaled_in[:, f % 2, part * S:(part + 1) * S], ACT.Identity,
                                          bias=bias[:, col:col + 1], scale=w[:, 2, col:col + 1])
                last.then_inc(s["scores_ready"], 1)
            if 0 <= step - late < FT:
                f = step - late
                act.wait_ge(s["convolved"], f + 1)
                gate = self.mixed[:, f % 3, 0:S] if self.conv else self.silu[:, f % 3, :]
                act.activation(gate, gate, ACT.Silu).then_inc(s["inputs_ready"], 1)
            if 0 <= step - late - 1 < FT:
                f = step - late - 1
                act.wait_ge(s["gates_ready"], f + 1)
                act.activation(c.hh[:, f, :], self.product[:, f % 2, :], ACT.Copy).then_inc(s["highs_ready"], 1)
        Residual.scalar(self, act, s)

    def vector(self, dve, s):
        c = self.core
        self.rows.vector(dve, s, self.factor, row=True)
        w = PARAM(c.param, "conv_w").rearrange("p (j f) -> p j f", j=3)
        taps, late = 0, 1 if self.conv else 0
        row = c.inv_row[:, :]

        for step in range(FT + 2 + late):
            if step < FT:
                f = step
                c.split_low(dve, self.up.first + f)
                dve.wait_ge(c.slot_used, self.up.first + f + 1)
                if f == 0:
                    self.rows.take_row(dve, s)
                ps = c.bank[f % 4]
                if self.conv:
                    if f >= 2:
                        dve.wait_ge(s["scores_ready"], f - 1)
                        dve.wait_ge(s["convolved"], f - 1)
                    dve.tensor_tensor(self.scaled_in[:, f % 2, :].rearrange("p (a t) -> p a t", a=2),
                                      ps[:, :].rearrange("p (a t) -> p a t", a=2),
                                      row.unsqueeze(1).to_broadcast([P, 2, S]), ALU.mult)\
                       .then_inc(s["partial_ready"], 1)
                else:
                    if f >= 3:
                        dve.wait_ge(s["gates_ready"], f - 2)
                    dve.tensor_tensor(self.silu[:, f % 3, :], ps[:, 0:S], row, ALU.mult).then_inc(s["convolved"], 1)
            if self.conv and 0 <= step - 1 < FT:
                f = step - 1
                dve.wait_ge(s["scores_ready"], f + 1)
                for j in (1, 0):
                    back = 2 - j
                    for part, col in ((0, f), (1, FT + f)):
                        if j == 0:
                            dve.wait_ge(s["dve_step"], 2 * f + 1 + part)
                        at = part * S
                        buf = self.mixed[:, f % 3, at + back:at + S]
                        i = dve.scalar_tensor_tensor(buf, self.scaled_in[:, f % 2, at:at + S - back],
                                                     w[:, j, col:col + 1], buf, ALU.mult, ALU.add)
                        if j == 1:
                            i.then_inc(s["dve_step"], 1)
                i.then_inc(s["convolved"], 1)
            if 0 <= step - late - 1 < FT:
                f = step - late - 1
                dve.wait_ge(s["inputs_ready"], f + 1)
                if f >= 2:
                    dve.wait_ge(s["hidden_ready"], f - 1)
                gate = self.mixed[:, f % 3, 0:S] if self.conv else self.silu[:, f % 3, :]
                value = self.mixed[:, f % 3, S:HALF] if self.conv else c.bank[f % 4][:, S:HALF]
                dve.tensor_tensor(self.product[:, f % 2, :], gate, value, ALU.mult).then_inc(s["gates_ready"], 1)
            if 0 <= step - late - 2 < FT:
                f = step - late - 2
                dve.wait_ge(s["highs_ready"], f + 1)
                dve.tensor_tensor(c.hl[:, f, :], self.product[:, f % 2, :], c.hh[:, f, :].bitcast(F32), ALU.subtract)\
                   .then_inc(s["hidden_ready"], 1)
        Residual.vector(self, dve, s)


class Merge(Stage):

    TILES = ((0, 1), (2,), (3, 4), (5, 6))

    def tensor(self, pe, s):
        c = self.core
        for n in range(4):
            branch, gate = c.plan[f"branch{n}"], c.plan[f"gate{n}"]
            kts = self.TILES[n]
            if n:
                pe.wait_ge(s["out_taken"], 4 * n)
            for half in range(2):
                for j, k in enumerate(kts):
                    i = half * len(kts) + j
                    w = c.piece(pe, branch, i)
                    for b in range(NB):
                        cut = slice(b * P, (b + 1) * P)
                        last = mm3(pe, c.bank[4 + 2 * half + b][:, :], (c.oh[:, k, cut], c.ol[:, k, cut]), w,
                                   j == 0, j == len(kts) - 1)
                    c.release(last, branch, i)
            for half in range(2):
                for k in range(KT):
                    i = half * KT + k
                    w = c.piece(pe, gate, i)
                    for b in range(NB):
                        cut = slice(b * P, (b + 1) * P)
                        last = mm3(pe, c.bank[2 * half + b][:, :], (c.xh[:, k, cut], c.xl[:, k, cut]), w,
                                   k == 0, k == KT - 1)
                    c.release(last, gate, i)

    def scalar(self, act, s):
        c = self.core
        for n in range(4):
            gate = c.plan[f"gate{n}"]
            for half in range(2):
                c.split_high(act, gate.first + 2 * half + 1)
                act.wait_ge(c.slot_used, gate.first + 2 * half + 2)
                for b in range(NB):
                    q = 2 * half + b
                    if n:
                        act.wait_ge(s["out_taken"], 4 * (n - 1) + q + 1)
                    act.activation(c.square[:, q // 2, (q % 2) * HALF:(q % 2 + 1) * HALF], c.bank[q][:, :],
                                   ACT.Sigmoid, scale=c.inv[:, 2 + b:3 + b]).then_inc(s["gates_ready"], 1)

    def vector(self, dve, s):
        c = self.core
        step = Steps(dve, s["dve_step"])
        for n in range(4):
            gate = c.plan[f"gate{n}"]
            for half in range(2):
                c.split_low(dve, gate.first + 2 * half + 1)
                for b in range(NB):
                    q = 2 * half + b
                    dve.wait_ge(s["gates_ready"], 4 * n + q + 1)
                    g = c.square[:, q // 2, (q % 2) * HALF:(q % 2 + 1) * HALF]
                    out = c.xn[:, b, half * HALF:(half + 1) * HALF]
                    if n == 0:
                        dve.tensor_tensor(out, g, c.bank[4 + q][:, :], ALU.mult).then_inc(s["out_taken"], 1)
                    else:
                        dve.wait_ge(s["out_taken"], 4 * n + q)
                        step(dve.tensor_tensor(c.square[:, 2, 0:HALF], g, c.bank[4 + q][:, :], ALU.mult))
                        dve.tensor_tensor(out, out, c.square[:, 2, 0:HALF], ALU.add).then_inc(s["out_taken"], 1)


class Unit:

    def __init__(self, q, k, v, parts, scale, dv, finish, cols, bias=None, minus=False, extra=None):
        self.q, self.k, self.v, self.parts, self.scale, self.dv = q, k, v, parts, scale, dv
        self.finish, self.cols, self.bias, self.minus, self.extra = finish, cols, bias, minus, extra
        self.n, self.nk = len(q), sum(parts)


class Attention(Stage):
    def __init__(self, core, units, before=None, loads=None):
        super().__init__(core)
        self.units, self.before, self.loads = units, before, loads

    def gpsimd(self, pool, s):
        if self.loads:
            self.loads.start(self.core, pool)
            self.loads.finish(self.core, pool)

    SCORE_BANKS = (0, 1, 6)

    def scores(self, i):
        u = self.units[i]
        bank = self.core.bank[self.SCORE_BANKS[i % 3]]
        return bank[:, :].rearrange("p (n k) -> p n k", n=2)[:, 0:u.n, 0:u.nk]

    def tensor(self, pe, s):
        c, units = self.core, self.units

        def score(i):
            u = units[i]
            if i >= 3:
                pe.wait_ge(s["logits_ready" if units[i - 3].bias is not None else "probs_ready"], i - 2)
            ps = self.scores(i)
            for j in range(u.n):
                last = mm(pe, ps[:, j, :], u.q[j], u.k[j], True, True)
            last.then_inc(s["scores_ready"], 1)

        def turn(i):
            u = units[i]
            pe.wait_ge(s["probs_ready"], i + 1)
            if i >= 2:
                pe.wait_ge(s["probs_copied"], i - 1)
            for j in range(u.n):
                for t, size in enumerate(u.parts):
                    at = (j * len(u.parts) + t) * P
                    last = pe.transpose(c.bank[2 + i % 2][0:size, at:at + P],
                                        c.prob[:, i % 4, j, t * P:t * P + size], c.ident)
            last.then_inc(s["probs_turned"], 1)

        def value(i):
            u = units[i]
            pe.wait_ge(s["probs_copied"], i + 1)
            if i >= 2:
                pe.wait_ge(s["out_taken"], i - 1)
            for j in range(u.n):
                for t, size in enumerate(u.parts):
                    last = mm(pe, c.bank[4 + i % 2][:, j * u.dv:(j + 1) * u.dv],
                              c.prob_t[0:size, i % 2, j * len(u.parts) + t, :], u.v[j][t],
                              t == 0, t == len(u.parts) - 1)
            last.then_inc(s["out_ready"], 1)

        for i in range(min(3, len(units))):
            score(i)
        for i in range(len(units) + 1):
            if i < len(units):
                turn(i)
            if i + 3 < len(units):
                score(i + 3)
            if i:
                value(i - 1)

    def scalar(self, act, s):
        c, units = self.core, self.units
        c.split_high(act, -LEAD)

        def exp(i):
            u = units[i]
            act.wait_ge(s["logits_ready"], i + 1)
            if i >= 4:
                act.wait_ge(s["probs_turned"], i - 3)
            for j in range(u.n):
                dst = c.prob[:, i % 4, j, 0:u.nk]
                src, scale = (dst, 1.0) if u.bias is not None else (self.scores(i)[:, j, :], u.scale)
                col = u.cols.start + j * (u.cols.step or 1)
                last = act.activation(dst, src, ACT.Exp, bias=c.nmax[:, col:col + 1],
                                      scale=scale, accum_out=c.den[:, col:col + 1])
            last.then_inc(s["probs_ready"], 1)

        exp(0)
        for i, u in enumerate(units):
            if i + 1 < len(units):
                exp(i + 1)
            act.wait_ge(s["probs_turned"], i + 1)
            if i >= 2:
                act.wait_ge(s["out_ready"], i - 1)
            size, tiles = u.parts[0], u.n * len(u.parts)
            act.activation(c.prob_t[0:size, i % 2, 0:tiles, :],
                           c.bank[2 + i % 2][0:size, 0:tiles * P].rearrange("p (n q) -> p n q", q=P),
                           ACT.Copy).then_inc(s["probs_copied"], 1)

    def vector(self, dve, s):
        c, units = self.core, self.units
        step = Steps(dve, s["dve_step"])

        def logits(i):
            u = units[i]
            dve.wait_ge(s["scores_ready"], i + 1)
            if i >= 4:
                dve.wait_ge(s["probs_turned"], i - 3)
            ps = self.scores(i)
            if u.bias is None:
                step(dve.tensor_reduce(c.nmax[:, u.cols], ps, AX.X, ALU.max, negate=True))
                dve.tensor_scalar(c.nmax[:, u.cols], c.nmax[:, u.cols], u.scale, None, ALU.mult)\
                   .then_inc(s["logits_ready"], 1)
                return
            t = c.prob[:, i % 4, 0:u.n, 0:u.nk]
            step(dve.scalar_tensor_tensor(t, ps, u.scale, u.bias, ALU.mult, ALU.subtract if u.minus else ALU.add))
            if u.extra is not None:
                step(dve.tensor_tensor(t, t, u.extra, ALU.add))
            dve.tensor_reduce(c.nmax[:, u.cols], t, AX.X, ALU.max, negate=True).then_inc(s["logits_ready"], 1)

        def finish(i):
            u = units[i]
            dve.wait_ge(s["out_ready"], i + 1)
            if i:
                dve.wait_ge(s["out_taken"], i)
            ps = c.bank[4 + i % 2][:, 0:u.n * u.dv].rearrange("p (n d) -> p n d", n=u.n)
            u.finish(dve, step, u, ps).then_inc(s["out_taken"], 1)

        logits(0)
        logits(1)
        for i in range(len(units) + 2):
            if i + 2 < len(units):
                logits(i + 2)
            if i >= 2:
                finish(i - 2)


def scaled(core, dst, factor=None, add=False):

    def finish(dve, step, u, ps):
        r = core.rden[:, u.cols]
        step(dve.reciprocal(r, core.den[:, u.cols]))
        if factor is not None:
            step(dve.tensor_tensor(r, r, factor, ALU.mult))
        if not add:
            return dve.tensor_tensor(dst, ps, r.unsqueeze(2).to_broadcast([P, u.n, u.dv]), ALU.mult)
        for j in range(u.n):
            col = u.cols.start + j * (u.cols.step or 1)
            last = dve.scalar_tensor_tensor(dst[:, j, :], ps[:, j, :], core.rden[:, col:col + 1], dst[:, j, :],
                                            ALU.mult, ALU.add)
        return last

    return finish


def kept(core, dst):
    return lambda dve, step, u, ps: dve.tensor_copy(dst, ps)


class Compress(Stage):

    def __init__(self, core):
        super().__init__(core)
        c = core
        self.m = c.plan["phi"]
        free = c.u[:, 0, 2600:3720]
        self.x = free[:, 0:512].rearrange("p (l c) -> p l c", c=16)
        self.xh = c.over("blocks_h", [P, 32, 16], F32R, c.xn_at)
        self.xl = c.over("blocks_l", [P, 32, 16], F32R, c.xn_at + 512 * 4)
        self.g = free[:, 512:544].rearrange("p (a c) -> p a c", a=2)
        self.v = core.small[:, 0:DH]
        self.k = core.small[:, DH:DH + 16]
        self.lf = free[:, 560:568].rearrange("p (b h) -> p b h", b=NB)
        self.t1 = free[:, 576:584].rearrange("p (b h) -> p b h", b=NB)
        self.t2 = free[:, 592:600].rearrange("p (b h) -> p b h", b=NB)
        self.cq = free[:, 608:616].rearrange("p (b h) -> p b h", b=NB)
        self.spread = c.square[:, 0, :].rearrange("p (b h q) -> p b h q", b=NB, h=4)
        self.gates = core.small[:, 96:96 + 24].rearrange("p (b g) -> p b g", b=NB)
        self.cmp_gates = core.small[:, 128:136].rearrange("p (b h) -> p b h", b=NB)

    def tensor(self, pe, s):
        c = self.core
        pe.wait_ge(s["inputs_ready"], 1)
        for l in range(32):
            c.piece(pe, self.m, l)
            w = c.raw[:, self.m.slot(l) % RING, self.m.offset(l):self.m.offset(l) + P]
            for part, rows in ((0, slice(0, DH)), (1, slice(DH, P))):
                last = mm(pe, c.bank[part][:, 0:16], w[rows], self.x[rows, l, :],
                           l == 0, l == 31)
            c.release(last, self.m, l)
        pe.wait_ge(s["partial_ready"], 1)
        upto, ones = CONST(c.const, "upto"), CONST(c.const, "ones")
        mm(pe, c.bank[2][:, 0:4], upto, self.lf[:, 0, :], True, True)
        mm(pe, c.bank[2][:, 4:8], ones, self.lf[:, 0, :], True, False)
        mm(pe, c.bank[2][:, 4:8], upto, self.lf[:, 1, :], False, True).then_inc(s["scores_ready"], 1)
        for h in range(4):
            ps = c.bank[3 + h // 2][:, (h % 2) * S:(h % 2 + 1) * S]
            mm(pe, ps[:, 0:P], self.spread[:, 0, h, :], upto, True, True)
            mm(pe, ps[:, P:S], self.spread[:, 0, h, :], ones, True, False)
            last = mm(pe, ps[:, P:S], self.spread[:, 1, h, :], upto, False, True)
        last.then_inc(s["scores_ready"], 1)
        pe.wait_ge(s["gates_ready"], 1)
        mm(pe, c.bank[5][:, 0:16], PARAM(c.param, "w2k"), self.g[:, 0, :], True, True)
        mm(pe, c.bank[6][0:16, 0:DH], self.g[:, 1, :], PARAM(c.param, "w2v"), True, True).then_inc(s["out_ready"], 1)

    def scalar(self, act, s):
        c = self.core
        act.wait_ge(s["convolved"], 1)
        act.activation(self.xh[:, :, :], self.x, ACT.Copy).then_inc(s["highs_ready"], 1)
        c.split_high(act, self.m.first + self.m.slots - 1)
        step = Steps(act, s["act_step"])
        act.wait_ge(s["sums_ready"], 1)
        step(act.activation(self.t2, self.t1, ACT.Abs))
        step(act.activation(self.t2, self.t2, ACT.Exp, scale=-1.0))
        act.activation(self.t2, self.t2, ACT.Ln, bias=1.0).then_inc(s["means_ready"], 1)
        for b in range(NB):
            last = act.activation(self.gates[:, b, :], c.u[:, b, 128:140], ACT.Sigmoid)
        last.then_inc(s["roots_ready"], 1)
        act.wait_ge(c.slot_used, self.m.first + self.m.slots)
        act.activation(self.g[:, 0, :], c.bank[0][:, 0:16], ACT.Gelu_apprx_tanh)
        act.activation(self.g[:, 1, :], c.bank[1][:, 0:16], ACT.Gelu_apprx_tanh).then_inc(s["gates_ready"], 1)

    def vector(self, dve, s):
        c = self.core
        step = Steps(dve, s["dve_step"])
        step(dve.memset(self.x[:, :, 15:16], 0.0))
        tok = c.t[:, 4, :].rearrange("p (c l) -> p l c", l=16)
        pos = PARAM(c.param, "cmp_pos")
        for part in range(2):
            cut = slice(16 * part, 16 * part + 16)
            last = dve.tensor_tensor(self.x[:, cut, 0:15], tok[:, :, part:part + 15],
                                     pos[:, cut].unsqueeze(2).to_broadcast([P, 16, 15]), ALU.add)
        last.then_inc(s["convolved"], 1)
        dve.wait_ge(s["highs_ready"], 1)
        dve.tensor_tensor(self.xl[:, :, :], self.x, self.xh[:, :, :].bitcast(F32), ALU.subtract)\
           .then_inc(s["inputs_ready"], 1)
        bias = PARAM(c.param, "f_bias")
        for b in range(NB):
            last = dve.tensor_tensor(self.t1[:, b, :], c.u[:, b, 780:784], bias, ALU.add)
        last.then_inc(s["sums_ready"], 1)
        c.split_low(dve, self.m.first + self.m.slots - 1)
        dve.wait_ge(s["means_ready"], 1)
        step(dve.scalar_tensor_tensor(self.lf, self.t1, 0.0, self.t2, ALU.min, ALU.subtract))
        dve.tensor_copy(self.spread, self.lf.unsqueeze(3).to_broadcast([P, NB, 4, P]))\
           .then_inc(s["partial_ready"], 1)
        dve.wait_ge(s["roots_ready"], 1)
        gates = self.gates.rearrange("p b (h r) -> p b h r", r=3)
        for b in range(NB):
            dve.tensor_scalar(self.cmp_gates[:, b, :], gates[:, b, :, 0], CONST(c.const, "cmp_valid")[:, b:b + 1],
                              None, ALU.mult)
        dve.wait_ge(s["scores_ready"], 2)
        step(dve.tensor_copy(self.cq, c.bank[2][:, 0:8].rearrange("p (b h) -> p b h", b=NB)))
        causal = CONST(c.const, "causal")
        for b in range(NB):
            nk = (b + 1) * P
            for h in range(4):
                ps = c.bank[3 + h // 2][:, (h % 2) * S:(h % 2) * S + nk]
                dve.scalar_tensor_tensor(c.forget[:, b, h, 0:nk], ps, self.cq[:, b, h:h + 1], causal[:, S - nk:S],
                                         ALU.subtract, ALU.subtract)
        dve.wait_ge(s["out_ready"], 1)
        dve.tensor_copy(self.k[:, 0:15], c.bank[5][:, 0:15])
        dve.tensor_copy(self.v[0:15, :], c.bank[6][0:15, 0:DH])


class Rope(Stage):

    def __init__(self, core, q, kv, rope, k):
        super().__init__(core)
        self.q, self.kv, self.rope, self.k = q, kv, rope, k

    def vector(self, dve, s):
        c = self.core
        step = Steps(dve, s["dve_step"])
        for b in range(NB):
            cos = CONST(c.const, "cos")[:, 16 * b:16 * b + 16]
            sin = CONST(c.const, "sin")[:, 16 * b:16 * b + 16]
            q = self.q(b).rearrange("p (h d) -> p h d", h=4)
            k = self.k(b).rearrange("p (h d) -> p h d", h=4)
            kv = self.kv(b).rearrange("p (h d) -> p h d", h=4)
            rope = self.rope(b).unsqueeze(1)
            for n, x in ((4, q[:, :, DH:96]), (1, rope)):
                t = c.square[:, b, 0:4 * n * 16].rearrange("p (a h d) -> p a h d", a=4, h=n)
                w = lambda a: a.unsqueeze(1).to_broadcast([P, n, 16])
                x1, x2 = x[:, :, 0:16], x[:, :, 16:32]
                dve.tensor_tensor(t[:, 0], x1, w(cos), ALU.mult)
                dve.tensor_tensor(t[:, 1], x2, w(sin), ALU.mult)
                dve.tensor_tensor(t[:, 2], x2, w(cos), ALU.mult)
                step(dve.tensor_tensor(t[:, 3], x1, w(sin), ALU.mult))
                dve.tensor_tensor(x1, t[:, 0], t[:, 1], ALU.subtract)
                step(dve.tensor_tensor(x2, t[:, 2], t[:, 3], ALU.add))
            dve.tensor_copy(k[:, :, 0:DH], kv[:, :, 0:DH])
            dve.tensor_copy(k[:, :, DH:96], rope.to_broadcast([P, 4, 32]))


class Dilated(Stage):

    def __init__(self, core, kept_products, base):
        super().__init__(core)
        c = core
        cut = slice(base, base + 12)
        shape = lambda a: a.rearrange("p (b g h) -> p b g h", b=NB, g=3)
        self.nm, self.den = shape(c.nmax[:, cut]), shape(c.den[:, cut])
        self.e = shape(c.rden[:, cut])
        self.m = c.stat[:, 0:4].rearrange("p (b h) -> p b h", b=NB)
        self.sum = c.stat[:, 4:8].rearrange("p (b h) -> p b h", b=NB)
        self.products = kept_products
        self.t = c.square[:, 0, 0:768].rearrange("p (b g h d) -> p b g h d", b=NB, g=3, h=2)

    def scalar(self, act, s):
        act.wait_ge(s["inputs_ready"], 1)
        for b in range(NB):
            last = act.activation(self.e[:, b], self.e[:, b], ACT.Exp)
        last.then_inc(s["probs_ready"], 1)

    def vector(self, dve, s):
        step = Steps(dve, s["dve_step"])
        nm, den, e, m, total = self.nm, self.den, self.e, self.m, self.sum
        step(dve.tensor_tensor(m, nm[:, :, 0], nm[:, :, 1], ALU.min))
        step(dve.tensor_tensor(m, m, nm[:, :, 2], ALU.min))
        for g in range(3):
            last = dve.tensor_tensor(e[:, :, g], m, nm[:, :, g], ALU.subtract)
        last.then_inc(s["inputs_ready"], 1)
        dve.wait_ge(s["probs_ready"], 1)
        flat = lambda a: a.rearrange("p b g h -> p (b g h)")
        step(dve.tensor_tensor(self.core.stat[:, 16:28], flat(e), flat(den), ALU.mult))
        ed = self.core.stat[:, 16:28].rearrange("p (b g h) -> p b g h", b=NB, g=3)
        step(dve.tensor_tensor(total, ed[:, :, 0], ed[:, :, 1], ALU.add))
        step(dve.tensor_tensor(total, total, ed[:, :, 2], ALU.add))
        step(dve.reciprocal(total, total))
        for g in range(3):
            last = dve.tensor_tensor(e[:, :, g], e[:, :, g], total, ALU.mult)
        step(last)
        for b in range(NB):
            x = self.products[:, b].rearrange("p g h d -> p (g h) d")
            w = e[:, b].rearrange("p g h -> p (g h)").unsqueeze(2).to_broadcast([P, 6, DH])
            last = dve.tensor_tensor(self.t[:, b].rearrange("p g h d -> p (g h) d"), x, w, ALU.mult)
        step(last)
        for b in range(NB):
            out = self.core.o[:, b, 256:384].rearrange("p (h d) -> p h d", h=2)
            step(dve.tensor_tensor(out, self.t[:, b, 0], self.t[:, b, 1], ALU.add))
            dve.tensor_tensor(out, out, self.t[:, b, 2], ALU.add)


class Select(Stage):

    def __init__(self, core, q, k, weights):
        super().__init__(core)
        self.q, self.k, self.weights = q, k, weights
        c = core
        self.relu = c.square[:, 0, :].rearrange("p (n j k) -> p n j k", n=2, j=2)
        self.score = c.square[:, 1, 0:HALF].rearrange("p (b k) -> p b k", b=NB)
        self.best = c.square[:, 1, HALF:HALF + 16].rearrange("p (b k) -> p b k", b=NB)
        self.w = c.square[:, 2, 0:16].rearrange("p (b h) -> p b h", b=NB)
        self.units = [(b, pair) for b in range(NB) for pair in ((0, 2), (1, 3), (4, 6), (5, 7))]

    def tensor(self, pe, s):
        c = self.core
        for i, (b, pair) in enumerate(self.units):
            nk = (b + 1) * P
            if i >= 2:
                pe.wait_ge(s["probs_ready"], i - 1)
            for j, h in enumerate(pair):
                last = mm(pe, c.bank[i % 2][:, j * S:j * S + nk], self.q(h)[:, b * P:(b + 1) * P],
                          self.k(h)[:, 0:nk], True, True)
            last.then_inc(s["scores_ready"], 1)

    def scalar(self, act, s):
        c = self.core
        for i, (b, pair) in enumerate(self.units):
            nk = (b + 1) * P
            act.wait_ge(s["scores_ready"], i + 1)
            if i >= 2:
                act.wait_ge(s["out_taken"], i - 1)
            ps = c.bank[i % 2][:, :].rearrange("p (j k) -> p j k", j=2)[:, :, 0:nk]
            act.activation(self.relu[:, i % 2, :, 0:nk], ps, ACT.Relu, scale=DH ** -0.5)\
               .then_inc(s["probs_ready"], 1)

    def vector(self, dve, s):
        c = self.core
        step = Steps(dve, s["dve_step"])
        for b in range(NB):
            step(dve.tensor_scalar(self.w[:, b, :], self.weights(b), 8 ** -0.5, None, ALU.mult))
        for i, (b, pair) in enumerate(self.units):
            nk = (b + 1) * P
            dve.wait_ge(s["probs_ready"], i + 1)
            for j, h in enumerate(pair):
                r, score, w = self.relu[:, i % 2, j, 0:nk], self.score[:, b, 0:nk], self.w[:, b, h:h + 1]
                if i % 4 == 0 and j == 0:
                    step(dve.tensor_scalar(score, r, w, None, ALU.mult))
                else:
                    m = dve.scalar_tensor_tensor(score, r, w, score, ALU.mult, ALU.add)
                    if j == 0:
                        step(m)
            m.then_inc(s["out_taken"], 1)
            dve.wait_ge(s["out_taken"], i + 1)
        for b in range(NB):
            nk = (b + 1) * P
            score = self.score[:, b, 0:nk]
            step(dve.memset(score[0:DH, nk - DH:nk], NEG))
            for n in range(TOP_K // 8):
                step(dve.max(self.best[:, b, :], score))
                step(dve.match_replace(score, self.best[:, b, :], score, TAKEN))
            dve.tensor_scalar(c.taken[:, b, 0:nk], score, TAKEN, NEG, ALU.not_equal, ALU.mult)


class Lambda(Stage):

    def vector(self, dve, s):
        c = self.core
        step = Steps(dve, s["dve_step"])
        lam = PARAM(c.param, "lam").rearrange("p (n d) -> p n d", n=4)
        for n in range(2):
            step(dve.tensor_tensor(c.square[:, 0, n * DH:(n + 1) * DH], lam[:, 2 * n, :], lam[:, 2 * n + 1, :], ALU.mult))
        dve.tensor_reduce(c.small[:, 144:146], c.square[:, 0, 0:2 * DH].rearrange("p (n d) -> p n d", n=2),
                          AX.X, ALU.add).then_inc(s["sums_ready"], 1)
        dve.wait_ge(s["probs_ready"], 1)
        step(dve.tensor_tensor(c.small[:, 140:141], c.small[:, 147:148], c.small[:, 146:147], ALU.subtract))
        step(dve.tensor_scalar(c.small[:, 140:141], c.small[:, 140:141], -LAMBDA_INIT, None, ALU.add))
        dve.tensor_copy(c.small[:, 141:142], c.small[:, 140:141])
        dve.memset(c.bias[0:DH, 0:12, S - DH:S], NEG)

    def scalar(self, act, s):
        c = self.core
        act.wait_ge(s["sums_ready"], 1)
        act.activation(c.small[:, 146:148], c.small[:, 144:146], ACT.Exp).then_inc(s["probs_ready"], 1)


class MaskBand(Stage):

    def vector(self, dve, s):
        dve.memset(self.core.bias[0:DH, 0:16, S - DH:S], NEG)


LAMBDA_INIT = 0.8 - 0.6 * math.exp(0.0)


class Store(Stage):
    def __init__(self, core, out):
        super().__init__(core)
        self.out = out

    def gpsimd(self, pool, s):
        c = self.core
        pool.dma_start(self.out, c.h[:, :, :]).then_inc(c.stored, 16)
        pool.wait_ge(c.stored, 16)



def half(tile, h, cols=slice(None)):
    return tile[(h % 2) * DH:(h % 2 + 1) * DH, h // 2, cols]


def block_cut(b):
    return slice(b * P, (b + 1) * P)


def first_units(c, compress):
    units = []
    rel = c.bias
    pairs = ((0, 2), (1, 3))
    for b in range(NB):
        nk, parts = (b + 1) * P, [P] * (b + 1)
        keys, qs = slice(0, nk), block_cut(b)
        for pair in pairs:
            q = [half(c.t, h, qs) for h in pair]
            rows = slice((pair[0] % 2) * DH, (pair[0] % 2 + 1) * DH)
            heads = slice(pair[0], 4, 2)
            dst = c.o[:, b, 0:256].rearrange("p (h d) -> p h d", d=DH)[:, heads, :]
            gates = compress.gates[:, b, :].rearrange("p (h r) -> p h r", r=3)
            at = 2 * len(units)
            mask = CONST(c.const, "cmp_mask")[:, 15 * b:15 * b + 15].unsqueeze(1).to_broadcast([P, 2, 15])
            units.append(Unit(q, [compress.k[rows, 0:15]] * 2, [[compress.v[0:15, :]]] * 2, [15], DH ** -0.5, DH,
                              scaled(c, dst, compress.cmp_gates[:, b, heads]), slice(at, at + 2), mask))
            for r, (kt, v0) in enumerate(((2, 0), (3, DH)), 1):
                at = 2 * len(units)
                k = c.t[rows, kt, keys]
                v = [c.u[:, t, v0:v0 + DH] for t in range(b + 1)]
                units.append(Unit(q, [k, k], [v, v], parts, DH ** -0.5, DH, scaled(c, dst, gates[:, heads, r], add=True),
                                  slice(at, at + 2), rel[:, heads, S - nk:S]))
    base = 2 * len(units)
    for b in range(NB):
        nk, parts = (b + 1) * P, [P] * (b + 1)
        keys, qs = slice(0, nk), block_cut(b)
        for heads in ((0, 2), (1, 3), (4,), (5,)):
            q = [half(c.t[:, 5:8, :], h, qs) for h in heads]
            k = [half(c.t[:, 8:11, :], h, keys) for h in heads]
            v = [[c.u[:, t, 140 + h * DH:140 + (h + 1) * DH] for t in range(b + 1)] for h in heads]
            cut = slice(heads[0], heads[-1] + 1, 2)
            dst = c.products[:, b].rearrange("p g h d -> p (g h) d")[:, cut, :]
            units.append(Unit(q, k, v, parts, DH ** -0.5, DH, kept(c, dst),
                              slice(base + 6 * b + heads[0], base + 6 * b + heads[-1] + 1, 2),
                              rel[:, slice(4 + heads[0], 4 + heads[-1] + 1, 2), S - nk:S]))
    at = base + 12
    for b in range(NB):
        nk, parts = (b + 1) * P, [P] * (b + 1)
        keys, qs = slice(0, nk), block_cut(b)
        for pair in pairs:
            heads = slice(pair[0], 4, 2)
            v = [[c.u[:, t, 524 + h * DH:524 + (h + 1) * DH] for t in range(b + 1)] for h in pair]
            dst = c.o[:, b, 384:640].rearrange("p (h d) -> p h d", d=DH)[:, heads, :]
            units.append(Unit([half(c.t[:, 11:13, :], h, qs) for h in pair], [half(c.t[:, 13:15, :], h, keys) for h in pair],
                              v, parts, DH ** -0.5, DH, scaled(c, dst), slice(at, at + 2),
                              c.forget[:, b, heads, 0:nk], minus=True))
            at += 2
        for pair in ((0, 1), (2, 3)):
            heads = slice(pair[0], pair[0] + 2)
            v = [[c.u[:, t, 1584 + h * P + DH:1584 + (h + 1) * P] for t in range(b + 1)] for h in pair]
            dst = c.o[:, b, 640:896].rearrange("p (h d) -> p h d", d=DH)[:, heads, :]
            mask = CONST(c.const, "causal")[:, S - nk:S].unsqueeze(1).to_broadcast([P, 2, nk])
            units.append(Unit([c.t[0:96, 15 + h, qs] for h in pair], [c.t[0:96, 19 + h, keys] for h in pair], v, parts,
                              96 ** -0.5, DH, scaled(c, dst), slice(at, at + 2), mask))
            at += 2
    return units, base


def turn_groups(rows, tiles, dst, gain, need, t0, cut):
    return [(need, [rows[:, (q + j) * P:(q + j + 1) * P] for j in range(min(4, tiles - q))], P, "f32",
             dst[:, t0 + q:t0 + min(q + 4, tiles), cut], gain) for q in range(0, tiles, 4)]


def memory_stages(c, layer):
    u, t, heads = c.u, c.t, 4
    wkv, wq, wo = c.plan[f"wkv{layer}"], c.plan[f"wq{layer}"], c.plan[f"wo{layer}"]
    mem = c.u[:, :, 2048:3072]
    gain = lambda n: PARAM(c.param, f"{n}{layer}")
    x = (c.xh, c.xl)
    out = [Project(c, x, [(wkv, n * KT, range(KT), HALF, [u[:, b, n * HALF:(n + 1) * HALF] for b in range(NB)])
                          for n in range(2)], source=Source(c, mem, x, gain=f"l{layer}_src", norm=True), scale=True),
           Project(c, x, [(wq, 0, range(KT), HALF, [u[:, b, D:D + HALF] for b in range(NB)])],
                   source=Source(c, c.h, x, gain=f"l{layer}_mem", norm=True), scale=True)]
    segments, groups = [], []
    for b in range(NB):
        for n, at in enumerate((0, D)):
            rows = u[:, b, at:at + HALF]
            segments.append((rows.rearrange("p (h d) -> p h d", h=heads), None, None, 1.0))
            groups += turn_groups(rows, heads, t, gain("mk" if n == 0 else "mq"), 2 * b + n + 1, 4 * n, block_cut(b))
    out.append(Turn(c, segments, groups))
    units = []
    for b in range(NB):
        for pair in ((0, 1), (2, 3)):
            at = 2 * len(units)
            dst = c.o[:, b, 0:HALF].rearrange("p (h d) -> p h d", h=heads)[:, pair[0]:pair[0] + 2, :]
            v = [[u[:, k, HALF + h * P:HALF + (h + 1) * P] for k in range(NB)] for h in pair]
            units.append(Unit([t[:, 4 + h, block_cut(b)] for h in pair], [t[:, h, :] for h in pair], v, [P, P],
                              P ** -0.5, P, scaled(c, dst), slice(at, at + 2)))
    out.append(Attention(c, units))
    turned = (c.oh, c.ol)
    out.append(Residual(c, f"wo{layer}", turned, heads, source=Source(c, c.o, turned, heads, base=0)))
    return out


def out_turn(c, tiles, gain=None, segments=()):
    groups = []
    for b in range(NB):
        for q in range(0, tiles, 4):
            n = min(4, tiles - q)
            cut = (slice(None), slice(q, q + n), block_cut(b))
            groups.append((len(segments), [c.o[:, b, (q + j) * P:(q + j + 1) * P] for j in range(n)], P, "pair",
                           (c.oh[cut], c.ol[cut]), gain if q >= 4 else None))
    return Turn(c, list(segments), groups)


def dram_row(dram, name):
    n = ROWS.index(name)
    return dram["rows"][n:n + 1, :].to_broadcast([P, D])


def first_mixer(c, dram):
    x, u = (c.xh, c.xl), c.u
    m = c.plan["in_n"]
    widths = [HALF, HALF, 1200 - 2 * HALF]
    st = [ProjectTurned(c, "in_t", 15, Source(c, c.h, x, gain="attn_pre", norm=True), Loads(*[spread(dram[n + "_rows"], dram[n + "_wide"]) for n in ("rel", "t5", "band")])),
          Project(c, x, [(m, n * KT, range(KT), w, [u[:, b, n * HALF:n * HALF + w] for b in range(NB)])
                         for n, w in enumerate(widths)],
                  Loads((c.bias[:, 0:10, :], toeplitz(dram["rel_wide"], 10)),
                        (c.gain[:, 0, :], dram_row(dram, "attn_post")), (c.gain[:, 1, :], dram_row(dram, "ffn_post"))), scale=True)]
    segments, groups = [], []
    for b in range(NB):
        q, kv = u[:, b, 784:1040], u[:, b, 1040:1168]
        segments += [(q.unsqueeze(1), None, None, 1.0), (kv.unsqueeze(1), None, None, 1.0)]
        for tile, rows, g in ((0, q[:, 0:P], "mla_q"), (1, q[:, P:2 * P], "mla_q"), (2, kv, "mla_kv")):
            col = PARAM(c.param, g)[:, tile % 2:tile % 2 + 1]
            cut = (slice(None), slice(tile, tile + 1), block_cut(b))
            groups.append((2 * b + (2 if tile == 2 else 1), [rows], P, "pair", (c.latent_h[cut], c.latent_l[cut]), col))
    m = c.plan["mla"]
    st += [Turn(c, segments, groups),
           Project(c, (c.latent_h, c.latent_l),
                   [(m, 0, (0, 1), 384, [u[:, b, 1200:1584] for b in range(NB)]),
                    (m, 2, (2,), HALF, [u[:, b, 1584:2096] for b in range(NB)])]),
           Rope(c, lambda b: u[:, b, 1200:1584], lambda b: u[:, b, 1584:2096], lambda b: u[:, b, 1168:1200],
                lambda b: u[:, b, 2096:2480])]
    groups = []
    for b in range(NB):
        for n, at in enumerate((1200, 2096)):
            groups.append((0, [u[:, b, at + 96 * h:at + 96 * (h + 1)] for h in range(4)], 96, "f32",
                           c.t[0:96, 15 + 4 * n:19 + 4 * n, block_cut(b)], None))
    compress = Compress(c)
    units, base = first_units(c, compress)
    st += [Turn(c, [], groups), compress, Attention(c, units), Dilated(c, c.products, base),
           out_turn(c, 7), Merge(c),
           Residual(c, "w_o", x, KT, gain=c.gain[:, 0, :], source=Source(c, c.xn, x, base=0))]
    return st


def even_mixer(c, dram):
    x, u, t = (c.xh, c.xl), c.u, c.t
    m, tail = c.plan["even"], c.plan["even_tail"]
    jobs = [(m, n * KT, range(KT), HALF, [u[:, b, n * HALF:(n + 1) * HALF] for b in range(NB)]) for n in range(7)]
    jobs.append((tail, 0, range(KT), 136, [u[:, b, 3584:3720] for b in range(NB)]))
    st = [Project(c, x, jobs, source=Source(c, c.h, x, gain="l0_mix", norm=True), scale=True)]
    segments, groups = [], []
    for b in range(NB):
        by_head = lambda a, n: u[:, b, a:a + n].rearrange("p (h d) -> p h d", d=DH)
        segments += [(by_head(0, D), None, None, 1.0), (by_head(3584, P), None, None, 1.0),
                     (by_head(1536, D), None, None, 1.0)]
        for at, tiles, t0, gain, need in ((0, 4, 0, "a_q", 1), (512, 4, 4, "a_k", 1), (1024, 4, 8, None, 1),
                                          (3584, 1, 12, "idx_k", 2), (1536, 4, 13, "b_q", 3), (2048, 4, 17, "b_k", 3)):
            col = PARAM(c.param, gain) if gain else None
            groups += turn_groups(u[:, b, at:at + tiles * P], tiles, t, col, 3 * b + need, t0, block_cut(b))
    st += [Turn(c, segments, groups), Lambda(c),
           Select(c, lambda h: half(t[:, 8:12, :], h), lambda h: t[(h % 2) * DH:(h % 2 + 1) * DH, 12, :],
                  lambda b: u[:, b, 3712:3720])]
    units = []
    for b in range(NB):
        nk, parts = (b + 1) * P, [P] * (b + 1)
        keys, qs = slice(0, nk), block_cut(b)
        for pair in ((0, 2), (1, 3), (4, 6), (5, 7)):
            at, heads = 2 * len(units), slice(pair[0], pair[1] + 1, 2)
            dst = c.o[:, b, 0:HALF].rearrange("p (h d) -> p h d", d=DH)[:, heads, :]
            v = [[u[:, k, 2560 + h * DH:2560 + (h + 1) * DH] for k in range(b + 1)] for h in pair]
            units.append(Unit([half(t, h, qs) for h in pair], [half(t[:, 4:8, :], h, keys) for h in pair], v, parts,
                              DH ** -0.5, DH, scaled(c, dst), slice(at, at + 2), c.bias[:, heads, S - nk:S],
                              extra=c.taken[:, b, 0:nk].unsqueeze(1).to_broadcast([P, 2, nk])))
        for pair in ((0, 1), (2, 3)):
            for part in range(2):
                at, heads = 2 * len(units), slice(pair[0], pair[0] + 2)
                rows = slice(part * DH, (part + 1) * DH)
                dst = c.o[:, b, HALF:D].rearrange("p (h d) -> p h d", d=P)[:, heads, :]
                v = [[u[:, k, 3072 + h * P:3072 + (h + 1) * P] for k in range(b + 1)] for h in pair]
                fin = scaled(c, dst, c.small[:, 140:142], add=True) if part else scaled(c, dst)
                units.append(Unit([t[rows, 13 + h, qs] for h in pair], [t[rows, 17 + h, keys] for h in pair], v, parts,
                                  DH ** -0.5, P, fin, slice(at, at + 2), c.bias[:, slice(8 + pair[0], 10 + pair[0]), S - nk:S]))
    st.append(Attention(c, units))
    norms = [(c.o[:, b, HALF:D].rearrange("p (h d) -> p h d", d=P), None, None, 1.0 - LAMBDA_INIT) for b in range(NB)]
    st.append(out_turn(c, 8, PARAM(c.param, "subln"), norms))
    return st


def odd_mixer(c, dram):
    x, u, t, m = (c.xh, c.xl), c.u, c.t, c.plan["odd"]
    st = [Project(c, x, [(m, n * KT, range(KT), HALF, [u[:, b, n * HALF:(n + 1) * HALF] for b in range(NB)])
                         for n in range(6)], source=Source(c, c.h, x, gain="l1_mix", norm=True), scale=True)]
    segments, groups = [], []
    for b in range(NB):
        for n, gain in enumerate(("c_q", "c_k")):
            rows = u[:, b, n * D:(n + 1) * D]
            segments.append((rows.rearrange("p (h d) -> p h d", d=DH), None, None, 1.0))
            groups += turn_groups(rows, 8, t, PARAM(c.param, gain), 2 * b + n + 1, 8 * n, block_cut(b))
    st += [Turn(c, segments, groups), MaskBand(c)]
    units = []
    for b in range(NB):
        nk, parts = (b + 1) * P, [P] * (b + 1)
        keys, qs = slice(0, nk), block_cut(b)
        for q in range(4):
            for r in range(2):
                pair = (4 * q + r, 4 * q + r + 2)
                at, heads = 2 * len(units), slice(pair[0], pair[1] + 1, 2)
                dst = c.o[:, b, :].rearrange("p (h d) -> p h d", d=DH)[:, heads, :]
                v = [[u[:, k, 2 * D + h * DH:2 * D + (h + 1) * DH] for k in range(b + 1)] for h in pair]
                units.append(Unit([half(t, h, qs) for h in pair], [half(t[:, 8:16, :], h, keys) for h in pair], v,
                                  parts, DH ** -0.5, DH, scaled(c, dst), slice(at, at + 2), c.bias[:, heads, S - nk:S]))
    st.append(Attention(c, units))
    return st


def stages_of(c, dram, out):
    x, turned = (c.xh, c.xl), (c.oh, c.ol)
    mem = dram["mem"].rearrange("(b p) d -> p b d", p=P)
    rows = lambda gain: Source(c, c.h, x, gain=gain, norm=True)
    st = [Setup(c, dram)]
    st += first_mixer(c, dram)
    st += [Ffn(c, "up", "down", rows("ffn_pre"), gain=c.gain[:, 1, :], conv=True,
               loads=Loads((c.bias[:, 0:12, :], toeplitz(dram["t5_wide"], 12))))]
    for layer in range(2):
        l = f"l{layer}"
        st.append(Ffn(c, f"up1_{layer}", f"down1_{layer}", rows(l + "_ffn1"), factor=0.5))
        if layer == 0:
            st += even_mixer(c, dram)
            st.append(Residual(c, "even_out", turned, KT, loads=Loads((c.u[:, :, 2048:3072], mem))))
        else:
            st += odd_mixer(c, dram)
            st.append(Residual(c, "odd_out", turned, KT, loads=Loads((c.u[:, :, 2048:3072], mem)),
                               source=Source(c, c.o, turned, base=0)))
        st += memory_stages(c, layer)
        after = [(c.bias[:, 0:16, :], toeplitz(dram["band_wide"], 16))] if layer == 0 else []
        st.append(Ffn(c, f"up2_{layer}", f"down2_{layer}", rows(l + "_ffn2"), factor=0.5, loads=Loads(*after)))
    st.append(Store(c, out.rearrange("a (b p) d -> p (a b) d", p=P)))
    return st


STOP = None


def program(nc, dram, out):
    core = Core(nc, dram["stream"])
    stages = stages_of(core, dram, out)
    if STOP is not None:
        stages = stages[:STOP] + stages[-1:]
    numbers = [sorted(x.num for x in s.values()) for s in core.sets]

    def meet(engine, n):
        engine.drain().then_inc(core.stage_done, 1)
        engine.wait_ge(core.stage_done, 4 * (n + 1))
        engine.nop(nofuse=True)

    with nc.Block() as block:

        @block.tensor
        def _(pe):
            for n, stage in enumerate(stages):
                stage.tensor(pe, core.sets[n % 2])
                meet(pe, n)

        @block.scalar
        def _(act):
            for n, stage in enumerate(stages):
                stage.scalar(act, core.sets[n % 2])
                meet(act, n)

        @block.vector
        def _(dve):
            for n, stage in enumerate(stages):
                stage.vector(dve, core.sets[n % 2])
                meet(dve, n)

        @block.gpsimd
        def _(pool):
            for n, stage in enumerate(stages):
                if n:
                    other = numbers[(n + 1) % 2]
                    pool.sem_clear(range(other[0], other[-1] + 1))
                stage.gpsimd(pool, core.sets[n % 2])
                meet(pool, n)

        @block.sync
        def _(sp):
            for n in range(core.act_next):
                if n >= RING:
                    sp.wait_ge(core.slot_used, n - RING + 1)
                sp.dma_start(core.raw[:, n % RING, :], core.stream[n]).then_inc(core.slot_loaded[n % RING], 16)


def kernel(**inputs):
    from concourse import bacc
    from concourse.bass_utils import run_bass_kernel_spmd as run

    x = {k: np.ascontiguousarray(v) for k, v in inputs.items()}
    nc = bacc.Bacc("TRN2", target_bir_lowering=False, num_devices=1)
    arrays = {
        "stream": pack_stream(x), "param": pack_params(x), "rows": pack_rows(x), "band_rows": pack_band_bias(x),
        "const": constants(), "table": tables(), "x": x["x"][0], "mem": x["mem_2"][0],
    }
    arrays = {k: np.ascontiguousarray(v) for k, v in arrays.items()}
    dram = {k: nc.dram_tensor(k + "_dram", v.shape, F32, kind="ExternalInput").ap() for k, v in arrays.items()}
    for name, heads in (("rel_rows", 10), ("t5_rows", 12)):
        dram[name] = nc.dram_tensor(name + "_dram", (heads, TOE), F32, kind="Internal").ap()
    for name, heads in (("rel_wide", 10), ("t5_wide", 12), ("band_wide", 16)):
        dram[name] = nc.dram_tensor(name + "_dram", (heads, P, TOE), F32, kind="Internal").ap()
    out = nc.dram_tensor("out_dram", (1, S, D), F32, kind="ExternalOutput").ap()
    program(nc, dram, out)
    r = run(nc, [{k + "_dram": v for k, v in arrays.items()}], core_ids=[0])
    return r.results[0]["out_dram"]
```

```python
import math

import numpy as np

import concourse.bass as bass
from concourse import mybir

F32 = mybir.dt.float32
F32R = mybir.dt.float32r
ACT = mybir.ActivationFunctionType
ALU = mybir.AluOpType
AX = mybir.AxisListType

P = 128
S = 256
NB = S // P
D = 1024
KT = D // P
DH = 64
FF = 2816
FT = FF // P
EPS = 1e-6
NEG = -1e30
TAKEN = -3e38
HALF = 512

SLOT = 2048
RING = 4
LEAD = 2
TOE = 384
TOP_K = S // 4



def rel_bucket(dist):
    dist = np.maximum(dist, 0)
    d = np.maximum(dist, 1).astype(np.float32)
    large = 16 + (np.log(d / np.float32(16)) / np.float32(math.log(128)) * np.float32(16)).astype(np.int32)
    return np.where(dist < 16, dist, np.minimum(large, 31))


def t5_bucket(rel):
    off = (rel < 0).astype(np.int32) * 16
    n = np.abs(rel)
    nf = np.maximum(n, 1).astype(np.float32)
    large = 8 + (np.log(nf / np.float32(8)) / np.float32(math.log(16)) * np.float32(8)).astype(np.int32)
    return off + np.where(n < 8, n, np.minimum(large, 15))


class Columns:

    def __init__(self, **widths):
        self.at, self.n = {}, 0
        for name, w in widths.items():
            self.at[name] = (self.n, w)
            self.n += w

    def __call__(self, tile, name):
        a, w = self.at[name]
        return tile[:, a:a + w]


CONST = Columns(ident=P, upto=P, ones=P, causal=S, cmp_mask=30, cmp_valid=2, cos=2 * 16, sin=2 * 16)
TABLE = Columns(hot_rel=TOE, hot_t5=TOE, rel_mask=TOE)
PARAM = Columns(mla_q=2, mla_kv=1, a_q=1, a_k=1, idx_k=1, b_q=1, b_k=1, subln=1, c_q=1, c_k=1,
                mq0=1, mk0=1, mq1=1, mk1=1, conv_w=3 * 2 * FT, conv_b=2 * FT, cmp_pos=32,
                gains=14 * KT, w2k=P, w2v=DH, lam=4 * DH, f_bias=4, rel=10, t5=12)
ROWS = ["attn_pre", "ffn_pre", "attn_post", "ffn_post", "l0_ffn1", "l0_mix", "l0_src", "l0_mem", "l0_ffn2",
        "l1_ffn1", "l1_mix", "l1_src", "l1_mem", "l1_ffn2"]


def constants():
    c = np.zeros((P, CONST.n), np.float32)
    p = np.arange(P)
    CONST(c, "ident")[:] = np.eye(P)
    CONST(c, "upto")[:] = p[:, None] <= p[None, :]
    CONST(c, "ones")[:] = 1
    k = np.arange(S)
    CONST(c, "causal")[:] = np.where(P + p[:, None] - k[None, :] >= 0, 0, NEG)
    end = np.arange(15) * 16 + 31
    for b in range(NB):
        t = b * P + p
        CONST(c, "cmp_mask")[:, 15 * b:15 * b + 15] = np.where(end[None, :] <= t[:, None], 0, NEG)
        CONST(c, "cmp_valid")[:, b] = t >= end[0]
        freq = (np.float32(10000.0) ** (-np.arange(0, 32, 2, dtype=np.float32) / np.float32(32))).astype(np.float32)
        angle = t.astype(np.float32)[:, None] * freq[None, :]
        CONST(c, "cos")[:, 16 * b:16 * b + 16] = np.cos(angle)
        CONST(c, "sin")[:, 16 * b:16 * b + 16] = np.sin(angle)
    return c


def tables():
    t = np.zeros((P, TABLE.n), np.float32)
    j = np.arange(TOE)
    dist = 255 - j
    for name, bucket in (("hot_rel", rel_bucket(dist)), ("hot_t5", t5_bucket(dist))):
        TABLE(t, name)[bucket, j] = 1
    for h in range(10):
        ok = dist >= 0
        if h >= 4:
            window, dilation = ((128, 1), (512, 4), (2048, 16))[(h - 4) // 2]
            ok = ok & (dist <= window) & (dist % dilation == 0)
        TABLE(t, "rel_mask")[h] = np.where(ok, 0, NEG)
    return t



class Matrix:

    def __init__(self, first, count, width):
        self.first, self.count, self.width = first, count, width
        self.per = SLOT // width
        self.slots = -(-count // self.per)

    def slot(self, i):
        return self.first + i // self.per

    def offset(self, i):
        return i % self.per * self.width

    def ends_slot(self, i):
        return i == self.count - 1 or i % self.per == self.per - 1


def by_chunk(w, width, chunks=None):
    k = w.shape[0] // P
    return [w[t * P:(t + 1) * P, c * width:(c + 1) * width]
            for c in range(chunks or -(-w.shape[1] // width)) for t in range(k)]


def by_tile(w, width):
    return [w[t * P:(t + 1) * P, c * width:(c + 1) * width]
            for t in range(w.shape[0] // P) for c in range(w.shape[1] // width)]


def first_in_columns():
    h64 = lambda base, i: list(range(base + 64 * i, base + 64 * i + 64))
    a_q, kv, b, c = 0, 256, 652, 1804
    tiles = []
    for t in range(2):
        tiles += h64(a_q, 2 * t) + h64(a_q, 2 * t + 1)
    tiles += h64(kv, 2) * 2 + h64(kv, 4) * 2 + h64(kv, 0) + h64(kv, 1)
    for base in (b, b + 384):
        for t in range(3):
            tiles += h64(base, 2 * t) + h64(base, 2 * t + 1)
    for base in (c, c + 256):
        for t in range(2):
            tiles += h64(base, 2 * t) + h64(base, 2 * t + 1)
    rows = (h64(kv, 3) + h64(kv, 5) + list(range(640, 652)) + list(range(b + 768, b + 1152))
            + list(range(c + 512, c + 768)) + list(range(2572, 2576)) + list(range(2576, 2992)))
    return tiles, rows


def even_in_columns():
    r = lambda a, n: list(range(a, a + n))
    main = r(0, 512) + r(512, 512) + r(1536, 512) + r(2120, 512) + r(2632, 512) + r(1024, 512) + r(3144, 512)
    return main, r(2048, 64) * 2 + r(2112, 8)


def stream_plan():
    plan = [("in_t", 15 * KT, P), ("in_n", 3 * KT, HALF), ("mla", 3, HALF), ("phi", 32, P)]
    for i in range(4):
        plan += [(f"gate{i}", 2 * KT, HALF), (f"branch{i}", 2 if i == 1 else 4, HALF)]
    plan += [("w_o", 2 * KT, HALF), ("up", FT * 2 * KT, P), ("down", 2 * FT, HALF)]
    for layer in range(2):
        plan += [(f"up1_{layer}", FT * 2 * KT, P), (f"down1_{layer}", 2 * FT, HALF)]
        if layer == 0:
            plan += [("even_tail", KT, S), ("even", 7 * KT, HALF), ("even_out", 2 * KT, HALF)]
        else:
            plan += [("odd", 6 * KT, HALF), ("odd_out", 2 * KT, HALF)]
        plan += [(f"wq{layer}", KT, HALF), (f"wkv{layer}", 2 * KT, HALF), (f"wo{layer}", 8, HALF)]
        plan += [(f"up2_{layer}", FT * 2 * KT, P), (f"down2_{layer}", 2 * FT, HALF)]
    out, first = {}, 0
    for name, count, width in plan:
        out[name] = Matrix(first, count, width)
        first += out[name].slots
    return out, first


def pack_stream(x):
    plan, slots = stream_plan()
    out = np.zeros((slots, P, SLOT), np.float32)

    def pairs(g, u):
        g, u = by_chunk(g, P), by_chunk(u, P)
        return [piece for f in range(FT) for piece in g[f * KT:(f + 1) * KT] + u[f * KT:(f + 1) * KT]]

    w_in = x["w_in"][0]
    tiles, rows = first_in_columns()
    pieces = {"in_t": by_chunk(w_in[:, tiles], P), "in_n": by_chunk(w_in[:, rows], HALF)}
    pieces["in_n"] = pieces["in_n"][KT:] + pieces["in_n"][:KT]
    w1 = [x[n][0].reshape(32, DH, P) for n in ("nsa_phi_k_w1", "nsa_phi_v_w1")]
    pieces["phi"] = [np.concatenate([w[i] for w in w1], 0) for i in range(32)]
    pieces["mla"] = by_chunk(x["mla_w_uq"][0], HALF) + by_chunk(x["mla_w_ukv"][0], HALF)
    for i, n in enumerate("abcd"):
        pieces[f"branch{i}"] = by_chunk(x["w_branch_" + n][0], HALF)
        pieces[f"gate{i}"] = by_chunk(x["w_merge_gate"][0, i], HALF)
    pieces["w_o"] = by_tile(x["w_o"][0], HALF)
    up = x["ffn_w_up"][0]
    pieces["up"] = pairs(up[:, :FF], up[:, FF:])
    pieces["down"] = by_tile(x["ffn_w_down"][0], HALF)
    for layer in range(2):
        g = lambda n: x[f"l{layer}_{n}_2"]
        for n in (1, 2):
            pieces[f"up{n}_{layer}"] = pairs(g(f"ffn{n}_wg"), g(f"ffn{n}_wu"))
            pieces[f"down{n}_{layer}"] = by_tile(g(f"ffn{n}_wd"), HALF)
        pieces[f"wkv{layer}"] = by_chunk(g("mem_wkv"), HALF)
        pieces[f"wq{layer}"] = by_chunk(g("mem_wq"), HALF)
        pieces[f"wo{layer}"] = by_tile(g("mem_wo"), HALF)
        if layer == 0:
            main, tail = even_in_columns()
            pieces["even"] = by_chunk(g("w_in")[:, main], HALF)
            pieces["even_tail"] = by_chunk(g("w_in")[:, tail], S)
            pieces["even_out"] = by_tile(g("w_out"), HALF)
        else:
            pieces["odd"] = by_chunk(g("w_in"), HALF)
            pieces["odd_out"] = by_tile(g("w_out"), HALF)
    for name, m in plan.items():
        assert len(pieces[name]) == m.count, name
        for i, piece in enumerate(pieces[name]):
            at = m.offset(i)
            out[m.slot(i), :, at:at + piece.shape[1]] = piece
    return out


def pack_params(x):
    a = np.zeros((P, PARAM.n), np.float32)
    put = lambda n, v: PARAM(a, n).__setitem__(slice(None), v)
    twice = lambda v: np.concatenate([v, v])[:, None]
    put("mla_q", x["mla_q_norm"][0].reshape(2, P).T)
    put("mla_kv", x["mla_kv_norm"][0][:, None])
    for n, k in (("a_q", "l0_a_q_norm_2"), ("a_k", "l0_a_k_norm_2"), ("idx_k", "l0_idx_k_norm_2"),
                 ("b_q", "l0_b_q_norm_2"), ("b_k", "l0_b_k_norm_2"), ("c_q", "l1_c_q_norm_2"), ("c_k", "l1_c_k_norm_2")):
        put(n, twice(x[k]))
    put("subln", x["l0_b_subln_2"][:, None])
    for layer in range(2):
        put(f"mq{layer}", x[f"l{layer}_mem_q_norm_2"][:, None])
        put(f"mk{layer}", x[f"l{layer}_mem_k_norm_2"][:, None])
    put("conv_w", x["ffn_conv_w"][0].reshape(3 * 2 * FT, P).T)
    put("conv_b", x["ffn_conv_b"][0].reshape(2 * FT, P).T)
    put("gains", pack_rows(x).reshape(len(ROWS) * KT, P).T)
    pos = x["nsa_cmp_pos"][0].T
    put("cmp_pos", np.concatenate([pos, pos], 0))
    put("w2k", np.concatenate([x["nsa_phi_k_w2"][0]] * 2, 1))
    put("w2v", x["nsa_phi_v_w2"][0])
    put("lam", np.concatenate([x[f"l0_b_{n}_2"] for n in ("lq1", "lk1", "lq2", "lk2")])[None, :])
    put("f_bias", x["fox_forget_bias"][0][None, :])
    PARAM(a, "rel")[:32] = x["rel_bias_table"]
    PARAM(a, "t5")[:32] = x["t5_bias_2"]
    return a


def pack_rows(x):
    first = [x[n][0] for n in ("norm_attn_pre", "norm_ffn_pre", "norm_attn_post", "norm_ffn_post")]
    rest = [x[f"l{layer}_{n}_2"] for layer in range(2)
            for n in ("ffn1_norm", "mix_norm", "mem_src_norm", "mem_norm", "ffn2_norm")]
    return np.stack(first + rest)


def pack_band_bias(x):
    table = x["l1_c_rel_bias_2"]
    return np.ascontiguousarray(table[511 - np.arange(TOE)].T)



NAMES = ["squares_ready", "sums_ready", "means_ready", "roots_ready", "rows_scaled", "tiles_turned",
         "turned_by_act", "turned_by_dve", "highs_ready", "banks_filled", "drained_by_act", "drained_by_dve",
         "gates_ready", "hidden_ready", "convolved", "scores_ready", "logits_ready", "probs_ready",
         "probs_turned", "probs_copied", "out_ready", "out_taken", "inputs_ready", "partial_ready",
         "act_step", "dve_step", "sum_step", "rows_turned", "high_turned", "low_turned", "norm_squares",
         "norm_means", "norm_roots", "inverse_ready", "wide_ready", "wide_turned", "row_ready", "scaled_ready"]


class Steps:

    def __init__(self, engine, sem):
        self.engine, self.sem, self.n = engine, sem, 0

    def __call__(self, instruction):
        self.n += 1
        instruction.then_inc(self.sem, 1)
        self.engine.wait_ge(self.sem, self.n)


class Core:

    def __init__(self, nc, stream):
        self.nc = nc
        self.plan, self.slots = stream_plan()
        self.stream = stream
        phi = self.plan["phi"]
        self.unsplit = range(phi.first, phi.first + phi.slots)
        self.top = -(-nc.sbuf_base // 64) * 64
        self.limit = nc.sbuf_usable_end
        t = self.tile
        raw_at = self.top
        self.raw = t("raw", [P, RING, SLOT])
        self.low = self.over("low", [P, RING, SLOT], F32R, raw_at)
        self.high = t("high", [P, RING, SLOT], F32R)
        self.h = t("h", [P, NB, D])
        self.xh = t("xh", [P, KT, S], F32R)
        self.xl = t("xl", [P, KT, S], F32R)
        arena = self.top
        self.u = t("u", [P, NB, 3720])
        self.o = t("o", [P, NB, D])
        self.small_rows = self.over("small_rows", [P, 2, TOE], F32, self.top - NB * D * 4)
        self.top = max(self.top, arena + 2 * FT * S * 4)
        self.hh = self.over("hh", [P, FT, S], F32R, arena)
        self.hl = self.over("hl", [P, FT, S], F32R, arena + FT * S * 4)
        turned = self.top
        self.t = t("t", [P, 23, S])
        self.oh = self.over("oh", [P, KT, S], F32R, turned)
        self.ol = self.over("ol", [P, KT, S], F32R, turned + KT * S * 4)
        xn = self.xn_at = self.top
        self.xn = t("xn", [P, NB, D])
        self.latent_h = self.over("latent_h", [P, 3, S], F32R, xn)
        self.latent_l = self.over("latent_l", [P, 3, S], F32R, xn + 3 * S * 4)
        self.forget = self.over("forget", [P, NB, 4, S], F32, xn)
        self.taken = self.over("taken", [P, NB, S], F32, xn)
        work = self.top
        self.prob = t("prob", [P, 4, 2, S])
        self.prob_t = t("prob_t", [P, 2, 4, P])
        self.square = self.over("square", [P, 3, D], F32, work)
        self.bias = t("bias", [P, 16, S])
        self.gain = t("gain", [P, 2, D])
        self.inv = t("inv", [P, 8])
        self.inv_wide = self.xn[:, 0, 0:S].rearrange("p (b q) -> p b q", b=NB)
        self.inv_row = t("inv_row", [P, S])
        self.const = t("const", [P, CONST.n])
        self.param = t("param", [P, PARAM.n])
        self.stat = t("stat", [P, 80])
        self.nmax = t("nmax", [P, 64])
        self.den = t("den", [P, 64])
        self.rden = t("rden", [P, 64])
        self.small = t("small", [P, 148])
        self.ident = CONST(self.const, "ident")
        self.products = self.u[:, 1, 2600:3368].rearrange("p (b g h d) -> p b g h d", b=NB, g=3, h=2)
        self.bank = [nc.alloc_psum_tensor(f"bank{i}", [P, HALF], F32) for i in range(8)]
        sem = nc.alloc_semaphore
        self.slot_loaded = [sem(f"slot_loaded{i}") for i in range(RING)]
        self.high_split, self.low_split, self.slot_used = sem("high_split"), sem("low_split"), sem("slot_used")
        self.stage_done, self.loaded, self.stored = sem("stage_done"), sem("loaded"), sem("stored")
        self.bounced, self.first_loaded = sem("bounced"), sem("first_loaded")
        self.sets = [{n: sem(f"{n}_{'even' if i == 0 else 'odd'}") for n in NAMES} for i in range(2)]
        self.act_next = self.dve_next = 0
        self.loads = 0

    def tile(self, name, shape, dtype=F32):
        size = int(np.prod(shape[1:])) * 4
        out = self.nc.alloc_sbuf_tensor_at(name, shape, dtype, offset=self.top)
        self.top += -(-size // 64) * 64
        assert self.top <= self.limit, (name, self.top, self.limit)
        return out

    def over(self, name, shape, dtype, at):
        return self.nc.alloc_sbuf_tensor_at(name, shape, dtype, offset=at)

    def split_high(self, act, last):
        for n in range(self.act_next, min(last + LEAD, self.slots - 1) + 1):
            act.wait_ge(self.slot_loaded[n % RING], 16 * (n // RING + 1))
            act.activation(self.high[:, n % RING, :], self.raw[:, n % RING, :], ACT.Copy).then_inc(self.high_split, 1)
            self.act_next = n + 1

    def split_low(self, dve, last):
        for n in range(self.dve_next, min(last + LEAD, self.slots - 1) + 1):
            dve.wait_ge(self.high_split, n + 1)
            if n in self.unsplit:
                dve.drain().then_inc(self.low_split, 1)
                self.dve_next = n + 1
                continue
            dve.tensor_tensor(self.low[:, n % RING, :], self.raw[:, n % RING, :],
                              self.high[:, n % RING, :].bitcast(F32), ALU.subtract).then_inc(self.low_split, 1)
            self.dve_next = n + 1

    def piece(self, pe, m, i, width=None):
        if i % m.per == 0:
            pe.wait_ge(self.low_split, m.slot(i) + 1)
        at, r = m.offset(i), m.slot(i) % RING
        cut = slice(at, at + (width or m.width))
        return self.high[:, r, cut], self.low[:, r, cut]

    def release(self, instruction, m, i):
        if m.ends_slot(i):
            instruction.then_inc(self.slot_used, 1)

    def finish_output(self, instruction, m, i, s):
        instruction.then_inc(self.slot_used if m.ends_slot(i) else s["banks_filled"], 1)

    def wait_output(self, engine, m, i, s, others):
        if m.ends_slot(i):
            engine.wait_ge(self.slot_used, m.slot(i) + 1)
        else:
            engine.wait_ge(s["banks_filled"], others)


def mm3(pe, out, left, right, start, stop):
    (lh, ll), (rh, rl) = left, right
    pe.matmul(out, lh, rh, start=start, stop=False)
    pe.matmul(out, lh, rl, start=False, stop=False)
    return pe.matmul(out, ll, rh, start=False, stop=stop)


def mm(pe, out, left, right, start, stop):
    return pe.matmul(out, left, right, start=start, stop=stop)


def keep_clock(pe, core, n):
    for _ in range(n):
        pe.matmul(core.bank[7][:, 0:S], core.xh[:, 0, 0:P], core.xh[:, 0, :], start=True, stop=True)


class Stage:
    def __init__(self, core):
        self.core = core

    def tensor(self, pe, s):
        pass

    def scalar(self, act, s):
        pass

    def vector(self, dve, s):
        pass

    def gpsimd(self, pool, s):
        pass


class Setup(Stage):

    def __init__(self, core, dram):
        super().__init__(core)
        self.dram = dram
        self.table = core.u[:, 0, 0:TABLE.n]

    def loads(self):
        c, dram = self.core, self.dram
        return [(c.const[:, :], dram["const"]), (c.param[:, :], dram["param"]), (self.table, dram["table"]),
                (c.h[:, :, :], dram["x"].rearrange("(b p) d -> p b d", p=P))]

    def tensor(self, pe, s):
        c = self.core
        pe.wait_ge(c.first_loaded, 16 * len(self.loads()))
        mm(pe, c.bank[0][0:10, 0:TOE], PARAM(c.param, "rel")[0:32], TABLE(self.table, "hot_rel")[0:32],
           True, True).then_inc(s["out_ready"], 1)
        mm(pe, c.bank[1][0:12, 0:TOE], PARAM(c.param, "t5")[0:32], TABLE(self.table, "hot_t5")[0:32],
           True, True).then_inc(s["out_ready"], 1)

    def scalar(self, act, s):
        self.core.split_high(act, 0)

    def vector(self, dve, s):
        c = self.core
        c.split_low(dve, 0)
        dve.wait_ge(s["out_ready"], 2)
        dve.tensor_tensor(c.small_rows[0:10, 0, :], c.bank[0][0:10, 0:TOE], TABLE(self.table, "rel_mask")[0:10],
                          ALU.add).then_inc(s["out_taken"], 1)
        dve.tensor_copy(c.small_rows[0:12, 1, :], c.bank[1][0:12, 0:TOE]).then_inc(s["out_taken"], 1)


class Loads:

    def __init__(self, *pairs):
        self.pairs = pairs

    def start(self, core, pool):
        for dst, src in self.pairs:
            pool.dma_start(dst, src).then_inc(core.loaded, 16)
            core.loads += 1

    def finish(self, core, pool):
        pool.wait_ge(core.loaded, 16 * core.loads)


def spread(rows, wide):
    heads = rows.shape[0]
    return wide[0:heads], bass.AP(tensor=rows.tensor, offset=rows.offset, ap=[[TOE, heads], [0, P], [1, TOE]])


def toeplitz(wide, heads):
    return bass.AP(tensor=wide.tensor, offset=wide.offset + P - 1, ap=[[TOE - 1, P], [P * TOE, heads], [1, S]])


class Turn(Stage):

    def __init__(self, core, batches, base=0):
        super().__init__(core)
        self.base, self.batches = base, []
        cols = seg = group = 0
        for batch in batches:
            segments, groups = batch or ((), ())
            first = cols
            entries = []
            for src, factor in segments:
                entries.append((seg, src, factor, slice(cols, cols + src.shape[1])))
                cols += src.shape[1]
                seg += 1
            before = seg - len(entries)
            turned = [(group + i, before + g[0] if g[0] else 0, *g[1:]) for i, g in enumerate(groups)]
            group += len(turned)
            self.batches.append((entries, turned, slice(first, cols)))
        assert cols <= 80
        self.by = [("act", "dve") if kind == "pair" else (("act",) if g % 2 == 0 else ("dve",))
                   for _, groups, _ in self.batches for g, _, _, _, kind, _, _ in groups]
        self.roots = [sum(bool(e) for e, _, _ in self.batches[:n + 1]) for n in range(len(self.batches))]

    def drained(self, engine, g):
        return sum(engine in b for b in self.by[:g + 1])

    def bank(self, g):
        return self.core.bank[self.base + g % 4]

    def turn_rows(self, pe, s, n):
        for g, need, sources, width, kind, dst, gain in self.batches[n][1]:
            if need:
                pe.wait_ge(s["rows_scaled"], need)
            if g >= 4:
                if self.drained("act", g - 4):
                    pe.wait_ge(s["turned_by_act"], self.drained("act", g - 4))
                if self.drained("dve", g - 4):
                    pe.wait_ge(s["turned_by_dve"], self.drained("dve", g - 4))
            for j, src in enumerate(sources):
                last = pe.transpose(self.bank(g)[0:width, j * P:(j + 1) * P], src, self.core.ident)
            last.then_inc(s["tiles_turned"], 1)

    def square_rows(self, act, s, n):
        c = self.core
        segments, _, cols = self.batches[n]
        for i, src, factor, at in segments:
            if i >= 3:
                act.wait_ge(s["sums_ready"], i - 2)
            h, w = src.shape[1], src.shape[2]
            sq = c.square[:, i % 3, 0:h * w].rearrange("p (h w) -> p h w", w=w)
            act.activation(sq, src, ACT.Square).then_inc(s["squares_ready"], 1)
        if segments:
            act.wait_ge(s["means_ready"], self.roots[n])
            act.activation(c.stat[:, cols], c.stat[:, cols], ACT.Sqrt).then_inc(s["roots_ready"], 1)

    def copy_high(self, act, s, n):
        for g, need, sources, width, kind, dst, gain in self.batches[n][1]:
            if "act" not in self.by[g]:
                continue
            act.wait_ge(s["tiles_turned"], g + 1)
            ps = self.bank(g)[0:width, 0:len(sources) * P].rearrange("p (n q) -> p n q", q=P)
            out = dst[0] if kind == "pair" else dst
            if gain is None:
                i = act.activation(out, ps, ACT.Copy)
            else:
                i = act.activation(out, ps, ACT.Copy, scale=gain)
            i.then_inc(s["turned_by_act"], 1)

    def scale_rows(self, dve, s, n, step):
        c = self.core
        segments, _, cols = self.batches[n]
        for i, src, factor, at in segments:
            h, w = src.shape[1], src.shape[2]
            dve.wait_ge(s["squares_ready"], i + 1)
            sq = c.square[:, i % 3, 0:h * w].rearrange("p (h w) -> p h w", w=w)
            dve.tensor_reduce(c.stat[:, at], sq, AX.X, ALU.add).then_inc(s["sums_ready"], 1)
        if segments:
            dve.wait_ge(s["sums_ready"], segments[-1][0] + 1)
        for i, src, factor, at in segments:
            w, f2 = src.shape[2], factor * factor
            m = dve.tensor_scalar(c.stat[:, at], c.stat[:, at], 1.0 / (w * f2), EPS / f2, ALU.mult, ALU.add)
            if i == segments[-1][0]:
                m.then_inc(s["means_ready"], 1)
        if segments:
            dve.wait_ge(s["roots_ready"], self.roots[n])
            step(dve.reciprocal(c.stat[:, cols], c.stat[:, cols]))
        for i, src, factor, at in segments:
            h, w = src.shape[1], src.shape[2]
            if h == 1:
                m = dve.tensor_scalar(src[:, 0, :], src[:, 0, :], c.stat[:, at], None, ALU.mult)
            else:
                m = dve.tensor_tensor(src, src, c.stat[:, at].unsqueeze(2).to_broadcast([P, h, w]), ALU.mult)
            m.then_inc(s["rows_scaled"], 1)

    def copy_low(self, dve, s, n):
        for g, need, sources, width, kind, dst, gain in self.batches[n][1]:
            if "dve" not in self.by[g]:
                continue
            ps = self.bank(g)[0:width, 0:len(sources) * P].rearrange("p (n q) -> p n q", q=P)
            dve.wait_ge(s["tiles_turned"], g + 1)
            if kind == "pair":
                dve.wait_ge(s["turned_by_act"], self.drained("act", g))
                hi = dst[0].bitcast(F32)
                if gain is None:
                    i = dve.tensor_tensor(dst[1], ps, hi, ALU.subtract)
                else:
                    i = dve.scalar_tensor_tensor(dst[1], ps, gain, hi, ALU.mult, ALU.subtract)
            elif gain is None:
                i = dve.tensor_copy(dst, ps)
            else:
                i = dve.tensor_scalar(dst, ps, gain, None, ALU.mult)
            i.then_inc(s["turned_by_dve"], 1)

    def tensor(self, pe, s):
        for n in range(len(self.batches)):
            self.turn_rows(pe, s, n)

    def scalar(self, act, s):
        for n in range(len(self.batches)):
            self.square_rows(act, s, n)
            self.copy_high(act, s, n)

    def vector(self, dve, s):
        step = Steps(dve, s["dve_step"])
        for n in range(len(self.batches)):
            self.scale_rows(dve, s, n, step)
            self.copy_low(dve, s, n)


class Source:

    def __init__(self, core, rows, dst, tiles=KT, gain=None, norm=False, base=2):
        self.core, self.rows, self.dst, self.tiles, self.norm = core, rows, dst, tiles, norm
        self.banks = {0: (0, 1, 2, 3), 4: (4, 5, 6, 7), 2: (4, 5, 6, 7, 2, 3)}[base]
        n = ROWS.index(gain) * KT if gain else None
        self.gain = PARAM(core.param, "gains")[:, n:n + KT] if gain else None

    def bank(self, k):
        return self.core.bank[self.banks[k % len(self.banks)]][:, 0:S]

    def tensor(self, pe, s, first=0, end=KT):
        for k in range(first, min(end, self.tiles)):
            if k >= len(self.banks):
                pe.wait_ge(s["low_turned"], k - len(self.banks) + 1)
            for b in range(NB):
                last = pe.transpose(self.bank(k)[:, b * P:(b + 1) * P], self.rows[:, b, k * P:(k + 1) * P],
                                    self.core.ident)
            last.then_inc(s["rows_turned"], 1)

    def arrive(self, pe, s, k):
        pe.wait_ge(s["low_turned"], k + 1)

    def row(self, pe, s):
        if not self.norm:
            return
        c = self.core
        pe.wait_ge(s["low_turned"], self.tiles)
        pe.wait_ge(s["wide_ready"], 1)
        for b in range(NB):
            last = pe.transpose(c.bank[7][:, b * P:(b + 1) * P], c.inv_wide[:, b, :], c.ident)
        last.then_inc(s["wide_turned"], 1)

    def scalar(self, act, s, first=0, end=KT):
        c = self.core
        for k in range(first, min(end, self.tiles)):
            act.wait_ge(s["rows_turned"], k + 1)
            scale = 1.0 if self.gain is None else self.gain[:, k:k + 1]
            act.activation(self.dst[0][:, k, :], self.bank(k), ACT.Copy, scale=scale).then_inc(s["high_turned"], 1)
        if not self.norm:
            return
        for b in range(NB):
            act.activation(c.xn[:, b, :], self.rows[:, b, :], ACT.Square, accum_out=c.inv[:, b:b + 1])\
               .then_inc(s["norm_squares"], 1)
        act.wait_ge(s["norm_means"], 1)
        act.activation(c.inv[:, 0:2], c.inv[:, 0:2], ACT.Sqrt).then_inc(s["norm_roots"], 1)

    def vector(self, dve, s, factor=1.0, row=False, first=0, end=KT):
        c = self.core
        for k in range(first, min(end, self.tiles)):
            dve.wait_ge(s["high_turned"], k + 1)
            high, low = self.dst[0][:, k, :].bitcast(F32), self.dst[1][:, k, :]
            if self.gain is None:
                i = dve.tensor_tensor(low, self.bank(k), high, ALU.subtract)
            else:
                i = dve.scalar_tensor_tensor(low, self.bank(k), self.gain[:, k:k + 1], high, ALU.mult, ALU.subtract)
            i.then_inc(s["low_turned"], 1)
        if not self.norm:
            return
        dve.wait_ge(s["norm_squares"], NB)
        dve.tensor_scalar(c.inv[:, 0:2], c.inv[:, 0:2], 1.0 / D, EPS, ALU.mult, ALU.add).then_inc(s["norm_means"], 1)
        dve.wait_ge(s["norm_roots"], 1)
        dve.reciprocal(c.inv[:, 2:4], c.inv[:, 0:2]).then_inc(s["inverse_ready"], 1)
        dve.wait_ge(s["inverse_ready"], 1)
        dve.tensor_scalar(c.inv[:, 4:6], c.inv[:, 2:4], factor, None, ALU.mult).then_inc(s["scaled_ready"], 1)
        if row:
            dve.tensor_copy(c.inv_wide[:, :, :], c.inv[:, 2:4].unsqueeze(2).to_broadcast([P, NB, P]))\
               .then_inc(s["wide_ready"], 1)

    def take_row(self, dve, s):
        c = self.core
        dve.wait_ge(s["wide_turned"], 1)
        dve.tensor_copy(c.inv_row[:, :], c.bank[7][:, 0:S]).then_inc(s["row_ready"], 1)
        dve.wait_ge(s["row_ready"], 1)


class ProjectTurned(Stage):

    def __init__(self, core, name, tiles, source, dram, loads):
        super().__init__(core)
        self.dram = dram
        self.m, self.tiles, self.source, self.loads = core.plan[name], tiles, source, loads
        self.last = [(t + 1) * KT - 1 for t in range(tiles)]
        self.others = [sum(not self.m.ends_slot(i) for i in self.last[:t + 1]) for t in range(tiles)]

    def gpsimd(self, pool, s):
        c = self.core
        for rows, n, heads in (("rel_rows", 0, 10), ("t5_rows", 1, 12)):
            pool.dma_start(self.dram[rows], c.small_rows[0:heads, n, :]).then_inc(c.bounced, 16)
        pool.wait_ge(c.bounced, 32)
        self.loads.start(c, pool)
        self.loads.finish(c, pool)

    def tensor(self, pe, s):
        c = self.core
        self.source.tensor(pe, s)
        for t in range(self.tiles):
            if t == 2:
                self.source.row(pe, s)
            if t >= 4:
                pe.wait_ge(s["drained_by_dve"], t - 3)
            for k in range(KT):
                if t == 0:
                    self.source.arrive(pe, s, k)
                i = t * KT + k
                last = mm3(pe, c.bank[t % 4][:, 0:S], c.piece(pe, self.m, i), (c.xh[:, k, :], c.xl[:, k, :]),
                           k == 0, k == KT - 1)
            c.finish_output(last, self.m, i, s)

    def scalar(self, act, s):
        self.source.scalar(act, s)
        self.core.split_high(act, self.m.slot(self.last[-1]))

    def vector(self, dve, s):
        c = self.core
        self.source.vector(dve, s, row=True)
        for t in range(self.tiles):
            c.split_low(dve, self.m.slot(self.last[t]))
            if t == 0:
                self.source.take_row(dve, s)
            c.wait_output(dve, self.m, self.last[t], s, self.others[t])
            dve.tensor_tensor(c.t[:, t, :], c.bank[t % 4][:, 0:S], c.inv_row[:, :], ALU.mult)\
               .then_inc(s["drained_by_dve"], 1)


class Project(Stage):

    def __init__(self, core, x, jobs, loads=None, source=None, scale=False, batches=None,
                 masked=0):
        super().__init__(core)
        self.masked = masked
        self.source, self.scale = source, scale
        self.x, self.jobs, self.loads = x, jobs, loads
        self.turn = Turn(core, batches or [None] * len(jobs), base=4)
        ends = [j[0].ends_slot(j[1] + len(j[2]) - 1) for j in jobs]
        self.others = [sum(not e for e in ends[:n + 1]) for n in range(len(jobs))]

    def gpsimd(self, pool, s):
        if self.masked:
            pool.memset(self.core.bias[0:DH, 0:self.masked, S - DH:S], NEG)
        if self.loads:
            self.loads.start(self.core, pool)
            self.loads.finish(self.core, pool)

    def rows_there(self, engine, s, n):
        engine.wait_ge(s["drained_by_act"], n + 1)
        engine.wait_ge(s["drained_by_dve"], n + 1)

    def tensor(self, pe, s):
        c = self.core
        xh, xl = self.x
        if self.source:
            self.source.tensor(pe, s)
        for n, (m, i0, kts, width, dst) in enumerate(self.jobs):
            if n >= 2:
                self.rows_there(pe, s, n - 2)
            for j, k in enumerate(kts):
                if self.source and n == 0:
                    self.source.arrive(pe, s, k)
                w = c.piece(pe, m, i0 + j, width)
                for b in range(NB):
                    cut = slice(b * P, (b + 1) * P)
                    last = mm3(pe, c.bank[2 * (n % 2) + b][:, 0:width], (xh[:, k, cut], xl[:, k, cut]), w,
                               j == 0, j == len(kts) - 1)
                if j == len(kts) - 1:
                    c.finish_output(last, m, i0 + j, s)
                else:
                    c.release(last, m, i0 + j)
            if n and self.turn.batches[n - 1][1]:
                self.rows_there(pe, s, n - 1)
                self.turn.turn_rows(pe, s, n - 1)
        if self.turn.batches[-1][1]:
            self.rows_there(pe, s, len(self.jobs) - 1)
            self.turn.turn_rows(pe, s, len(self.jobs) - 1)

    def scalar(self, act, s):
        c = self.core
        if self.source:
            self.source.scalar(act, s)
            act.wait_ge(s["inverse_ready"], 1)
        for n, (m, i0, kts, width, dst) in enumerate(self.jobs):
            c.split_high(act, m.slot(i0 + len(kts) - 1))
            c.wait_output(act, m, i0 + len(kts) - 1, s, self.others[n])
            act.activation(dst[0], c.bank[2 * (n % 2)][:, 0:width], ACT.Copy,
                           scale=c.inv[:, 2:3] if self.scale else 1.0).then_inc(s["drained_by_act"], 1)
            if self.turn.batches[n][0]:
                self.rows_there(act, s, n)
                self.turn.square_rows(act, s, n)
            if n:
                self.turn.copy_high(act, s, n - 1)
        self.turn.copy_high(act, s, len(self.jobs) - 1)

    def vector(self, dve, s):
        c = self.core
        step = Steps(dve, s["dve_step"])
        if self.source:
            self.source.vector(dve, s)
        for n, (m, i0, kts, width, dst) in enumerate(self.jobs):
            c.split_low(dve, m.slot(i0 + len(kts) - 1))
            c.wait_output(dve, m, i0 + len(kts) - 1, s, self.others[n])
            ps = c.bank[2 * (n % 2) + 1][:, 0:width]
            if self.scale:
                i = dve.tensor_scalar(dst[1], ps, c.inv[:, 3:4], None, ALU.mult)
            else:
                i = dve.tensor_copy(dst[1], ps)
            i.then_inc(s["drained_by_dve"], 1)
            if self.turn.batches[n][0]:
                self.rows_there(dve, s, n)
                self.turn.scale_rows(dve, s, n, step)
            if n:
                self.turn.copy_low(dve, s, n - 1)
        self.turn.copy_low(dve, s, len(self.jobs) - 1)


class Residual(Stage):

    def __init__(self, core, name, x, kts, factor=1.0, gain=None, loads=None, source=None):
        super().__init__(core)
        self.source = source
        self.m, self.x, self.kts, self.factor, self.gain, self.loads = core.plan[name], x, kts, factor, gain, loads

    def gpsimd(self, pool, s):
        if self.loads:
            self.loads.start(self.core, pool)
            self.loads.finish(self.core, pool)

    def tensor(self, pe, s):
        c, m = self.core, self.m
        xh, xl = self.x
        if self.source:
            self.source.tensor(pe, s)
        for k in range(self.kts):
            self.input_wait(pe, s, k)
            for half in range(2):
                i = 2 * k + half
                w = c.piece(pe, m, i)
                for b in range(NB):
                    cut = slice(b * P, (b + 1) * P)
                    last = mm3(pe, c.bank[4 + 2 * b + half][:, :], (xh[:, k, cut], xl[:, k, cut]), w,
                               k == 0, k == self.kts - 1)
                c.release(last, m, i)

    def row_factor(self, b):
        return self.factor

    def input_wait(self, pe, s, k):
        if self.source:
            self.source.arrive(pe, s, k)

    def scalar(self, act, s):
        c = self.core
        if self.source:
            self.source.scalar(act, s)
        c.split_high(act, self.m.slot(self.m.count - 1))
        if self.gain is None:
            return
        act.activation(c.stat[:, 8:9], c.ident[:, 0:1], ACT.Sqrt)
        act.wait_ge(c.slot_used, self.m.slot(self.m.count - 1) + 1)
        for b in range(NB):
            for half in range(2):
                act.activation(c.square[:, b, half * HALF:(half + 1) * HALF], c.bank[4 + 2 * b + half][:, :], ACT.Square,
                               accum_out=c.stat[:, 2 * b + half:2 * b + half + 1]).then_inc(s["squares_ready"], 1)
        act.wait_ge(s["means_ready"], 1)
        act.activation(c.stat[:, 4:6], c.stat[:, 4:6], ACT.Sqrt).then_inc(s["roots_ready"], 1)

    def vector(self, dve, s):
        c = self.core
        if self.source:
            self.source.vector(dve, s)
        c.split_low(dve, self.m.slot(self.m.count - 1))
        step = Steps(dve, s["sum_step"])
        dve.wait_ge(c.slot_used, self.m.slot(self.m.count - 1) + 1)
        quarters = [(b, slice(half * HALF, (half + 1) * HALF), c.bank[4 + 2 * b + half][:, :])
                    for b in range(NB) for half in range(2)]
        if self.gain is None:
            for b, cut, ps in quarters:
                dve.scalar_tensor_tensor(c.h[:, b, cut], ps, self.row_factor(b), c.h[:, b, cut], ALU.mult, ALU.add)
            return
        for n, (b, cut, ps) in enumerate(quarters):
            dve.wait_ge(s["squares_ready"], n + 1)
            dve.tensor_tensor(c.xn[:, b, cut], ps, self.gain[:, cut], ALU.mult).then_inc(s["out_ready"], 1)
        sums = c.stat[:, 0:4].rearrange("p (b f) -> p b f", f=2)
        step(dve.tensor_reduce(c.stat[:, 4:6], sums, AX.X, ALU.add))
        dve.tensor_scalar(c.stat[:, 4:6], c.stat[:, 4:6], 1.0 / D, EPS, ALU.mult, ALU.add).then_inc(s["means_ready"], 1)
        dve.wait_ge(s["roots_ready"], 1)
        step(dve.reciprocal(c.stat[:, 4:6], c.stat[:, 4:6]))
        dve.wait_ge(s["out_ready"], 4)
        for b, cut, ps in quarters:
            dve.scalar_tensor_tensor(c.h[:, b, cut], c.xn[:, b, cut], c.stat[:, 4 + b:5 + b], c.h[:, b, cut],
                                     ALU.mult, ALU.add)


class Ffn(Residual):

    def __init__(self, core, up, down, source, factor=1.0, gain=None, conv=False, loads=None):
        super().__init__(core, down, (core.hh, core.hl), FT, factor, gain, loads)
        self.up, self.conv, self.rows = core.plan[up], conv, source
        work = core.square[:, :, :].rearrange("p a b -> p (a b)")
        part = lambda at, n, w: work[:, at:at + n * w].rearrange("p (n w) -> p n w", n=n)
        self.product = part(0, 2, S)
        self.silu = part(2 * S, 3, S)
        self.mixed = part(2 * S, 3, HALF)
        self.scaled_in = part(2 * S + 3 * HALF, 2, HALF)

    def row_factor(self, b):
        return self.core.inv[:, 4 + b:5 + b]

    def tensor(self, pe, s):
        c = self.core
        self.rows.tensor(pe, s)
        for f in range(FT):
            if f == 1:
                self.rows.row(pe, s)
            if f >= 4:
                pe.wait_ge(s["partial_ready" if self.conv else "gates_ready"], f - 3)
            for part in range(2):
                for k in range(KT):
                    if f == 0 and part == 0:
                        self.rows.arrive(pe, s, k)
                    i = (2 * f + part) * KT + k
                    last = mm3(pe, c.bank[f % 4][:, part * S:(part + 1) * S], c.piece(pe, self.up, i),
                               (c.xh[:, k, :], c.xl[:, k, :]), k == 0, k == KT - 1)
                    c.release(last, self.up, i)
        super().tensor(pe, s)

    def input_wait(self, pe, s, k):
        pe.wait_ge(s["hidden_ready"], k + 1)

    def scalar(self, act, s):
        c = self.core
        self.rows.scalar(act, s)
        w = PARAM(c.param, "conv_w").rearrange("p (j f) -> p j f", j=3)
        bias = PARAM(c.param, "conv_b")
        late = 1 if self.conv else 0

        c.split_high(act, self.up.first)
        for step in range(FT + 1 + late):
            if step < FT:
                c.split_high(act, self.up.first + step + 1)
            if step < FT and self.conv:
                f = step
                act.wait_ge(s["partial_ready"], f + 1)
                if f >= 3:
                    act.wait_ge(s["gates_ready"], f - 2)
                for part, col in ((0, f), (1, FT + f)):
                    last = act.activation(self.mixed[:, f % 3, part * S:(part + 1) * S],
                                          self.scaled_in[:, f % 2, part * S:(part + 1) * S], ACT.Identity,
                                          bias=bias[:, col:col + 1], scale=w[:, 2, col:col + 1])
                last.then_inc(s["scores_ready"], 1)
            if 0 <= step - late < FT:
                f = step - late
                act.wait_ge(s["convolved"], f + 1)
                gate = self.mixed[:, f % 3, 0:S] if self.conv else self.silu[:, f % 3, :]
                act.activation(gate, gate, ACT.Silu).then_inc(s["inputs_ready"], 1)
            if 0 <= step - late - 1 < FT:
                f = step - late - 1
                act.wait_ge(s["gates_ready"], f + 1)
                act.activation(c.hh[:, f, :], self.product[:, f % 2, :], ACT.Copy).then_inc(s["highs_ready"], 1)
        Residual.scalar(self, act, s)

    def vector(self, dve, s):
        c = self.core
        self.rows.vector(dve, s, self.factor, row=True)
        w = PARAM(c.param, "conv_w").rearrange("p (j f) -> p j f", j=3)
        taps, late = 0, 1 if self.conv else 0
        row = c.inv_row[:, :]

        c.split_low(dve, self.up.first)
        for step in range(FT + 2 + late):
            if step < FT:
                f = step
                dve.wait_ge(c.slot_used, self.up.first + f + 1)
                if f == 0:
                    self.rows.take_row(dve, s)
                ps = c.bank[f % 4]
                if self.conv:
                    if f >= 2:
                        dve.wait_ge(s["scores_ready"], f - 1)
                        dve.wait_ge(s["convolved"], f - 1)
                    dve.tensor_tensor(self.scaled_in[:, f % 2, :].rearrange("p (a t) -> p a t", a=2),
                                      ps[:, :].rearrange("p (a t) -> p a t", a=2),
                                      row.unsqueeze(1).to_broadcast([P, 2, S]), ALU.mult)\
                       .then_inc(s["partial_ready"], 1)
                else:
                    if f >= 3:
                        dve.wait_ge(s["gates_ready"], f - 2)
                    dve.tensor_tensor(self.silu[:, f % 3, :], ps[:, 0:S], row, ALU.mult).then_inc(s["convolved"], 1)
            if self.conv and 0 <= step - 1 < FT:
                f = step - 1
                dve.wait_ge(s["scores_ready"], f + 1)
                for j in (1, 0):
                    back = 2 - j
                    for part, col in ((0, f), (1, FT + f)):
                        if j == 0:
                            dve.wait_ge(s["dve_step"], 2 * f + 1 + part)
                        at = part * S
                        buf = self.mixed[:, f % 3, at + back:at + S]
                        i = dve.scalar_tensor_tensor(buf, self.scaled_in[:, f % 2, at:at + S - back],
                                                     w[:, j, col:col + 1], buf, ALU.mult, ALU.add)
                        if j == 1:
                            i.then_inc(s["dve_step"], 1)
                i.then_inc(s["convolved"], 1)
            if 0 <= step - late - 1 < FT:
                f = step - late - 1
                dve.wait_ge(s["inputs_ready"], f + 1)
                if f >= 2:
                    dve.wait_ge(s["hidden_ready"], f - 1)
                gate = self.mixed[:, f % 3, 0:S] if self.conv else self.silu[:, f % 3, :]
                value = self.mixed[:, f % 3, S:HALF] if self.conv else c.bank[f % 4][:, S:HALF]
                dve.tensor_tensor(self.product[:, f % 2, :], gate, value, ALU.mult).then_inc(s["gates_ready"], 1)
            if 0 <= step - late - 2 < FT:
                f = step - late - 2
                dve.wait_ge(s["highs_ready"], f + 1)
                dve.tensor_tensor(c.hl[:, f, :], self.product[:, f % 2, :], c.hh[:, f, :].bitcast(F32), ALU.subtract)\
                   .then_inc(s["hidden_ready"], 1)
            if step < FT:
                c.split_low(dve, self.up.first + step + 1)
        Residual.vector(self, dve, s)


class Merge(Stage):

    TILES = ((0, 1), (2,), (3, 4), (5, 6))

    def __init__(self, core):
        super().__init__(core)
        self.source = Source(core, core.o, (core.oh, core.ol), 7, base=4)

    def tensor(self, pe, s):
        c = self.core
        for n in range(4):
            branch, gate = c.plan[f"branch{n}"], c.plan[f"gate{n}"]
            kts = self.TILES[n]
            for half in range(2):
                if n == 0:
                    self.source.tensor(pe, s, 4 * half, 4 * half + 4)
                if n:
                    pe.wait_ge(s["gates_ready"], 4 * (n - 1) + 2 * half + 2)
                for k in range(KT):
                    i = half * KT + k
                    w = c.piece(pe, gate, i)
                    for b in range(NB):
                        cut = slice(b * P, (b + 1) * P)
                        last = mm3(pe, c.bank[2 * half + b][:, :], (c.xh[:, k, cut], c.xl[:, k, cut]), w,
                                   k == 0, k == KT - 1)
                    c.release(last, gate, i)
            if n:
                pe.wait_ge(s["out_taken"], 4 * n)
            else:
                pe.wait_ge(s["low_turned"], self.source.tiles)
            for half in range(2):
                for j, k in enumerate(kts):
                    i = half * len(kts) + j
                    w = c.piece(pe, branch, i)
                    for b in range(NB):
                        cut = slice(b * P, (b + 1) * P)
                        last = mm3(pe, c.bank[4 + 2 * half + b][:, :], (c.oh[:, k, cut], c.ol[:, k, cut]), w,
                                   j == 0, j == len(kts) - 1)
                    c.release(last, branch, i)

    def scalar(self, act, s):
        c = self.core
        for n in range(4):
            gate = c.plan[f"gate{n}"]
            for half in range(2):
                if n == 0 and half == 0:
                    self.source.scalar(act, s, 0, 4)
                c.split_high(act, gate.first + 2 * half + 1)
                if n == 0 and half == 0:
                    self.source.scalar(act, s, 4)
                if half:
                    c.split_high(act, gate.first + gate.slots)
                act.wait_ge(c.slot_used, gate.first + 2 * half + 2)
                for b in range(NB):
                    q = 2 * half + b
                    if n:
                        act.wait_ge(s["out_taken"], 4 * (n - 1) + q + 1)
                    act.activation(c.square[:, q // 2, (q % 2) * HALF:(q % 2 + 1) * HALF], c.bank[q][:, :],
                                   ACT.Sigmoid, scale=c.inv[:, 2 + b:3 + b]).then_inc(s["gates_ready"], 1)

    def vector(self, dve, s):
        c = self.core
        step = Steps(dve, s["dve_step"])
        for n in range(4):
            gate = c.plan[f"gate{n}"]
            for half in range(2):
                if n == 0 and half == 0:
                    self.source.vector(dve, s, first=0, end=4)
                c.split_low(dve, gate.first + 2 * half + 1)
                if n == 0 and half == 0:
                    self.source.vector(dve, s, first=4)
                if half == 0:
                    c.split_low(dve, gate.first + gate.slots)
                    dve.wait_ge(c.slot_used, gate.first + gate.slots + 1)
                for b in range(NB):
                    q = 2 * half + b
                    dve.wait_ge(s["gates_ready"], 4 * n + q + 1)
                    g = c.square[:, q // 2, (q % 2) * HALF:(q % 2 + 1) * HALF]
                    out = c.xn[:, b, half * HALF:(half + 1) * HALF]
                    if n == 0:
                        dve.tensor_tensor(out, g, c.bank[4 + q][:, :], ALU.mult).then_inc(s["out_taken"], 1)
                    else:
                        dve.wait_ge(s["out_taken"], 4 * n + q)
                        step(dve.tensor_tensor(c.square[:, 2, 0:HALF], g, c.bank[4 + q][:, :], ALU.mult))
                        dve.tensor_tensor(out, out, c.square[:, 2, 0:HALF], ALU.add).then_inc(s["out_taken"], 1)


class Unit:

    def __init__(self, q, k, v, parts, scale, dv, finish, cols, bias=None, minus=False, extra=None):
        self.q, self.k, self.v, self.parts, self.scale, self.dv = q, k, v, parts, scale, dv
        self.finish, self.cols, self.bias, self.minus, self.extra = finish, cols, bias, minus, extra
        self.n, self.nk = len(q), sum(parts)


class Attention(Stage):

    def __init__(self, core, units, select=None, loads=None, fill=0):
        super().__init__(core)
        self.fill = fill
        self.units, self.select, self.loads = units, select, loads

    def gpsimd(self, pool, s):
        if self.loads:
            self.loads.start(self.core, pool)
            self.loads.finish(self.core, pool)

    SCORE_BANKS = (0, 1, 6)

    def scores(self, i):
        u = self.units[i]
        bank = self.core.bank[self.SCORE_BANKS[i % 3]]
        return bank[:, :].rearrange("p (n k) -> p n k", n=2)[:, 0:u.n, 0:u.nk]

    def tensor(self, pe, s):
        c, units = self.core, self.units

        def score(i):
            u = units[i]
            if i >= 3:
                pe.wait_ge(s["logits_ready" if units[i - 3].bias is not None else "probs_ready"], i - 2)
            ps = self.scores(i)
            for j in range(u.n):
                last = mm(pe, ps[:, j, :], u.q[j], u.k[j], True, True)
            last.then_inc(s["scores_ready"], 1)

        def turn(i):
            u = units[i]
            pe.wait_ge(s["probs_ready"], i + 1)
            if i >= 2:
                pe.wait_ge(s["probs_copied"], i - 1)
            for j in range(u.n):
                for t, size in enumerate(u.parts):
                    at = (j * len(u.parts) + t) * P
                    last = pe.transpose(c.bank[2 + i % 2][0:size, at:at + P],
                                        c.prob[:, i % 4, j, t * P:t * P + size], c.ident)
            last.then_inc(s["probs_turned"], 1)

        def value(i):
            u = units[i]
            pe.wait_ge(s["probs_copied"], i + 1)
            if i >= 2:
                pe.wait_ge(s["out_taken"], i - 1)
            for j in range(u.n):
                for t, size in enumerate(u.parts):
                    last = mm(pe, c.bank[4 + i % 2][:, j * u.dv:(j + 1) * u.dv],
                              c.prob_t[0:size, i % 2, j * len(u.parts) + t, :], u.v[j][t],
                              t == 0, t == len(u.parts) - 1)
            last.then_inc(s["out_ready"], 1)

        for i in range(min(3, len(units))):
            score(i)
        keep_clock(pe, c, self.fill)
        for i in range(len(units) + 1):
            if i < len(units):
                turn(i)
            if i + 3 < len(units):
                score(i + 3)
            if i:
                value(i - 1)

    def scalar(self, act, s):
        c, units = self.core, self.units
        c.split_high(act, -LEAD)

        def exp(i):
            u = units[i]
            act.wait_ge(s["logits_ready"], i + 1)
            if i >= 4:
                act.wait_ge(s["probs_turned"], i - 3)
            for j in range(u.n):
                dst = c.prob[:, i % 4, j, 0:u.nk]
                src, scale = (dst, 1.0) if u.bias is not None else (self.scores(i)[:, j, :], u.scale)
                col = u.cols.start + j * (u.cols.step or 1)
                last = act.activation(dst, src, ACT.Exp, bias=c.nmax[:, col:col + 1],
                                      scale=scale, accum_out=c.den[:, col:col + 1])
            last.then_inc(s["probs_ready"], 1)

        exp(0)
        for i, u in enumerate(units):
            if i + 1 < len(units):
                exp(i + 1)
            act.wait_ge(s["probs_turned"], i + 1)
            if i >= 2:
                act.wait_ge(s["out_ready"], i - 1)
            size, tiles = u.parts[0], u.n * len(u.parts)
            act.activation(c.prob_t[0:size, i % 2, 0:tiles, :],
                           c.bank[2 + i % 2][0:size, 0:tiles * P].rearrange("p (n q) -> p n q", q=P),
                           ACT.Copy).then_inc(s["probs_copied"], 1)

    def vector(self, dve, s):
        c, units = self.core, self.units
        step = Steps(dve, s["dve_step"])

        def logits(i):
            u = units[i]
            dve.wait_ge(s["scores_ready"], i + 1)
            if i >= 4:
                dve.wait_ge(s["probs_turned"], i - 3)
            ps = self.scores(i)
            if u.bias is None:
                step(dve.tensor_reduce(c.nmax[:, u.cols], ps, AX.X, ALU.max, negate=True))
                dve.tensor_scalar(c.nmax[:, u.cols], c.nmax[:, u.cols], u.scale, None, ALU.mult)\
                   .then_inc(s["logits_ready"], 1)
                return
            t = c.prob[:, i % 4, 0:u.n, 0:u.nk]
            step(dve.scalar_tensor_tensor(t, ps, u.scale, u.bias, ALU.mult, ALU.subtract if u.minus else ALU.add))
            if u.extra is not None:
                step(dve.tensor_tensor(t, t, u.extra, ALU.add))
            dve.tensor_reduce(c.nmax[:, u.cols], t, AX.X, ALU.max, negate=True).then_inc(s["logits_ready"], 1)

        def finish(i):
            u = units[i]
            dve.wait_ge(s["out_ready"], i + 1)
            if i:
                dve.wait_ge(s["out_taken"], i)
            ps = c.bank[4 + i % 2][:, 0:u.n * u.dv].rearrange("p (n d) -> p n d", n=u.n)
            u.finish(dve, step, u, ps).then_inc(s["out_taken"], 1)

        logits(0)
        logits(1)
        for i in range(len(units) + 2):
            if i + 2 < len(units):
                logits(i + 2)
            if self.select and i < 8 and i % 2 == 0:
                self.select.search(dve, step, 4 + i // 2)
            if i >= 2:
                finish(i - 2)


def scaled(core, dst, factor=None, add=False):

    def finish(dve, step, u, ps):
        r = core.rden[:, u.cols]
        step(dve.reciprocal(r, core.den[:, u.cols]))
        if factor is not None:
            step(dve.tensor_tensor(r, r, factor, ALU.mult))
        if not add:
            return dve.tensor_tensor(dst, ps, r.unsqueeze(2).to_broadcast([P, u.n, u.dv]), ALU.mult)
        for j in range(u.n):
            col = u.cols.start + j * (u.cols.step or 1)
            last = dve.scalar_tensor_tensor(dst[:, j, :], ps[:, j, :], core.rden[:, col:col + 1], dst[:, j, :],
                                            ALU.mult, ALU.add)
        return last

    return finish


def kept(core, dst):
    return lambda dve, step, u, ps: dve.tensor_copy(dst, ps)


class Compress(Stage):

    def __init__(self, core):
        super().__init__(core)
        c = core
        self.m = c.plan["phi"]
        free = c.u[:, 0, 2600:3720]
        self.x = c.xn[:, 1, :].rearrange("p (l c) -> p l c", c=32)
        self.g = free[:, 512:544].rearrange("p (a c) -> p a c", a=2)
        self.v = core.small[:, 0:DH]
        self.k = core.small[:, DH:DH + 16]
        self.lf = free[:, 560:568].rearrange("p (b h) -> p b h", b=NB)
        self.t1 = free[:, 576:584].rearrange("p (b h) -> p b h", b=NB)
        self.t2 = free[:, 592:600].rearrange("p (b h) -> p b h", b=NB)
        self.cq = free[:, 608:616].rearrange("p (b h) -> p b h", b=NB)
        self.spread = c.square[:, 0, :].rearrange("p (b h q) -> p b h q", b=NB, h=4)
        self.gates = core.small[:, 96:96 + 24].rearrange("p (b g) -> p b g", b=NB)
        self.cmp_gates = core.small[:, 128:136].rearrange("p (b h) -> p b h", b=NB)

    def blocks(self, pe, first, end):
        c = self.core
        for l in range(first, end):
            c.piece(pe, self.m, l)
            w = c.raw[:, self.m.slot(l) % RING, self.m.offset(l):self.m.offset(l) + P]
            last = mm(pe, c.bank[0][:, 0:32], w, self.x[:, l, :], l == 0, l == 31)
            c.release(last, self.m, l)

    def tensor(self, pe, s):
        c = self.core
        pe.wait_ge(s["inputs_ready"], 1)
        self.blocks(pe, 0, 16)
        pe.wait_ge(s["partial_ready"], 1)
        upto, ones = CONST(c.const, "upto"), CONST(c.const, "ones")
        mm(pe, c.bank[2][:, 0:4], upto, self.lf[:, 0, :], True, True)
        mm(pe, c.bank[2][:, 4:8], ones, self.lf[:, 0, :], True, False)
        mm(pe, c.bank[2][:, 4:8], upto, self.lf[:, 1, :], False, True).then_inc(s["scores_ready"], 1)
        for h in range(4):
            ps = c.bank[3 + h // 2][:, (h % 2) * S:(h % 2 + 1) * S]
            mm(pe, ps[:, 0:P], self.spread[:, 0, h, :], upto, True, True)
            mm(pe, ps[:, P:S], self.spread[:, 0, h, :], ones, True, False)
            last = mm(pe, ps[:, P:S], self.spread[:, 1, h, :], upto, False, True)
        last.then_inc(s["scores_ready"], 1)
        self.blocks(pe, 16, 32)
        pe.wait_ge(s["gates_ready"], 1)
        mm(pe, c.bank[5][:, 0:16], PARAM(c.param, "w2k"), self.g[:, 0, :], True, True)
        mm(pe, c.bank[6][0:16, 0:DH], self.g[:, 1, :], PARAM(c.param, "w2v"), True, True).then_inc(s["out_ready"], 1)

    def scalar(self, act, s):
        c = self.core
        step = Steps(act, s["act_step"])
        act.wait_ge(s["sums_ready"], 1)
        step(act.activation(self.t2, self.t1, ACT.Abs))
        step(act.activation(self.t2, self.t2, ACT.Exp, scale=-1.0))
        act.activation(self.t2, self.t2, ACT.Ln, bias=1.0).then_inc(s["means_ready"], 1)
        for b in range(NB):
            last = act.activation(self.gates[:, b, :], c.u[:, b, 128:140], ACT.Sigmoid)
        last.then_inc(s["roots_ready"], 1)
        c.split_high(act, self.m.first + self.m.slots - 1)
        act.wait_ge(c.slot_used, self.m.first + self.m.slots)
        act.activation(self.g, c.bank[0][:, 0:32].rearrange("p (a c) -> p a c", a=2), ACT.Gelu_apprx_tanh)\
           .then_inc(s["gates_ready"], 1)

    def vector(self, dve, s):
        c = self.core
        step = Steps(dve, s["dve_step"])
        step(dve.memset(c.xn[:, 1, :], 0.0))
        for rows, at in ((slice(0, DH), 0), (slice(DH, P), 16)):
            tok = c.t[rows, 4, :].rearrange("p (c l) -> p l c", l=16)
            pos = PARAM(c.param, "cmp_pos")[rows]
            for part in range(2):
                cut = slice(16 * part, 16 * part + 16)
                last = dve.tensor_tensor(self.x[rows, cut, at:at + 15], tok[:, :, part:part + 15],
                                         pos[:, cut].unsqueeze(2).to_broadcast([DH, 16, 15]), ALU.add)
        last.then_inc(s["inputs_ready"], 1)
        bias = PARAM(c.param, "f_bias")
        for b in range(NB):
            last = dve.tensor_tensor(self.t1[:, b, :], c.u[:, b, 780:784], bias, ALU.add)
        last.then_inc(s["sums_ready"], 1)
        dve.wait_ge(s["means_ready"], 1)
        step(dve.scalar_tensor_tensor(self.lf, self.t1, 0.0, self.t2, ALU.min, ALU.subtract))
        dve.tensor_copy(self.spread, self.lf.unsqueeze(3).to_broadcast([P, NB, 4, P]))\
           .then_inc(s["partial_ready"], 1)
        dve.wait_ge(s["roots_ready"], 1)
        gates = self.gates.rearrange("p b (h r) -> p b h r", r=3)
        for b in range(NB):
            dve.tensor_scalar(self.cmp_gates[:, b, :], gates[:, b, :, 0], CONST(c.const, "cmp_valid")[:, b:b + 1],
                              None, ALU.mult)
        dve.wait_ge(s["scores_ready"], 2)
        step(dve.tensor_copy(self.cq, c.bank[2][:, 0:8].rearrange("p (b h) -> p b h", b=NB)))
        causal = CONST(c.const, "causal")
        for b in range(NB):
            nk = (b + 1) * P
            if b == 1:
                dve.wait_ge(s["gates_ready"], 1)
            for h in range(4):
                ps = c.bank[3 + h // 2][:, (h % 2) * S:(h % 2) * S + nk]
                dve.scalar_tensor_tensor(c.forget[:, b, h, 0:nk], ps, self.cq[:, b, h:h + 1], causal[:, S - nk:S],
                                         ALU.subtract, ALU.subtract)
        c.split_low(dve, self.m.first + self.m.slots - 1)
        dve.wait_ge(s["out_ready"], 1)
        dve.tensor_copy(self.k[:, 0:15], c.bank[5][:, 0:15])
        dve.tensor_copy(self.v[0:15, :], c.bank[6][0:15, 0:DH])


class Rope(Turn):

    def __init__(self, core, groups, q, kv, rope, k):
        super().__init__(core, [((), groups)])
        self.q, self.kv, self.rope, self.k = q, kv, rope, k

    def vector(self, dve, s):
        c = self.core
        step = Steps(dve, s["dve_step"])
        for b in range(NB):
            cos = CONST(c.const, "cos")[:, 16 * b:16 * b + 16]
            sin = CONST(c.const, "sin")[:, 16 * b:16 * b + 16]
            q = self.q(b).rearrange("p (h d) -> p h d", h=4)
            k = self.k(b).rearrange("p (h d) -> p h d", h=4)
            kv = self.kv(b).rearrange("p (h d) -> p h d", h=4)
            rope = self.rope(b).unsqueeze(1)
            for n, x in ((4, q[:, :, DH:96]), (1, rope)):
                t = c.square[:, b, 0:4 * n * 16].rearrange("p (a h d) -> p a h d", a=4, h=n)
                w = lambda a: a.unsqueeze(1).to_broadcast([P, n, 16])
                x1, x2 = x[:, :, 0:16], x[:, :, 16:32]
                dve.tensor_tensor(t[:, 0], x1, w(cos), ALU.mult)
                dve.tensor_tensor(t[:, 1], x2, w(sin), ALU.mult)
                dve.tensor_tensor(t[:, 2], x2, w(cos), ALU.mult)
                step(dve.tensor_tensor(t[:, 3], x1, w(sin), ALU.mult))
                dve.tensor_tensor(x1, t[:, 0], t[:, 1], ALU.subtract)
                step(dve.tensor_tensor(x2, t[:, 2], t[:, 3], ALU.add))
            dve.tensor_copy(k[:, :, 0:DH], kv[:, :, 0:DH])
            dve.tensor_copy(k[:, :, DH:96], rope.to_broadcast([P, 4, 32])).then_inc(s["rows_scaled"], 1)
        self.copy_low(dve, s, 0)


class Dilated(Stage):

    def __init__(self, core, kept_products, base):
        super().__init__(core)
        c = core
        cut = slice(base, base + 12)
        shape = lambda a: a.rearrange("p (b g h) -> p b g h", b=NB, g=3)
        self.nm, self.den = shape(c.nmax[:, cut]), shape(c.den[:, cut])
        self.e = shape(c.rden[:, cut])
        self.m = c.stat[:, 0:4].rearrange("p (b h) -> p b h", b=NB)
        self.sum = c.stat[:, 4:8].rearrange("p (b h) -> p b h", b=NB)
        self.products = kept_products
        self.t = c.square[:, 0, 0:768].rearrange("p (b g h d) -> p b g h d", b=NB, g=3, h=2)

    def scalar(self, act, s):
        act.wait_ge(s["inputs_ready"], 1)
        for b in range(NB):
            last = act.activation(self.e[:, b], self.e[:, b], ACT.Exp)
        last.then_inc(s["probs_ready"], 1)

    def vector(self, dve, s):
        step = Steps(dve, s["dve_step"])
        nm, den, e, m, total = self.nm, self.den, self.e, self.m, self.sum
        step(dve.tensor_tensor(m, nm[:, :, 0], nm[:, :, 1], ALU.min))
        step(dve.tensor_tensor(m, m, nm[:, :, 2], ALU.min))
        for g in range(3):
            last = dve.tensor_tensor(e[:, :, g], m, nm[:, :, g], ALU.subtract)
        last.then_inc(s["inputs_ready"], 1)
        dve.wait_ge(s["probs_ready"], 1)
        flat = lambda a: a.rearrange("p b g h -> p (b g h)")
        step(dve.tensor_tensor(self.core.stat[:, 16:28], flat(e), flat(den), ALU.mult))
        ed = self.core.stat[:, 16:28].rearrange("p (b g h) -> p b g h", b=NB, g=3)
        step(dve.tensor_tensor(total, ed[:, :, 0], ed[:, :, 1], ALU.add))
        step(dve.tensor_tensor(total, total, ed[:, :, 2], ALU.add))
        step(dve.reciprocal(total, total))
        for g in range(3):
            last = dve.tensor_tensor(e[:, :, g], e[:, :, g], total, ALU.mult)
        step(last)
        for b in range(NB):
            x = self.products[:, b].rearrange("p g h d -> p (g h) d")
            w = e[:, b].rearrange("p g h -> p (g h)").unsqueeze(2).to_broadcast([P, 6, DH])
            last = dve.tensor_tensor(self.t[:, b].rearrange("p g h d -> p (g h) d"), x, w, ALU.mult)
        step(last)
        for b in range(NB):
            out = self.core.o[:, b, 256:384].rearrange("p (h d) -> p h d", h=2)
            step(dve.tensor_tensor(out, self.t[:, b, 0], self.t[:, b, 1], ALU.add))
            dve.tensor_tensor(out, out, self.t[:, b, 2], ALU.add)


class Select(Stage):

    def __init__(self, core, q, k, weights):
        super().__init__(core)
        self.q, self.k, self.weights = q, k, weights
        c = core
        self.relu = c.square[:, 0, :].rearrange("p (n j k) -> p n j k", n=2, j=2)
        self.score = c.xn[:, 1, 0:HALF].rearrange("p (b k) -> p b k", b=NB)
        self.best = c.xn[:, 1, HALF:HALF + 16].rearrange("p (b k) -> p b k", b=NB)
        self.w = c.square[:, 2, 0:16].rearrange("p (b h) -> p b h", b=NB)
        self.units = [(b, pair) for b in range(NB) for pair in ((0, 2), (1, 3), (4, 6), (5, 7))]

    def tensor(self, pe, s):
        c = self.core
        for i, (b, pair) in enumerate(self.units):
            nk = (b + 1) * P
            if i >= 2:
                pe.wait_ge(s["probs_ready"], i - 1)
            for j, h in enumerate(pair):
                last = mm(pe, c.bank[i % 2][:, j * S:j * S + nk], self.q(h)[:, b * P:(b + 1) * P],
                          self.k(h)[:, 0:nk], True, True)
            last.then_inc(s["scores_ready"], 1)

    def scalar(self, act, s):
        c = self.core
        for i, (b, pair) in enumerate(self.units):
            nk = (b + 1) * P
            act.wait_ge(s["scores_ready"], i + 1)
            if i >= 2:
                act.wait_ge(s["out_taken"], i - 1)
            ps = c.bank[i % 2][:, :].rearrange("p (j k) -> p j k", j=2)[:, :, 0:nk]
            act.activation(self.relu[:, i % 2, :, 0:nk], ps, ACT.Relu, scale=DH ** -0.5)\
               .then_inc(s["probs_ready"], 1)

    def vector(self, dve, s):
        c = self.core
        step = Steps(dve, s["dve_step"])
        for b in range(NB):
            step(dve.tensor_scalar(self.w[:, b, :], self.weights(b), 8 ** -0.5, None, ALU.mult))
        for i, (b, pair) in enumerate(self.units):
            nk = (b + 1) * P
            dve.wait_ge(s["probs_ready"], i + 1)
            for j, h in enumerate(pair):
                r, score, w = self.relu[:, i % 2, j, 0:nk], self.score[:, b, 0:nk], self.w[:, b, h:h + 1]
                if i % 4 == 0 and j == 0:
                    step(dve.tensor_scalar(score, r, w, None, ALU.mult))
                else:
                    m = dve.scalar_tensor_tensor(score, r, w, score, ALU.mult, ALU.add)
                    if j == 0:
                        step(m)
            m.then_inc(s["out_taken"], 1)
            dve.wait_ge(s["out_taken"], i + 1)
            if b == 1:
                self.search(dve, step, i % 4)

    def search(self, dve, step, part):
        c = self.core
        b, quarter = part // 4, part % 4
        nk = (b + 1) * P
        score = self.score[:, b, 0:nk]
        if quarter == 0:
            step(dve.memset(score[0:DH, nk - DH:nk], NEG))
        for n in range(TOP_K // 8 // 4):
            step(dve.max(self.best[:, b, :], score))
            step(dve.match_replace(score, self.best[:, b, :], score, TAKEN))
        if quarter == 3:
            step(dve.tensor_scalar(c.taken[:, b, 0:nk], score, TAKEN, NEG, ALU.not_equal, ALU.mult))


class Lambda(Stage):

    def vector(self, dve, s):
        c = self.core
        step = Steps(dve, s["dve_step"])
        lam = PARAM(c.param, "lam").rearrange("p (n d) -> p n d", n=4)
        for n in range(2):
            step(dve.tensor_tensor(c.square[:, 0, n * DH:(n + 1) * DH], lam[:, 2 * n, :], lam[:, 2 * n + 1, :], ALU.mult))
        dve.tensor_reduce(c.small[:, 144:146], c.square[:, 0, 0:2 * DH].rearrange("p (n d) -> p n d", n=2),
                          AX.X, ALU.add).then_inc(s["sums_ready"], 1)
        dve.wait_ge(s["probs_ready"], 1)
        step(dve.tensor_tensor(c.small[:, 140:141], c.small[:, 147:148], c.small[:, 146:147], ALU.subtract))
        step(dve.tensor_scalar(c.small[:, 140:141], c.small[:, 140:141], -LAMBDA_INIT, None, ALU.add))
        dve.tensor_copy(c.small[:, 141:142], c.small[:, 140:141])

    def scalar(self, act, s):
        c = self.core
        act.wait_ge(s["sums_ready"], 1)
        act.activation(c.small[:, 146:148], c.small[:, 144:146], ACT.Exp).then_inc(s["probs_ready"], 1)


LAMBDA_INIT = 0.8 - 0.6 * math.exp(0.0)


class Store(Stage):
    def __init__(self, core, out):
        super().__init__(core)
        self.out = out

    def gpsimd(self, pool, s):
        c = self.core
        pool.dma_start(self.out, c.h[:, :, :]).then_inc(c.stored, 16)
        pool.wait_ge(c.stored, 16)



def half(tile, h, cols=slice(None)):
    return tile[(h % 2) * DH:(h % 2 + 1) * DH, h // 2, cols]


def block_cut(b):
    return slice(b * P, (b + 1) * P)


def first_units(c, compress):
    units = []
    rel = c.bias
    pairs = ((0, 2), (1, 3))
    for b in range(NB):
        nk, parts = (b + 1) * P, [P] * (b + 1)
        keys, qs = slice(0, nk), block_cut(b)
        for pair in pairs:
            q = [half(c.t, h, qs) for h in pair]
            rows = slice((pair[0] % 2) * DH, (pair[0] % 2 + 1) * DH)
            heads = slice(pair[0], 4, 2)
            dst = c.o[:, b, 0:256].rearrange("p (h d) -> p h d", d=DH)[:, heads, :]
            gates = compress.gates[:, b, :].rearrange("p (h r) -> p h r", r=3)
            at = 2 * len(units)
            mask = CONST(c.const, "cmp_mask")[:, 15 * b:15 * b + 15].unsqueeze(1).to_broadcast([P, 2, 15])
            units.append(Unit(q, [compress.k[rows, 0:15]] * 2, [[compress.v[0:15, :]]] * 2, [15], DH ** -0.5, DH,
                              scaled(c, dst, compress.cmp_gates[:, b, heads]), slice(at, at + 2), mask))
            for r, (kt, v0) in enumerate(((2, 0), (3, DH)), 1):
                at = 2 * len(units)
                k = c.t[rows, kt, keys]
                v = [c.u[:, t, v0:v0 + DH] for t in range(b + 1)]
                units.append(Unit(q, [k, k], [v, v], parts, DH ** -0.5, DH, scaled(c, dst, gates[:, heads, r], add=True),
                                  slice(at, at + 2), rel[:, heads, S - nk:S]))
    base = 2 * len(units)
    for b in range(NB):
        nk, parts = (b + 1) * P, [P] * (b + 1)
        keys, qs = slice(0, nk), block_cut(b)
        for heads in ((0, 2), (1, 3), (4,), (5,)):
            q = [half(c.t[:, 5:8, :], h, qs) for h in heads]
            k = [half(c.t[:, 8:11, :], h, keys) for h in heads]
            v = [[c.u[:, t, 140 + h * DH:140 + (h + 1) * DH] for t in range(b + 1)] for h in heads]
            cut = slice(heads[0], heads[-1] + 1, 2)
            dst = c.products[:, b].rearrange("p g h d -> p (g h) d")[:, cut, :]
            units.append(Unit(q, k, v, parts, DH ** -0.5, DH, kept(c, dst),
                              slice(base + 6 * b + heads[0], base + 6 * b + heads[-1] + 1, 2),
                              rel[:, slice(4 + heads[0], 4 + heads[-1] + 1, 2), S - nk:S]))
    at = base + 12
    for b in range(NB):
        nk, parts = (b + 1) * P, [P] * (b + 1)
        keys, qs = slice(0, nk), block_cut(b)
        for pair in pairs:
            heads = slice(pair[0], 4, 2)
            v = [[c.u[:, t, 524 + h * DH:524 + (h + 1) * DH] for t in range(b + 1)] for h in pair]
            dst = c.o[:, b, 384:640].rearrange("p (h d) -> p h d", d=DH)[:, heads, :]
            units.append(Unit([half(c.t[:, 11:13, :], h, qs) for h in pair], [half(c.t[:, 13:15, :], h, keys) for h in pair],
                              v, parts, DH ** -0.5, DH, scaled(c, dst), slice(at, at + 2),
                              c.forget[:, b, heads, 0:nk], minus=True))
            at += 2
        for pair in ((0, 1), (2, 3)):
            heads = slice(pair[0], pair[0] + 2)
            v = [[c.u[:, t, 1584 + h * P + DH:1584 + (h + 1) * P] for t in range(b + 1)] for h in pair]
            dst = c.o[:, b, 640:896].rearrange("p (h d) -> p h d", d=DH)[:, heads, :]
            mask = CONST(c.const, "causal")[:, S - nk:S].unsqueeze(1).to_broadcast([P, 2, nk])
            units.append(Unit([c.t[0:96, 15 + h, qs] for h in pair], [c.t[0:96, 19 + h, keys] for h in pair], v, parts,
                              96 ** -0.5, DH, scaled(c, dst), slice(at, at + 2), mask))
            at += 2
    return units, base


def head_batch(c, at, width, t0, gain, head=DH):
    segments, groups = [], []
    for b in range(NB):
        rows = c.u[:, b, at:at + width]
        if gain:
            segments.append((rows.rearrange("p (h d) -> p h d", d=head), 1.0))
        groups += turn_groups(rows, width // P, c.t, PARAM(c.param, gain) if gain else None, len(segments), t0, block_cut(b))
    return segments, groups


def turn_groups(rows, tiles, dst, gain, need, t0, cut):
    return [(need, [rows[:, (q + j) * P:(q + j + 1) * P] for j in range(min(4, tiles - q))], P, "f32",
             dst[:, t0 + q:t0 + min(q + 4, tiles), cut], gain) for q in range(0, tiles, 4)]


def memory_stages(c, layer):
    u, t, heads = c.u, c.t, 4
    wkv, wq, wo = c.plan[f"wkv{layer}"], c.plan[f"wq{layer}"], c.plan[f"wo{layer}"]
    mem = c.u[:, :, 2048:3072]
    x = (c.xh, c.xl)
    keys, queries = head_batch(c, 0, HALF, 0, f"mk{layer}", P), head_batch(c, D, HALF, 4, f"mq{layer}", P)
    both = (keys[0] + queries[0], keys[1] + [(g[0] + NB, *g[1:]) for g in queries[1]])
    out = [Project(c, x, [(wq, 0, range(KT), HALF, [u[:, b, D:D + HALF] for b in range(NB)])],
                   source=Source(c, c.h, x, gain=f"l{layer}_mem", norm=True), scale=True),
           Project(c, x, [(wkv, n * KT, range(KT), HALF, [u[:, b, n * HALF:(n + 1) * HALF] for b in range(NB)])
                          for n in range(2)], source=Source(c, mem, x, gain=f"l{layer}_src", norm=True), scale=True,
                   batches=[both, None])]
    units = []
    for b in range(NB):
        for pair in ((0, 1), (2, 3)):
            at = 2 * len(units)
            dst = c.o[:, b, 0:HALF].rearrange("p (h d) -> p h d", h=heads)[:, pair[0]:pair[0] + 2, :]
            v = [[u[:, k, HALF + h * P:HALF + (h + 1) * P] for k in range(NB)] for h in pair]
            units.append(Unit([t[:, 4 + h, block_cut(b)] for h in pair], [t[:, h, :] for h in pair], v, [P, P],
                              P ** -0.5, P, scaled(c, dst), slice(at, at + 2)))
    out.append(Attention(c, units))
    turned = (c.oh, c.ol)
    out.append(Residual(c, f"wo{layer}", turned, heads, source=Source(c, c.o, turned, heads, base=0)))
    return out


def out_turn(c, tiles, gain=None, segments=()):
    groups = []
    for b in range(NB):
        for q in range(0, tiles, 4):
            n = min(4, tiles - q)
            cut = (slice(None), slice(q, q + n), block_cut(b))
            groups.append((len(segments), [c.o[:, b, (q + j) * P:(q + j + 1) * P] for j in range(n)], P, "pair",
                           (c.oh[cut], c.ol[cut]), gain if q >= 4 else None))
    return Turn(c, [(list(segments), groups)])


def dram_row(dram, name):
    n = ROWS.index(name)
    return dram["rows"][n:n + 1, :].to_broadcast([P, D])


def first_mixer(c, dram):
    x, u = (c.xh, c.xl), c.u
    segments, groups = [], []
    for b in range(NB):
        q, kv = u[:, b, 784:1040], u[:, b, 1040:1168]
        segments += [(q.unsqueeze(1), 1.0), (kv.unsqueeze(1), 1.0)]
        for tile, rows, g in ((0, q[:, 0:P], "mla_q"), (1, q[:, P:2 * P], "mla_q"), (2, kv, "mla_kv")):
            col = PARAM(c.param, g)[:, tile % 2:tile % 2 + 1]
            cut = (slice(None), slice(tile, tile + 1), block_cut(b))
            groups.append((2 * b + (2 if tile == 2 else 1), [rows], P, "pair", (c.latent_h[cut], c.latent_l[cut]), col))
    m = c.plan["in_n"]
    jobs = [(m, i * KT, range(KT), w, [u[:, b, n * HALF:n * HALF + w] for b in range(NB)])
            for i, (n, w) in enumerate(((1, HALF), (2, 1200 - 2 * HALF), (0, HALF)))]
    st = [ProjectTurned(c, "in_t", 15, Source(c, c.h, x, gain="attn_pre", norm=True), dram,
                        Loads(spread(dram["rel_rows"], dram["rel_wide"]))),
          Project(c, x, jobs,
                  Loads((c.bias[:, 0:10, :], toeplitz(dram["rel_wide"], 10)),
                        (c.gain[:, 0, :], dram_row(dram, "attn_post")), (c.gain[:, 1, :], dram_row(dram, "ffn_post"))),
                  scale=True, batches=[None, (segments, groups), None])]
    m = c.plan["mla"]
    turned = []
    for b in range(NB):
        for n, at in enumerate((1200, 2096)):
            turned.append((b + 1, [u[:, b, at + 96 * h:at + 96 * (h + 1)] for h in range(4)], 96, "f32",
                           c.t[0:96, 15 + 4 * n:19 + 4 * n, block_cut(b)], None))
    st += [Project(c, (c.latent_h, c.latent_l),
                   [(m, 0, (0, 1), 384, [u[:, b, 1200:1584] for b in range(NB)]),
                    (m, 2, (2,), HALF, [u[:, b, 1584:2096] for b in range(NB)])]),
           Rope(c, turned, lambda b: u[:, b, 1200:1584], lambda b: u[:, b, 1584:2096], lambda b: u[:, b, 1168:1200],
                lambda b: u[:, b, 2096:2480])]
    compress = Compress(c)
    units, base = first_units(c, compress)
    st += [compress,
           Attention(c, units, loads=Loads(*[spread(dram[n + "_rows"], dram[n + "_wide"]) for n in ("t5", "band")]), fill=24),
           Dilated(c, c.products, base), Merge(c),
           Residual(c, "w_o", x, KT, gain=c.gain[:, 0, :], source=Source(c, c.xn, x, base=0))]
    return st


def even_mixer(c, dram):
    x, u, t = (c.xh, c.xl), c.u, c.t
    m, tail = c.plan["even"], c.plan["even_tail"]
    jobs = [(tail, 0, range(KT), 136, [u[:, b, 3584:3720] for b in range(NB)])]
    jobs += [(m, n * KT, range(KT), HALF, [u[:, b, n * HALF:(n + 1) * HALF] for b in range(NB)]) for n in range(7)]
    batches = [head_batch(c, 3584, P, 12, "idx_k"), head_batch(c, 0, HALF, 0, "a_q"), head_batch(c, HALF, HALF, 4, "a_k"),
               head_batch(c, 2 * HALF, HALF, 8, None), head_batch(c, 3 * HALF, HALF, 13, "b_q"),
               head_batch(c, 4 * HALF, HALF, 17, "b_k"), None, None]
    st = [Project(c, x, jobs, source=Source(c, c.h, x, gain="l0_mix", norm=True), scale=True, batches=batches,
                  masked=12)]
    select = (Select(c, lambda h: half(t[:, 8:12, :], h), lambda h: t[(h % 2) * DH:(h % 2 + 1) * DH, 12, :],
                     lambda b: u[:, b, 3712:3720]))
    st += [Lambda(c), select]
    units = []
    for b in range(NB):
        nk, parts = (b + 1) * P, [P] * (b + 1)
        keys, qs = slice(0, nk), block_cut(b)
        for pair in ((0, 1), (2, 3)):
            for part in range(2):
                at, heads = 2 * len(units), slice(pair[0], pair[0] + 2)
                rows = slice(part * DH, (part + 1) * DH)
                dst = c.o[:, b, HALF:D].rearrange("p (h d) -> p h d", d=P)[:, heads, :]
                v = [[u[:, k, 3072 + h * P:3072 + (h + 1) * P] for k in range(b + 1)] for h in pair]
                fin = scaled(c, dst, c.small[:, 140:142], add=True) if part else scaled(c, dst)
                units.append(Unit([t[rows, 13 + h, qs] for h in pair], [t[rows, 17 + h, keys] for h in pair], v, parts,
                                  DH ** -0.5, P, fin, slice(at, at + 2), c.bias[:, slice(8 + pair[0], 10 + pair[0]), S - nk:S]))
    for b in range(NB):
        nk, parts = (b + 1) * P, [P] * (b + 1)
        keys, qs = slice(0, nk), block_cut(b)
        for pair in ((0, 2), (1, 3), (4, 6), (5, 7)):
            at, heads = 2 * len(units), slice(pair[0], pair[1] + 1, 2)
            dst = c.o[:, b, 0:HALF].rearrange("p (h d) -> p h d", d=DH)[:, heads, :]
            v = [[u[:, k, 2560 + h * DH:2560 + (h + 1) * DH] for k in range(b + 1)] for h in pair]
            units.append(Unit([half(t, h, qs) for h in pair], [half(t[:, 4:8, :], h, keys) for h in pair], v, parts,
                              DH ** -0.5, DH, scaled(c, dst), slice(at, at + 2), c.bias[:, heads, S - nk:S],
                              extra=c.taken[:, b, 0:nk].unsqueeze(1).to_broadcast([P, 2, nk])))
    st.append(Attention(c, units, select))
    norms = [(c.o[:, b, HALF:D].rearrange("p (h d) -> p h d", d=P), 1.0 - LAMBDA_INIT) for b in range(NB)]
    st.append(out_turn(c, 8, PARAM(c.param, "subln"), norms))
    return st


def odd_mixer(c, dram):
    x, u, t, m = (c.xh, c.xl), c.u, c.t, c.plan["odd"]
    batches = [head_batch(c, n * HALF, HALF, 4 * n, "c_q" if n < 2 else "c_k") for n in range(4)] + [None, None]
    st = [Project(c, x, [(m, n * KT, range(KT), HALF, [u[:, b, n * HALF:(n + 1) * HALF] for b in range(NB)])
                         for n in range(6)], source=Source(c, c.h, x, gain="l1_mix", norm=True), scale=True,
                  batches=batches, masked=16)]
    units = []
    for b in range(NB):
        nk, parts = (b + 1) * P, [P] * (b + 1)
        keys, qs = slice(0, nk), block_cut(b)
        for q in range(4):
            for r in range(2):
                pair = (4 * q + r, 4 * q + r + 2)
                at, heads = 2 * len(units), slice(pair[0], pair[1] + 1, 2)
                dst = c.o[:, b, :].rearrange("p (h d) -> p h d", d=DH)[:, heads, :]
                v = [[u[:, k, 2 * D + h * DH:2 * D + (h + 1) * DH] for k in range(b + 1)] for h in pair]
                units.append(Unit([half(t, h, qs) for h in pair], [half(t[:, 8:16, :], h, keys) for h in pair], v,
                                  parts, DH ** -0.5, DH, scaled(c, dst), slice(at, at + 2), c.bias[:, heads, S - nk:S]))
    st.append(Attention(c, units, fill=16))
    return st


def stages_of(c, dram, out):
    x, turned = (c.xh, c.xl), (c.oh, c.ol)
    mem = dram["mem"].rearrange("(b p) d -> p b d", p=P)
    rows = lambda gain: Source(c, c.h, x, gain=gain, norm=True)
    st = [Setup(c, dram)]
    st += first_mixer(c, dram)
    st += [Ffn(c, "up", "down", rows("ffn_pre"), gain=c.gain[:, 1, :], conv=True,
               loads=Loads((c.bias[:, 0:12, :], toeplitz(dram["t5_wide"], 12))))]
    for layer in range(2):
        l = f"l{layer}"
        st.append(Ffn(c, f"up1_{layer}", f"down1_{layer}", rows(l + "_ffn1"), factor=0.5))
        if layer == 0:
            st += even_mixer(c, dram)
            st.append(Residual(c, "even_out", turned, KT, loads=Loads((c.u[:, :, 2048:3072], mem))))
        else:
            st += odd_mixer(c, dram)
            st.append(Residual(c, "odd_out", turned, KT, loads=Loads((c.u[:, :, 2048:3072], mem)),
                               source=Source(c, c.o, turned, base=0)))
        st += memory_stages(c, layer)
        after = [(c.bias[:, 0:16, :], toeplitz(dram["band_wide"], 16))] if layer == 0 else []
        st.append(Ffn(c, f"up2_{layer}", f"down2_{layer}", rows(l + "_ffn2"), factor=0.5, loads=Loads(*after)))
    st.append(Store(c, out.rearrange("a (b p) d -> p (a b) d", p=P)))
    return st


def program(nc, dram, out):
    core = Core(nc, dram["stream"])
    stages = stages_of(core, dram, out)
    numbers = [sorted(x.num for x in s.values()) for s in core.sets]

    def meet(engine, n):
        engine.drain().then_inc(core.stage_done, 1)
        engine.wait_ge(core.stage_done, 4 * (n + 1))
        engine.nop(nofuse=True)

    with nc.Block() as block:

        @block.tensor
        def _(pe):
            for n, stage in enumerate(stages):
                stage.tensor(pe, core.sets[n % 2])
                meet(pe, n)

        @block.scalar
        def _(act):
            for n, stage in enumerate(stages):
                stage.scalar(act, core.sets[n % 2])
                meet(act, n)

        @block.vector
        def _(dve):
            for n, stage in enumerate(stages):
                stage.vector(dve, core.sets[n % 2])
                meet(dve, n)

        @block.gpsimd
        def _(pool):
            for n, stage in enumerate(stages):
                if n:
                    other = numbers[(n + 1) % 2]
                    pool.sem_clear(range(other[0], other[-1] + 1))
                stage.gpsimd(pool, core.sets[n % 2])
                meet(pool, n)

        @block.sync
        def _(sp):
            for dst, src in stages[0].loads():
                sp.dma_start(dst, src).then_inc(core.first_loaded, 16)
            for n in range(core.act_next):
                if n >= RING:
                    sp.wait_ge(core.slot_used, n - RING + 1)
                sp.dma_start(core.raw[:, n % RING, :], core.stream[n]).then_inc(core.slot_loaded[n % RING], 16)


def kernel(**inputs):
    from concourse import bacc
    from concourse.bass_utils import run_bass_kernel_spmd as run

    x = {k: np.ascontiguousarray(v) for k, v in inputs.items()}
    nc = bacc.Bacc("TRN2", target_bir_lowering=False, num_devices=1)
    arrays = {
        "stream": pack_stream(x), "param": pack_params(x), "rows": pack_rows(x), "band_rows": pack_band_bias(x),
        "const": constants(), "table": tables(), "x": x["x"][0], "mem": x["mem_2"][0],
    }
    arrays = {k: np.ascontiguousarray(v) for k, v in arrays.items()}
    dram = {k: nc.dram_tensor(k + "_dram", v.shape, F32, kind="ExternalInput").ap() for k, v in arrays.items()}
    for name, heads in (("rel_rows", 10), ("t5_rows", 12)):
        dram[name] = nc.dram_tensor(name + "_dram", (heads, TOE), F32, kind="Internal").ap()
    for name, heads in (("rel_wide", 10), ("t5_wide", 12), ("band_wide", 16)):
        dram[name] = nc.dram_tensor(name + "_dram", (heads, P, TOE), F32, kind="Internal").ap()
    out = nc.dram_tensor("out_dram", (1, S, D), F32, kind="ExternalOutput").ap()
    program(nc, dram, out)
    r = run(nc, [{k + "_dram": v for k, v in arrays.items()}], core_ids=[0])
    return r.results[0]["out_dram"]
```
